# Optimizing a Trainium2 kernel written in Bass

```python
import jax, jax.numpy as jnp
from jax import lax
import numpy as np
import math
import jax
import jax.numpy as jnp

D_MODEL = 1024
BATCH = 1
SEQ = 256
DEPTH = 2

GRID_W = 64
CTX_LEN = 256
HEAD_DIM = 64
AXIS_DIM = HEAD_DIM // 2
ROPE_THETA = 10000.0
EPS = 1e-6
Q_BLOCK = 128
N_MOD = 6

GLA_HEADS = 4
GLA_DK = 64
GLA_DV = 128
GLA_GATE_RANK = 16
GLA_GATE_NORM = 16.0
GLA_CHUNK = 64
ATT_HEADS = 8
ATT_KV_HEADS = 2
SWA_HEADS = 16
SWA_KV_HEADS = 2
SWA_WINDOW = 128
MOE_GROUPS = 4
MOE_EXPERTS_PER_GROUP = 4
MOE_TOPK = 2
D_EXPERT = 256

EVEN_WIDTHS = (GLA_HEADS * GLA_DK, GLA_HEADS * GLA_DK, GLA_HEADS * GLA_DV, GLA_HEADS * GLA_DV,
               2 * GLA_GATE_RANK, ATT_HEADS * HEAD_DIM, ATT_KV_HEADS * HEAD_DIM, ATT_KV_HEADS * HEAD_DIM)
EVEN_IN = sum(EVEN_WIDTHS)
EVEN_MIX = GLA_HEADS * GLA_DV + ATT_HEADS * HEAD_DIM
ODD_Q = SWA_HEADS * HEAD_DIM
ODD_KV = SWA_KV_HEADS * HEAD_DIM
ODD_IN = ODD_Q + 2 * ODD_KV
ODD_MIX = ODD_Q
N_EVEN = (DEPTH + 1) // 2
N_ODD = DEPTH // 2


def _split(z, widths):
    return jnp.split(z, np.cumsum(widths)[:-1].tolist(), axis=-1)

def rms_norm(x, gain):
    xf = x.astype(jnp.float32)
    y = xf * lax.rsqrt(jnp.mean(xf * xf, axis=-1, keepdims=True) + EPS)
    return (y * gain.astype(jnp.float32)).astype(x.dtype)

def modulate(x, gain, shift, scale):
    return rms_norm(x, gain) * (1 + scale) + shift

def axial_rope_tables(n):
    rows = n // GRID_W
    row = jnp.repeat(jnp.arange(rows, dtype=jnp.int32), GRID_W)
    col = jnp.tile(jnp.arange(GRID_W, dtype=jnp.int32), rows)
    inv_freq = ROPE_THETA ** (-jnp.arange(0, AXIS_DIM, 2, dtype=jnp.float32) / AXIS_DIM)
    ang = jnp.stack([row[:, None] * inv_freq, col[:, None] * inv_freq], axis=1)
    return jnp.cos(ang), jnp.sin(ang)

def apply_axial_rope(x, cos, sin):
    B, n, H, _ = x.shape
    xs = x.reshape(B, n, H, 2, 2, AXIS_DIM // 2)
    x1, x2 = xs[..., 0, :], xs[..., 1, :]
    c = cos[None, :, None].astype(x.dtype)
    s = sin[None, :, None].astype(x.dtype)
    out = jnp.stack([x1 * c - x2 * s, x2 * c + x1 * s], axis=-2)
    return out.reshape(B, n, H, HEAD_DIM)

def heads(z, n_heads, gain):
    B, L, _ = z.shape
    return rms_norm(z.reshape(B, L, n_heads, HEAD_DIM), gain)

def group_q(q, n_kv):
    B, L, H, Dh = q.shape
    return q.reshape(B, L, n_kv, H // n_kv, Dh)

def softmax_attend(q, k, v, mask=None, sink=None):
    B, Q, KV, G, Dh = q.shape
    s = jnp.einsum('bqhgd,bkhd->bhgqk', q, k).astype(jnp.float32) * (Dh ** -0.5)
    if mask is not None:
        s = jnp.where(mask, s, -jnp.inf)
    if sink is not None:
        sink_col = jnp.broadcast_to(sink.reshape(1, KV, G, 1, 1).astype(jnp.float32), s.shape[:-1] + (1,))
        p = jax.nn.softmax(jnp.concatenate([s, sink_col], axis=-1), axis=-1)[..., :-1]
    else:
        p = jax.nn.softmax(s, axis=-1)
    o = jnp.einsum('bhgqk,bkhd->bqhgd', p.astype(v.dtype), v)
    return o.reshape(B, Q, KV * G * Dh)

def blocked_dense_attention(q, k, v):
    B, S = q.shape[:2]
    nb = S // Q_BLOCK
    qb = jnp.moveaxis(q.reshape(B, nb, Q_BLOCK, *q.shape[2:]), 1, 0)
    ob = lax.map(lambda qi: softmax_attend(qi, k, v), qb)
    return jnp.moveaxis(ob, 0, 1).reshape(B, S, -1)

def banded_window_attention(q, k, v, k_ctx, v_ctx, sink):
    B, S = q.shape[:2]
    nb = S // Q_BLOCK
    span = Q_BLOCK + 2 * SWA_WINDOW
    pad = ((0, 0), (SWA_WINDOW, SWA_WINDOW), (0, 0), (0, 0))
    kp = jnp.pad(k, pad)
    vp = jnp.pad(v, pad)
    qb = jnp.moveaxis(q.reshape(B, nb, Q_BLOCK, *q.shape[2:]), 1, 0)
    ctx_ok = jnp.ones((Q_BLOCK, k_ctx.shape[1]), dtype=bool)

    def block(args):
        qi, bi = args
        start = bi * Q_BLOCK
        kb = lax.dynamic_slice_in_dim(kp, start, span, axis=1)
        vb = lax.dynamic_slice_in_dim(vp, start, span, axis=1)
        qpos = start + jnp.arange(Q_BLOCK, dtype=jnp.int32)
        kpos = start - SWA_WINDOW + jnp.arange(span, dtype=jnp.int32)
        band = (kpos[None, :] >= 0) & (kpos[None, :] < S) & (jnp.abs(kpos[None, :] - qpos[:, None]) <= SWA_WINDOW)
        mask = jnp.concatenate([band, ctx_ok], axis=1)
        return softmax_attend(qi, jnp.concatenate([kb, k_ctx], axis=1), jnp.concatenate([vb, v_ctx], axis=1), mask, sink)

    ob = lax.map(block, (qb, jnp.arange(nb, dtype=jnp.int32)))
    return jnp.moveaxis(ob, 0, 1).reshape(B, S, -1)

def gla_chunk_scan(q, k, v, g, s0):
    B, H, L, DK = q.shape
    DV = v.shape[-1]
    n = L // GLA_CHUNK

    def chunks(t):
        return jnp.moveaxis(t.reshape(B, H, n, GLA_CHUNK, t.shape[-1]), 2, 0)

    lower_tri = jnp.tril(jnp.ones((GLA_CHUNK, GLA_CHUNK), dtype=bool))[:, :, None]

    def step(s, blk):
        qc, kc, vc, gc = blk
        b = jnp.cumsum(gc, axis=2)
        o = jnp.einsum('bhtk,bhkv->bhtv', qc * jnp.exp(b), s)
        diff = b[:, :, :, None, :] - b[:, :, None, :, :]
        decay = jnp.exp(jnp.where(lower_tri, diff, -jnp.inf))
        att = jnp.einsum('bhtk,bhsk,bhtsk->bhts', qc, kc, decay)
        o = o + jnp.einsum('bhts,bhsv->bhtv', att, vc)
        b_end = b[:, :, -1:, :]
        s = jnp.exp(b_end[:, :, 0, :, None]) * s + jnp.einsum('bhsk,bhsv->bhkv', kc * jnp.exp(b_end - b), vc)
        return s, o

    s_fin, o = lax.scan(step, s0, (chunks(q), chunks(k), chunks(v), chunks(g)))
    return jnp.moveaxis(o, 0, 2).reshape(B, H, L, DV), s_fin

def gla_inputs(q, k, v, lr, gate_w, gate_b):
    B, L, _ = q.shape

    def hd(t, d):
        return t.reshape(B, L, GLA_HEADS, d).transpose(0, 2, 1, 3).astype(jnp.float32)

    z = jnp.einsum('blzr,zrk->zblk', lr.reshape(B, L, 2, GLA_GATE_RANK), gate_w) + gate_b[:, None, None, :]
    g = jax.nn.log_sigmoid(z.astype(jnp.float32)) / GLA_GATE_NORM
    g = g.reshape(2, B, L, GLA_HEADS, GLA_DK).transpose(0, 1, 3, 2, 4)
    return hd(q, GLA_DK) * (GLA_DK ** -0.5), hd(k, GLA_DK), hd(v, GLA_DV), g

def gla_bidirectional(lat, ctx):
    ql, kl, vl, gl = lat
    qc, kc, vc, gc = ctx
    B = ql.shape[0]
    s0 = jnp.zeros((B, GLA_HEADS, GLA_DK, GLA_DV), jnp.float32)

    def rev(t):
        return jnp.flip(t, axis=2)

    oc_f, sc_f = gla_chunk_scan(qc, kc, vc, gc[0], s0)
    oc_b, sc_b = gla_chunk_scan(rev(qc), rev(kc), rev(vc), rev(gc[1]), s0)
    ol_f, _ = gla_chunk_scan(ql, kl, vl, gl[0], sc_f)
    ol_b, _ = gla_chunk_scan(rev(ql), rev(kl), rev(vl), rev(gl[1]), sc_b)
    return ol_f + rev(ol_b), oc_f + rev(oc_b)

def gla_output(o, r, gain):
    B, H, L, _ = o.shape
    o = rms_norm(o.transpose(0, 2, 1, 3), gain).astype(r.dtype)
    return (o * jax.nn.silu(r.reshape(B, L, H, GLA_DV))).reshape(B, L, H * GLA_DV)

def even_mixer(h_lat, h_ctx, w_in, w_out, gate_w, gate_b, gla_norm, q_norm, k_norm, cos, sin):
    B, S, _ = h_lat.shape
    Lc = h_ctx.shape[1]
    z_l = _split(h_lat @ w_in, EVEN_WIDTHS)
    z_c = _split(h_ctx @ w_in, EVEN_WIDTHS)
    o_gla_l, o_gla_c = gla_bidirectional(gla_inputs(z_l[0], z_l[1], z_l[2], z_l[4], gate_w, gate_b),
                                         gla_inputs(z_c[0], z_c[1], z_c[2], z_c[4], gate_w, gate_b))
    a_l = gla_output(o_gla_l, z_l[3], gla_norm)
    a_c = gla_output(o_gla_c, z_c[3], gla_norm)
    q_l = group_q(apply_axial_rope(heads(z_l[5], ATT_HEADS, q_norm), cos, sin), ATT_KV_HEADS)
    k_l = apply_axial_rope(heads(z_l[6], ATT_KV_HEADS, k_norm), cos, sin)
    v_l = z_l[7].reshape(B, S, ATT_KV_HEADS, HEAD_DIM)
    q_c = group_q(heads(z_c[5], ATT_HEADS, q_norm), ATT_KV_HEADS)
    k_c = heads(z_c[6], ATT_KV_HEADS, k_norm)
    v_c = z_c[7].reshape(B, Lc, ATT_KV_HEADS, HEAD_DIM)
    b_l = blocked_dense_attention(q_l, jnp.concatenate([k_l, k_c], axis=1), jnp.concatenate([v_l, v_c], axis=1))
    b_c = softmax_attend(q_c, k_c, v_c)
    return jnp.concatenate([a_l, b_l], axis=-1) @ w_out, jnp.concatenate([a_c, b_c], axis=-1) @ w_out

def odd_mixer(h_lat, h_ctx, w_in, w_out, sink, q_norm, k_norm, cos, sin, need_ctx):
    B, S, _ = h_lat.shape
    Lc = h_ctx.shape[1]
    q_l, k_l, v_l = _split(h_lat @ w_in, (ODD_Q, ODD_KV, ODD_KV))
    k_c, v_c = _split(h_ctx @ w_in[:, ODD_Q:], (ODD_KV, ODD_KV))
    q = group_q(apply_axial_rope(heads(q_l, SWA_HEADS, q_norm), cos, sin), SWA_KV_HEADS)
    k = apply_axial_rope(heads(k_l, SWA_KV_HEADS, k_norm), cos, sin)
    v = v_l.reshape(B, S, SWA_KV_HEADS, HEAD_DIM)
    kc = heads(k_c, SWA_KV_HEADS, k_norm)
    vc = v_c.reshape(B, Lc, SWA_KV_HEADS, HEAD_DIM)
    m_l = banded_window_attention(q, k, v, kc, vc, sink) @ w_out
    if not need_ctx:
        return m_l, None
    qc = group_q(heads(h_ctx @ w_in[:, :ODD_Q], SWA_HEADS, q_norm), SWA_KV_HEADS)
    return m_l, softmax_attend(qc, kc, vc, None, sink) @ w_out

def hier_moe(h, wg, bg, we, be, w_gate, w_up, w_down):
    N = h.shape[0]
    g_logits = (h @ wg + bg).astype(jnp.float32)
    g_prob = jax.nn.softmax(g_logits, axis=-1)
    g_idx = jnp.argmax(g_logits, axis=-1)
    g_weight = jnp.take_along_axis(g_prob, g_idx[:, None], axis=-1)
    e_logits = (h @ we + be).astype(jnp.float32).reshape(N, MOE_GROUPS, MOE_EXPERTS_PER_GROUP)
    e_sel = jnp.take_along_axis(e_logits, g_idx[:, None, None], axis=1)[:, 0]
    top_p, top_i = lax.top_k(jax.nn.softmax(e_sel, axis=-1), MOE_TOPK)
    top_p = top_p / jnp.sum(top_p, axis=-1, keepdims=True)
    e_weight = jnp.sum(jax.nn.one_hot(top_i, MOE_EXPERTS_PER_GROUP, dtype=jnp.float32) * top_p[..., None], axis=1)
    combine = (jax.nn.one_hot(g_idx, MOE_GROUPS, dtype=jnp.float32)[:, :, None]
               * (g_weight * e_weight)[:, None, :]).astype(h.dtype)
    out = jnp.zeros_like(h)
    for g in range(MOE_GROUPS):
        a = jnp.einsum('nd,edf->nef', h, w_gate[g])
        u = jnp.einsum('nd,edf->nef', h, w_up[g])
        hid = jax.nn.silu(a) * u * combine[:, g, :, None]
        out = out + jnp.einsum('nef,efd->nd', hid, w_down[g])
    return out

def first_inputs(seed: int = 0) -> dict:
    key = jax.random.key(seed)
    ks = iter(jax.random.split(key, 32))
    D = D_MODEL
    G, E = MOE_GROUPS, MOE_EXPERTS_PER_GROUP

    def nrm(shape, scale):
        return scale * jax.random.normal(next(ks), shape, jnp.float32)

    def gain(shape):
        return 1.0 + 0.02 * jax.random.normal(next(ks), shape, jnp.float32)

    return {
        'x': nrm((BATCH, SEQ, D), 1.0),
        'c': nrm((BATCH, D), 1.0),
        'ctx': nrm((BATCH, CTX_LEN, D), 1.0),
        'c_ctx': nrm((D,), 1.0),
        'mod_w': nrm((DEPTH, D, N_MOD * D), 0.5 * D ** -0.5),
        'mod_b': nrm((DEPTH, N_MOD * D), 0.02),
        'norm_mix': gain((DEPTH, D)),
        'norm_ffn': gain((DEPTH, D)),
        'ev_w_in': nrm((N_EVEN, D, EVEN_IN), D ** -0.5),
        'ev_w_out': nrm((N_EVEN, EVEN_MIX, D), EVEN_MIX ** -0.5),
        'gla_gate_w': nrm((N_EVEN, 2, GLA_GATE_RANK, GLA_HEADS * GLA_DK), GLA_GATE_RANK ** -0.5),
        'gla_gate_b': nrm((N_EVEN, 2, GLA_HEADS * GLA_DK), 0.1),
        'gla_out_norm': gain((N_EVEN, GLA_DV)),
        'att_q_norm': gain((N_EVEN, HEAD_DIM)),
        'att_k_norm': gain((N_EVEN, HEAD_DIM)),
        'od_w_in': nrm((N_ODD, D, ODD_IN), D ** -0.5),
        'od_w_out': nrm((N_ODD, ODD_MIX, D), ODD_MIX ** -0.5),
        'swa_sink': nrm((N_ODD, SWA_HEADS), 1.0),
        'swa_q_norm': gain((N_ODD, HEAD_DIM)),
        'swa_k_norm': gain((N_ODD, HEAD_DIM)),
        'router_group_w': nrm((DEPTH, D, G), D ** -0.5),
        'router_group_b': nrm((DEPTH, G), 0.01),
        'router_expert_w': nrm((DEPTH, D, G * E), D ** -0.5),
        'router_expert_b': nrm((DEPTH, G * E), 0.01),
        'exp_w_gate': nrm((DEPTH, G, E, D, D_EXPERT), D ** -0.5),
        'exp_w_up': nrm((DEPTH, G, E, D, D_EXPERT), D ** -0.5),
        'exp_w_down': nrm((DEPTH, G, E, D_EXPERT, D), D_EXPERT ** -0.5),
    }

def first_block(x, c, ctx, c_ctx, mod_w, mod_b, norm_mix, norm_ffn, ev_w_in, ev_w_out, gla_gate_w, gla_gate_b,
              gla_out_norm, att_q_norm, att_k_norm, od_w_in, od_w_out, swa_sink, swa_q_norm, swa_k_norm,
              router_group_w, router_group_b, router_expert_w, router_expert_b, exp_w_gate, exp_w_up, exp_w_down):
    B, S, D = x.shape
    cos, sin = axial_rope_tables(S)
    sc = jax.nn.silu(c)
    scc = jax.nn.silu(c_ctx)[None]
    for i in range(DEPTH):
        last = i == DEPTH - 1
        j = i // 2
        mod_l = jnp.split((sc @ mod_w[i] + mod_b[i])[:, None, :], N_MOD, axis=-1)
        mod_c = jnp.split((scc @ mod_w[i] + mod_b[i])[:, None, :], N_MOD, axis=-1)
        h_l = modulate(x, norm_mix[i], mod_l[0], mod_l[1])
        h_c = modulate(ctx, norm_mix[i], mod_c[0], mod_c[1])
        if i % 2 == 0:
            m_l, m_c = even_mixer(h_l, h_c, ev_w_in[j], ev_w_out[j], gla_gate_w[j], gla_gate_b[j],
                                  gla_out_norm[j], att_q_norm[j], att_k_norm[j], cos, sin)
        else:
            m_l, m_c = odd_mixer(h_l, h_c, od_w_in[j], od_w_out[j], swa_sink[j], swa_q_norm[j],
                                 swa_k_norm[j], cos, sin, not last)
        x = x + mod_l[2] * m_l
        moe_p = (router_group_w[i], router_group_b[i], router_expert_w[i], router_expert_b[i],
                 exp_w_gate[i], exp_w_up[i], exp_w_down[i])
        if last:
            f_l = hier_moe(modulate(x, norm_ffn[i], mod_l[3], mod_l[4]).reshape(B * S, D), *moe_p)
            x = x + mod_l[5] * f_l.reshape(B, S, D)
        else:
            ctx = ctx + mod_c[2] * m_c
            tok = jnp.concatenate([modulate(x, norm_ffn[i], mod_l[3], mod_l[4]).reshape(B * S, D),
                                   modulate(ctx, norm_ffn[i], mod_c[3], mod_c[4]).reshape(-1, D)], axis=0)
            f = hier_moe(tok, *moe_p)
            x = x + mod_l[5] * f[:B * S].reshape(B, S, D)
            ctx = ctx + mod_c[5] * f[B * S:].reshape(ctx.shape)
    return x


DEPTH_2 = 4

N_MIXERS = 4
RMS_EPS = 1e-6
NEG_INF = -1e30
TINY = 1e-30

A_HEADS = D_MODEL // HEAD_DIM
A_KV_HEADS = A_HEADS // 4
A_GROUP = A_HEADS // A_KV_HEADS
A_CMP_BLOCK = 32
A_CMP_STRIDE = 16
A_CMP_HIDDEN = 4 * HEAD_DIM
A_SEL_BLOCK = 64
A_SEL_TOPK = 16
A_WINDOW = 512
A_Q_BLOCK = 64
A_FORCE_BONUS = 1e3
A_SPLITS = (A_HEADS * HEAD_DIM,) + (A_KV_HEADS * HEAD_DIM,) * 6 + (3 * A_HEADS, D_MODEL)
A_IN = sum(A_SPLITS)

B_HEADS = D_MODEL // (2 * HEAD_DIM)
B_IN = 4 * D_MODEL

C_PATTERNS = ((128, 1), (512, 4), (2048, 16))
C_GROUPS = 3
C_HEADS = 4
C_V_DIM = D_MODEL // C_HEADS
C_Q_BLOCK = 64
C_IN = 2 * C_GROUPS * C_HEADS * HEAD_DIM + 2 * D_MODEL

D_HEADS = D_MODEL // HEAD_DIM
D_IN = 4 * D_MODEL


def rms_norm_2(x, gain):
    xf = x.astype(jnp.float32)
    y = xf * lax.rsqrt(jnp.mean(xf * xf, axis=-1, keepdims=True) + RMS_EPS)
    return (y * gain.astype(jnp.float32)).astype(x.dtype)

def alibi_slopes(n):
    return jnp.asarray(np.array([2.0 ** (-8.0 * (i + 1) / n) for i in range(n)], np.float32))

def split_cols(a, sizes):
    return jnp.split(a, [int(c) for c in np.cumsum(sizes)[:-1]], axis=-1)

def masked_softmax(s, mask):
    s = jnp.where(mask, s, NEG_INF)
    e = jnp.where(mask, jnp.exp(s - jnp.max(s, axis=-1, keepdims=True)), 0.0)
    return e / jnp.maximum(jnp.sum(e, axis=-1, keepdims=True), TINY)

def unblock(o):
    nq, b, h, t, d = o.shape
    return o.transpose(1, 0, 3, 2, 4).reshape(b, nq * t, h * d)

def nsa_mixer(u, w_in, w_out, pos_k, pos_v, w1_k, w2_k, w1_v, w2_v):
    B, S, _ = u.shape
    H, Hk, G, dh = A_HEADS, A_KV_HEADS, A_GROUP, HEAD_DIM
    L, st, SB, W, TQ = A_CMP_BLOCK, A_CMP_STRIDE, A_SEL_BLOCK, A_WINDOW, A_Q_BLOCK
    f32 = jnp.float32
    q, kc, vc, ks, vs, kw, vw, gl, z = split_cols(u @ w_in, A_SPLITS)
    q = q.reshape(B, S, Hk, G, dh).transpose(0, 2, 3, 1, 4).astype(f32) * dh ** -0.5

    def heads(a):
        return a.reshape(B, S, Hk, dh).transpose(0, 2, 1, 3).astype(f32)

    kc, vc, ks, vs, kw, vw = (heads(a) for a in (kc, vc, ks, vs, kw, vw))

    n_cmp = (S - L) // st + 1
    cidx = st * np.arange(n_cmp)[:, None] + np.arange(L)[None, :]
    cmp_end = jnp.asarray(cidx[:, -1])

    def compress(a, pos, w1, w2):
        blk = (a[:, :, cidx] + pos).reshape(B, Hk, n_cmp, L * dh)
        return jax.nn.gelu(blk @ w1) @ w2

    kcmp = compress(kc, pos_k, w1_k, w2_k).astype(f32)
    vcmp = compress(vc, pos_v, w1_v, w2_v).astype(f32)

    n_sel = S // SB
    ov = np.zeros((n_cmp, n_sel), np.float32)
    np.add.at(ov, (np.repeat(np.arange(n_cmp), L), (cidx // SB).ravel()), 1.0 / L)
    ov = jnp.asarray(ov)
    ks_blk = ks.reshape(B, Hk, n_sel, SB, dh)
    vs_blk = vs.reshape(B, Hk, n_sel, SB, dh)
    topk = min(A_SEL_TOPK, n_sel)
    bi = jnp.arange(B)[:, None, None, None]
    hi = jnp.arange(Hk)[None, :, None, None]

    kw_p = jnp.pad(kw, ((0, 0), (0, 0), (W, 0), (0, 0)))
    vw_p = jnp.pad(vw, ((0, 0), (0, 0), (W, 0), (0, 0)))
    slopes = alibi_slopes(H).reshape(1, Hk, G, 1, 1)

    def block(i):
        q0 = i * TQ
        t = q0 + jnp.arange(TQ)
        qb = lax.dynamic_slice_in_dim(q, q0, TQ, axis=3)
        dist = t[:, None] - cmp_end[None, :]
        p_c = masked_softmax(jnp.einsum('bhgqd,bhnd->bhgqn', qb, kcmp) - slopes * dist.astype(f32), dist >= 0)
        o_c = jnp.einsum('bhgqn,bhnd->bhgqd', p_c, vcmp)
        imp = jnp.einsum('bhgqn,nj->bhqj', p_c, ov)
        cur = (t // SB)[:, None]
        j = jnp.arange(n_sel)[None, :]
        forced = (j == 0) | (j == cur) | (j == cur - 1)
        imp = jnp.where(j > cur, -1.0, imp + jnp.where(forced, A_FORCE_BONUS, 0.0))
        _, sel = lax.top_k(imp, topk)
        ksel = ks_blk[bi, hi, sel].reshape(B, Hk, TQ, topk * SB, dh)
        vsel = vs_blk[bi, hi, sel].reshape(B, Hk, TQ, topk * SB, dh)
        pos = (sel[..., None] * SB + jnp.arange(SB)).reshape(B, Hk, TQ, topk * SB)
        dist = (t[:, None] - pos)[:, :, None]
        p_s = masked_softmax(jnp.einsum('bhgqd,bhqkd->bhgqk', qb, ksel) - slopes * dist.astype(f32), dist >= 0)
        o_s = jnp.einsum('bhgqk,bhqkd->bhgqd', p_s, vsel)
        kwin = lax.dynamic_slice_in_dim(kw_p, q0, TQ + W, axis=2)
        vwin = lax.dynamic_slice_in_dim(vw_p, q0, TQ + W, axis=2)
        spos = q0 - W + jnp.arange(TQ + W)
        dist = t[:, None] - spos[None, :]
        mask = (dist >= 0) & (dist < W) & (spos[None, :] >= 0)
        p_w = masked_softmax(jnp.einsum('bhgqd,bhkd->bhgqk', qb, kwin) - slopes * dist.astype(f32), mask)
        o_w = jnp.einsum('bhgqk,bhkd->bhgqd', p_w, vwin)
        return jnp.stack([o_c, o_s, o_w])

    outs = lax.map(block, jnp.arange(S // TQ))
    outs = outs.transpose(1, 2, 0, 5, 3, 4, 6).reshape(3, B, S, H, dh)
    gates = jax.nn.sigmoid(gl.astype(f32)).reshape(B, S, 3, H).transpose(2, 0, 1, 3)[..., None]
    o = jnp.sum(gates * outs, axis=0).reshape(B, S, H * dh)
    return (o.astype(u.dtype) * jax.nn.silu(z)) @ w_out

def diff_mixer(u, w_in, w_out, lam, sub_gain, lambda_init):
    B, S, _ = u.shape
    H, dh, TQ = B_HEADS, HEAD_DIM, Q_BLOCK
    f32 = jnp.float32
    q, k, v, z = split_cols(u @ w_in, (D_MODEL,) * 4)
    q = q.reshape(B, S, H, 2, dh).transpose(0, 2, 3, 1, 4).astype(f32) * dh ** -0.5
    k = k.reshape(B, S, H, 2, dh).transpose(0, 2, 3, 1, 4).astype(f32)
    v = v.reshape(B, S, H, 2 * dh).transpose(0, 2, 1, 3).astype(f32)
    lamf = lam.astype(f32)
    lam_full = jnp.exp(jnp.sum(lamf[0] * lamf[1])) - jnp.exp(jnp.sum(lamf[2] * lamf[3])) + lambda_init
    slopes = alibi_slopes(H).reshape(1, H, 1, 1, 1)
    kpos = jnp.arange(S)

    def block(i):
        q0 = i * TQ
        t = q0 + jnp.arange(TQ)
        qb = lax.dynamic_slice_in_dim(q, q0, TQ, axis=3)
        dist = t[:, None] - kpos[None, :]
        p = masked_softmax(jnp.einsum('bhmqd,bhmkd->bhmqk', qb, k) - slopes * dist.astype(f32), dist >= 0)
        a = p[:, :, 0] - lam_full * p[:, :, 1]
        return jnp.einsum('bhqk,bhkd->bhqd', a, v)

    o = lax.map(block, jnp.arange(S // TQ))
    o = o.transpose(1, 0, 3, 2, 4).reshape(B, S, H, 2 * dh)
    o = (rms_norm_2(o, sub_gain) * (1.0 - lambda_init)).reshape(B, S, H * 2 * dh)
    return (o.astype(u.dtype) * jax.nn.silu(z)) @ w_out

def dilated_mixer(u, w_in, w_out):
    B, S, _ = u.shape
    G, Hg, dh, dv, TQ = C_GROUPS, C_HEADS, HEAD_DIM, C_V_DIM, C_Q_BLOCK
    f32 = jnp.float32
    qk = G * Hg * dh
    q, k, v, z = split_cols(u @ w_in, (qk, qk, D_MODEL, D_MODEL))
    q = q.reshape(B, S, G, Hg, dh).transpose(2, 0, 3, 1, 4).astype(f32) * dh ** -0.5
    k = k.reshape(B, S, G, Hg, dh).transpose(2, 0, 3, 1, 4).astype(f32)
    v = v.reshape(B, S, Hg, dv).transpose(0, 2, 1, 3).astype(f32)
    slopes = alibi_slopes(G * Hg).reshape(G, Hg)

    def block(i):
        q0 = i * TQ
        t = q0 + jnp.arange(TQ)
        outs, lses = [], []
        for g, (w, d) in enumerate(C_PATTERNS):
            offs = d * np.arange(w // d + 1)
            p = t[:, None] - offs[None, :]
            valid = p >= 0
            pc = jnp.maximum(p, 0)
            kg = jnp.take(k[g], pc, axis=2)
            vg = jnp.take(v, pc, axis=2)
            qb = lax.dynamic_slice_in_dim(q[g], q0, TQ, axis=2)
            s = jnp.einsum('bhqd,bhqnd->bhqn', qb, kg) - slopes[g][None, :, None, None] * offs.astype(np.float32)
            s = jnp.where(valid, s, NEG_INF)
            m = jnp.max(s, axis=-1, keepdims=True)
            e = jnp.where(valid, jnp.exp(s - m), 0.0)
            l = jnp.sum(e, axis=-1, keepdims=True)
            outs.append(jnp.einsum('bhqn,bhqnd->bhqd', e / l, vg))
            lses.append(m[..., 0] + jnp.log(l[..., 0]))
        wts = jax.nn.softmax(jnp.stack(lses), axis=0)[..., None]
        return jnp.sum(wts * jnp.stack(outs), axis=0)

    o = unblock(lax.map(block, jnp.arange(S // TQ)))
    return (o.astype(u.dtype) * jax.nn.silu(z)) @ w_out

def stick_mixer(u, w_in, w_out):
    B, S, _ = u.shape
    H, dh, TQ = D_HEADS, HEAD_DIM, Q_BLOCK
    f32 = jnp.float32
    q, k, v, z = split_cols(u @ w_in, (D_MODEL,) * 4)
    q = q.reshape(B, S, H, dh).transpose(0, 2, 1, 3).astype(f32) * dh ** -0.5
    k = k.reshape(B, S, H, dh).transpose(0, 2, 1, 3).astype(f32)
    v = v.reshape(B, S, H, dh).transpose(0, 2, 1, 3).astype(f32)
    kpos = jnp.arange(S)

    def block(i):
        q0 = i * TQ
        t = q0 + jnp.arange(TQ)
        qb = lax.dynamic_slice_in_dim(q, q0, TQ, axis=2)
        logits = jnp.einsum('bhqd,bhkd->bhqk', qb, k)
        causal = kpos[None, :] < t[:, None]
        log_om = jnp.where(causal, jax.nn.log_sigmoid(-logits), 0.0)
        between = lax.cumsum(log_om, axis=3, reverse=True) - log_om
        a = jnp.where(causal, jnp.exp(jax.nn.log_sigmoid(logits) + between), 0.0)
        return jnp.einsum('bhqk,bhkd->bhqd', a, v)

    o = unblock(lax.map(block, jnp.arange(S // TQ)))
    return (o.astype(u.dtype) * jax.nn.silu(z)) @ w_out

def second_inputs(seed: int = 0) -> dict:
    key = jax.random.key(seed)
    ks = jax.random.split(key, 20)
    n_a = (DEPTH_2 + 3) // 4
    n_b = (DEPTH_2 + 2) // 4
    n_c = (DEPTH_2 + 1) // 4
    n_d = DEPTH_2 // 4
    L, dh = A_CMP_BLOCK, HEAD_DIM

    def dense(k, shape, fan_in):
        return jax.random.normal(k, shape, jnp.float32) * fan_in ** -0.5

    def gain(k, shape):
        return 1.0 + 0.02 * jax.random.normal(k, shape, jnp.float32)

    return {
        'x': jax.random.normal(ks[0], (BATCH, SEQ, D_MODEL), jnp.float32),
        'norm_pre': gain(ks[1], (DEPTH_2, D_MODEL)),
        'norm_post': gain(ks[2], (DEPTH_2, D_MODEL)),
        'a_w_in': dense(ks[3], (n_a, D_MODEL, A_IN), D_MODEL),
        'a_w_out': dense(ks[4], (n_a, D_MODEL, D_MODEL), D_MODEL),
        'a_cmp_pos_k': 0.1 * jax.random.normal(ks[5], (n_a, L, dh), jnp.float32),
        'a_cmp_pos_v': 0.1 * jax.random.normal(ks[6], (n_a, L, dh), jnp.float32),
        'a_cmp_w1_k': dense(ks[7], (n_a, L * dh, A_CMP_HIDDEN), L * dh),
        'a_cmp_w2_k': dense(ks[8], (n_a, A_CMP_HIDDEN, dh), A_CMP_HIDDEN),
        'a_cmp_w1_v': dense(ks[9], (n_a, L * dh, A_CMP_HIDDEN), L * dh),
        'a_cmp_w2_v': dense(ks[10], (n_a, A_CMP_HIDDEN, dh), A_CMP_HIDDEN),
        'b_w_in': dense(ks[11], (n_b, D_MODEL, B_IN), D_MODEL),
        'b_w_out': dense(ks[12], (n_b, D_MODEL, D_MODEL), D_MODEL),
        'b_lambda': 0.1 * jax.random.normal(ks[13], (n_b, 4, dh), jnp.float32),
        'b_sub_gain': gain(ks[14], (n_b, 2 * dh)),
        'c_w_in': dense(ks[15], (n_c, D_MODEL, C_IN), D_MODEL),
        'c_w_out': dense(ks[16], (n_c, D_MODEL, D_MODEL), D_MODEL),
        'd_w_in': dense(ks[17], (n_d, D_MODEL, D_IN), D_MODEL),
        'd_w_out': dense(ks[18], (n_d, D_MODEL, D_MODEL), D_MODEL),
    }

def second_block(x, norm_pre, norm_post, a_w_in, a_w_out, a_cmp_pos_k, a_cmp_pos_v, a_cmp_w1_k, a_cmp_w2_k,
              a_cmp_w1_v, a_cmp_w2_v, b_w_in, b_w_out, b_lambda, b_sub_gain, c_w_in, c_w_out, d_w_in, d_w_out):
    h = x
    for i in range(DEPTH_2):
        m, j = i % N_MIXERS, i // N_MIXERS
        u = rms_norm_2(h, norm_pre[i])
        if m == 0:
            y = nsa_mixer(u, a_w_in[j], a_w_out[j], a_cmp_pos_k[j], a_cmp_pos_v[j],
                          a_cmp_w1_k[j], a_cmp_w2_k[j], a_cmp_w1_v[j], a_cmp_w2_v[j])
        elif m == 1:
            lambda_init = 0.8 - 0.6 * math.exp(-0.3 * i)
            y = diff_mixer(u, b_w_in[j], b_w_out[j], b_lambda[j], b_sub_gain[j], lambda_init)
        elif m == 2:
            y = dilated_mixer(u, c_w_in[j], c_w_out[j])
        else:
            y = stick_mixer(u, d_w_in[j], d_w_out[j])
        h = h + rms_norm_2(y, norm_post[i])
    return h


def setup_inputs(seed=0):
    out = dict(first_inputs(seed))
    for name, value in second_inputs(seed + 1).items():
        if name != "x":
            out[name + "_2"] = value
    return out


def reference(
    x, c, ctx, c_ctx, mod_w, mod_b, norm_mix, norm_ffn, ev_w_in, ev_w_out, gla_gate_w,
    gla_gate_b, gla_out_norm, att_q_norm, att_k_norm, od_w_in, od_w_out, swa_sink, swa_q_norm,
    swa_k_norm, router_group_w, router_group_b, router_expert_w, router_expert_b, exp_w_gate,
    exp_w_up, exp_w_down, norm_pre_2, norm_post_2, a_w_in_2, a_w_out_2, a_cmp_pos_k_2,
    a_cmp_pos_v_2, a_cmp_w1_k_2, a_cmp_w2_k_2, a_cmp_w1_v_2, a_cmp_w2_v_2, b_w_in_2, b_w_out_2,
    b_lambda_2, b_sub_gain_2, c_w_in_2, c_w_out_2, d_w_in_2, d_w_out_2,
):
    x = first_block(
        x, c, ctx, c_ctx, mod_w, mod_b, norm_mix, norm_ffn, ev_w_in, ev_w_out, gla_gate_w,
        gla_gate_b, gla_out_norm, att_q_norm, att_k_norm, od_w_in, od_w_out, swa_sink,
        swa_q_norm, swa_k_norm, router_group_w, router_group_b, router_expert_w,
        router_expert_b, exp_w_gate, exp_w_up, exp_w_down,
    )
    return second_block(
        x, norm_pre_2, norm_post_2, a_w_in_2, a_w_out_2, a_cmp_pos_k_2, a_cmp_pos_v_2,
        a_cmp_w1_k_2, a_cmp_w2_k_2, a_cmp_w1_v_2, a_cmp_w2_v_2, b_w_in_2, b_w_out_2, b_lambda_2,
        b_sub_gain_2, c_w_in_2, c_w_out_2, d_w_in_2, d_w_out_2,
    )


_drawn_inputs = setup_inputs


def setup_inputs(seed=0):
    import zlib

    import numpy as np

    out = dict(_drawn_inputs(seed))
    spreads = {}
    factors = {'norm_mix': 2.797,
     'gla_gate_b': 2.914,
     'gla_out_norm': 5.802,
     'att_q_norm': 8.0,
     'att_k_norm': 8.0,
     'swa_sink': 8.0,
     'swa_q_norm': 8.0,
     'swa_k_norm': 8.0,
     'router_group_b': 55.698,
     'router_expert_b': 18.489,
     'a_cmp_pos_k_2': 14.43,
     'b_sub_gain_2': 29.808,
     'norm_ffn': 3.551,
     'norm_post_2': 4.157}
    for name, (base, spread) in spreads.items():
        noise = np.random.default_rng([zlib.crc32(name.encode()), seed]).standard_normal(out[name].shape)
        drawn = base * np.exp(spread * noise) if base else spread * noise
        out[name] = jnp.asarray(drawn.astype(out[name].dtype))
    for name, factor in factors.items():
        out[name] = (out[name] * factor).astype(out[name].dtype)
    return out
```

```python
from contextlib import ExitStack

import numpy as np

import concourse.bass as bass
from concourse import mybir

F32 = mybir.dt.float32
U32 = mybir.dt.uint32
ACT = mybir.ActivationFunctionType
ALU = mybir.AluOpType
AX = mybir.AxisListType

P = 128
S = 256
D = 1024
KT = D // P
LAT, CTX = 0, 1
NT = 2 * S // P
LT = S // P
HALF = 4 * 512
SLOTS = 6
NEG = -1e30
EPS = 1e-6
TINY = 1e-30
HD = 64
QSCALE = HD ** -0.5

N_MOD = 6
GLA_H, GLA_DK, GLA_DV = 4, 64, 128
GLA_GATE_NORM = 16.0
GATE_RANK = 16
LEVELS = [128, 64, 32, 16, 8, 4, 2, 1]
NE, NG, EPG = 16, 4, 4
FE = 256
CMP_N, CMP_L, CMP_ST = (S - 32) // 16 + 1, 32, 16
LAMBDA_INIT = 0.8 - 0.6 * float(np.exp(-0.3))
C_PATTERNS = ((128, 1), (512, 4), (2048, 16))


def alibi(n):
    return [float(np.float32(2.0 ** (-8.0 * (i + 1) / n))) for i in range(n)]


def fields(table):
    at, out = 0, {}
    for name, width in table:
        out[name] = (at, at + width)
        at += width
    return out, at


SMALL, N_SMALL = fields([
    ("cond", KT * 2), ("mod_b", 2 * 48), ("norm_mix", 2 * KT), ("norm_ffn", 2 * KT), ("norm_pre", 4 * KT),
    ("gate_b", 4), ("att_q", HD), ("att_k", HD), ("swa_q", HD), ("swa_k", HD), ("gla_norm", GLA_DV),
    ("sub_gain", 2 * HD), ("router_b", 2 * 20), ("sink", 16), ("lam", 4 * HD), ("pos_k", 16), ("pos_v", 16),
    ("router_w", 2 * KT * 20), ("lr_w", KT * 32), ("gl_w", KT * 48), ("gate_w", 2 * 256),
    ("w2_k", 2 * 128), ("w2_v", 2 * 64)])
CONST, N_CONST = fields([("ident", P), ("causal", LT * S), ("rope", LT * 64), ("diag2", P),
                         ("gla_masks", 2 * 7 * P)])
LATE, N_LATE = fields([("band", LT * 512), ("cmp_bias", LT * 16 * CMP_N), ("cmp_valid", LT * CMP_N)])
PHASE = max(2 * 7 * P, N_LATE)
DILATED, N_DILATED = fields([("dilated", 3 * LT * S), ("strict", LT * S)])


def const_arrays():
    p = np.arange(P)
    t = np.arange(S).reshape(LT, P)
    k = np.arange(S)
    dist = t[:, :, None] - k[None, None, :]
    causal = np.where(dist >= 0, -dist, NEG)
    inv = (np.float32(10000.0) ** (-np.arange(0, 32, 2, dtype=np.float32) / np.float32(32))).astype(np.float32)
    row, col = (np.arange(S) // 64).astype(np.float32), (np.arange(S) % 64).astype(np.float32)
    ang = np.stack([row[:, None] * inv, col[:, None] * inv], 1)
    rope = np.stack([np.cos(ang), np.sin(ang)], 1).reshape(LT, P, 64)
    masks = np.zeros((2, 7, P, P))
    for n, m in enumerate(LEVELS[1:]):
        blk, right = p // (2 * m), (p // m) % 2
        fwd = (blk[:, None] == blk[None, :]) & (right[:, None] == 0) & (right[None, :] == 1)
        masks[0, n], masks[1, n] = fwd, fwd.T
    band = np.zeros((LT, P, 512))
    band[:, :, :S] = np.where(np.abs(dist) <= 128, 0.0, NEG)
    end = CMP_ST * np.arange(CMP_N) + CMP_L - 1
    cd = t[:, :, None] - end[None, None, :]
    sl = np.array(alibi(16))
    cmp_bias = np.where(cd[:, :, None, :] >= 0, -sl[None, None, :, None] * cd[:, :, None, :], NEG)
    dil = np.stack([np.where((dist >= 0) & (dist <= w) & (dist % d == 0), -dist, NEG) for w, d in C_PATTERNS])

    def pack(a):
        return np.moveaxis(a, -2, 0).reshape(P, -1).astype(np.float32)

    const = np.concatenate([np.eye(P), pack(causal), pack(rope), 2 * np.eye(P), pack(masks)], 1)
    late = np.concatenate([pack(band), np.moveaxis(cmp_bias, 1, 0).reshape(P, -1),
                           pack((cd >= 0).astype(np.float64))], 1)
    dilated = np.concatenate([pack(dil), pack(np.where(dist > 0, 0.0, NEG))], 1)
    return [np.ascontiguousarray(a, np.float32) for a in (const, late, dilated)]


def by_rows(w):
    return w.reshape(-1, P, w.shape[1]).transpose(1, 0, 2)


def chunks_of(w):
    r = by_rows(w)
    out = []
    for n in range(0, w.shape[1], 512):
        if n + 512 <= w.shape[1]:
            out += [r[:, 0:4, n:n + 512], r[:, 4:8, n:n + 512]]
        else:
            out.append(r[:, :, n:n + 256])
    return out


def expert_order():
    out = [("up", 0), ("up", 1), ("down", 0)]
    for i in range(1, NE // 2):
        out += [("up", 2 * i), ("down", 2 * i - 1), ("up", 2 * i + 1), ("down", 2 * i)]
    return out + [("down", NE - 1)]


def expert_chunks(gate, up, down):
    out = []
    for kind, e in expert_order():
        if kind == "up":
            out += chunks_of(np.concatenate([gate[e // EPG, e % EPG], up[e // EPG, e % EPG]], 1))
        else:
            out.append(by_rows(down[e // EPG, e % EPG]))
    return out


def host_layout(a):
    a = {k: np.asarray(v) for k, v in a.items()}
    ev, od, aw, cw = a["ev_w_in"][0], a["od_w_in"][0], a["a_w_in_2"][0], a["c_w_in_2"][0]
    w = chunks_of(a["mod_w"][0])
    w += chunks_of(np.concatenate([ev[:, 0:1536], ev[:, 1568:2336]], 1))
    w += chunks_of(a["ev_w_out"][0])
    w += expert_chunks(a["exp_w_gate"][0], a["exp_w_up"][0], a["exp_w_down"][0])
    w += chunks_of(a["mod_w"][1])
    w += chunks_of(od[:, 1024:1280]) + chunks_of(od[:, 0:1024])
    w += chunks_of(a["od_w_out"][0])
    w += expert_chunks(a["exp_w_gate"][1], a["exp_w_up"][1], a["exp_w_down"][1])
    w += chunks_of(np.concatenate([aw[:, 0:2560], aw[:, 2608:3632]], 1))
    for name in ("a_cmp_w1_k_2", "a_cmp_w1_v_2"):
        r = by_rows(a[name][0])
        w += [r[:, 0:8], r[:, 8:16]]
    w += chunks_of(a["a_w_out_2"][0])
    w += chunks_of(a["b_w_in_2"][0]) + chunks_of(a["b_w_out_2"][0])
    w += chunks_of(cw) + chunks_of(a["c_w_out_2"][0])
    w += chunks_of(a["d_w_in_2"][0]) + chunks_of(a["d_w_out_2"][0])
    weights = np.empty((len(w), P, HALF), np.float32)
    for n, c in enumerate(w):
        weights[n] = c.reshape(P, HALF)

    def cols(v):
        v = v.reshape(-1, P)
        return v.T

    def row(v):
        return np.broadcast_to(v.reshape(1, -1), (P, v.size))

    def pos(v):
        return v.reshape(16, P).T

    gate_w = np.zeros((P, 2, 256), np.float32)
    gate_w[0:16, 0], gate_w[16:32, 1] = a["gla_gate_w"][0, 0], a["gla_gate_w"][0, 1]
    cond = np.stack([cols(a["c"]), cols(a["c_ctx"])], 2)
    router_w = np.concatenate([a["router_group_w"], a["router_expert_w"]], 2)
    router_b = np.concatenate([a["router_group_b"], a["router_expert_b"]], 1)
    w2k = by_rows(a["a_cmp_w2_k_2"][0])
    parts = {
        "cond": cond, "mod_b": cols(a["mod_b"]), "norm_mix": cols(a["norm_mix"]), "norm_ffn": cols(a["norm_ffn"]),
        "norm_pre": cols(a["norm_pre_2"]), "gate_b": cols(a["gla_gate_b"][0]),
        "att_q": row(a["att_q_norm"]), "att_k": row(a["att_k_norm"]), "swa_q": row(a["swa_q_norm"]),
        "swa_k": row(a["swa_k_norm"]), "gla_norm": row(a["gla_out_norm"]), "sub_gain": row(a["b_sub_gain_2"]),
        "router_b": row(router_b), "sink": row(a["swa_sink"]), "lam": row(a["b_lambda_2"]),
        "pos_k": pos(a["a_cmp_pos_k_2"]), "pos_v": pos(a["a_cmp_pos_v_2"]),
        "router_w": np.stack([by_rows(router_w[i]) for i in range(2)], 1),
        "lr_w": by_rows(ev[:, 1536:1568]), "gl_w": by_rows(aw[:, 2560:2608]), "gate_w": gate_w,
        "w2_k": np.concatenate([w2k, w2k], 2), "w2_v": by_rows(a["a_cmp_w2_v_2"][0]),
    }
    small = np.empty((P, N_SMALL), np.float32)
    for name, (lo, hi) in SMALL.items():
        small[:, lo:hi] = parts[name].reshape(P, hi - lo)
    const, late, dilated = const_arrays()
    return {
        "x": np.ascontiguousarray(a["x"][0]), "ctx": np.ascontiguousarray(a["ctx"][0]), "weights": weights,
        "small": small, "norm_post": np.ascontiguousarray(a["norm_post_2"]),
        "const": const, "late": late, "dilated": dilated,
    }


class Banks:

    def __init__(self, banks, full, free):
        self.banks, self.full, self.free = banks, full, free
        self.fills = self.drains = 0

    def take(self, pe):
        n = self.fills
        if n >= len(self.banks):
            pe.wait_ge(self.free, n - len(self.banks) + 1)
        self.fills += 1
        return self.banks[n % len(self.banks)]

    def drained(self, pe, fills=None):
        fills = self.fills if fills is None else fills
        if fills:
            pe.wait_ge(self.free, fills)

    def filled_bank(self, eng):
        self.drains += 1
        eng.wait_ge(self.full, self.drains)
        return self.banks[(self.drains - 1) % len(self.banks)]


class Seen:

    def __init__(self, eng):
        self.eng, self.count = eng, {}

    def next(self, semaphore, n=1):
        self.count[semaphore.name] = self.count.get(semaphore.name, 0) + n
        self.eng.wait_ge(semaphore, self.count[semaphore.name])


def build_program(nc, d_x, d_ctx, d_w, d_small, d_post, d_const, d_late, d_dilated, d_out, layers=6):
    with ExitStack() as stack:
        def sb(name, *shape):
            return stack.enter_context(nc.sbuf_tensor(name, [P, *shape], F32))

        def sem(name):
            return stack.enter_context(nc.semaphore(name))

        bank = [stack.enter_context(nc.psum_tensor(f"bank{i}", [P, 512], F32)) for i in range(8)]

        x = sb("x", NT, D)
        ring = sb("ring", SLOTS, HALF)
        hT_flat = sb("hT", KT * 2 * S)
        Z = sb("Z", NT * 2336)
        mix = sb("mix", NT, D)
        rows = sb("rows", 2 * D)
        const = sb("const", N_CONST - 2 * 7 * P)
        phase = sb("phase", PHASE)
        small = sb("small", N_SMALL)
        post_row = sb("post_row", D)
        arena = sb("arena", 8200)
        scratch = sb("scratch", 1024)
        stat = sb("stat", 768)
        modT = sb("modT", 48, 2)
        modA = sb("modA", 2, KT, 2)
        cond = sb("cond", KT, 2)
        half_neg = sb("half_neg", 64)

        hT4 = hT_flat[:, :].rearrange("p (k t) -> p k t", k=KT)
        hT2 = hT_flat[:, 0:KT * S].rearrange("p (k t) -> p k t", k=KT)
        hT_spare = hT_flat[:, KT * S:]

        def sm(name, pattern=None, **sizes):
            lo, hi = SMALL[name]
            v = small[:, lo:hi]
            return v.rearrange(pattern, **sizes) if pattern else v

        def cn(name):
            lo, hi = CONST[name]
            return const[:, lo:hi]

        ident = cn("ident")
        causal = cn("causal").rearrange("p (t k) -> p t k", t=LT)
        rope = cn("rope").rearrange("p (t c a f) -> p t c a f", t=LT, c=2, a=2)
        gla_masks = phase[:, 0:2 * 7 * P].rearrange("p (d l t) -> p d l t", d=2, l=7).bitcast(U32)

        def late(name):
            lo, hi = LATE[name]
            return phase[:, lo:hi]

        band = late("band").rearrange("p (t k) -> p t k", t=LT)
        cmp_bias = late("cmp_bias").rearrange("p (t n) -> p t n", t=LT)
        cmp_valid = late("cmp_valid").rearrange("p (t n) -> p t n", t=LT)
        dilated = rows[:, 0:3 * LT * S].rearrange("p (g t k) -> p g t k", g=3, t=LT)
        strict = rows[:, 3 * LT * S:4 * LT * S].rearrange("p (t k) -> p t k", t=LT)
        gate_rows = rows[:, :].rearrange("p (s n) -> p s n", s=2)

        x_loaded, small_loaded, const_loaded = sem("x_loaded"), sem("small_loaded"), sem("const_loaded")
        late_loaded, dilated_loaded, post_loaded = sem("late_loaded"), sem("dilated_loaded"), sem("post_loaded")
        slot_full = [sem(f"slot_full{s}") for s in range(SLOTS)]
        chunk_used = sem("chunk_used")
        a_full, a_free = sem("a_full"), sem("a_free")
        s_full, s_free = sem("s_full"), sem("s_free")
        v_full, v_free = sem("v_full"), sem("v_free")
        cond_ready = sem("cond_ready")
        mod_ready = sem("mod_ready")
        sumsq_ready = sem("sumsq_ready")
        meansq_ready = sem("meansq_ready")
        rstd_ready = sem("rstd_ready")
        normed_ready = sem("normed_ready")
        x_ready = sem("x_ready")
        heads_ready = sem("heads_ready")
        mix_ready = sem("mix_ready")
        z_act_ready = sem("z_act_ready")
        gate_in, gate_soft = sem("gate_in"), sem("gate_soft")
        expo_in, expo_out = sem("expo_in"), sem("expo_out")
        level_ready = sem("level_ready")
        gla_done = sem("gla_done")
        max_ready = sem("max_ready")
        probs_ready = sem("probs_ready")
        maps_ready = sem("maps_ready")
        probs_mixed = sem("probs_mixed")
        soft_in, soft_out = sem("soft_in"), sem("soft_out")
        cmp_blk, cmp_hid, cmp_probs = sem("cmp_blk"), sem("cmp_hid"), sem("cmp_probs")
        raw_full = sem("raw_full")
        cmp_in, cmp_out = sem("cmp_in"), sem("cmp_out")
        route_in, route_out = sem("route_in"), sem("route_out")
        g_full, g_free = sem("g_full"), sem("g_free")
        u_full, u_free = sem("u_full"), sem("u_free")
        d_full, d_free = sem("d_full"), sem("d_free")
        dve_step = sem("dve_step")
        pool_step = sem("pool_step")
        out_done = sem("out_done")

        A = Banks(bank[0:4], a_full, a_free)
        SC = Banks(bank[4:6], s_full, s_free)
        V = Banks(bank[6:8], v_full, v_free)

        whole = {}
        tenancy = []
        moe_at = {}

        zs = {0: Z[:, :].rearrange("p (t n) -> p t n", t=NT),
              1: Z[:, 0:NT * 1280].rearrange("p (t n) -> p t n", t=NT),
              2: Z[:, 0:LT * 3632].rearrange("p (t n) -> p t n", t=LT),
              3: Z[:, 0:LT * 4096].rearrange("p (t n) -> p t n", t=LT),
              4: Z[:, 0:LT * 3584].rearrange("p (t n) -> p t n", t=LT),
              5: Z[:, 0:LT * 4096].rearrange("p (t n) -> p t n", t=LT)}
        zo = {T: Z[:, 0:T * D].rearrange("p (t n) -> p t n", t=T) for T in (2, 4)}

        def ar(lo, n):
            return arena[:, lo:lo + n]

        qT = ar(0, 1024).rearrange("p (f t) -> p f t", f=2)
        kT = ar(1024, 1024).rearrange("p (f t) -> p f t", f=2)
        cum = ar(2048, 2056).rearrange("p (d f s t) -> p d f s t", d=2, f=2, s=2)
        X = [ar(4104 + 2048 * b, 2048) for b in range(2)]
        lrT = rows[:, 0:512]
        att_same = hT_flat[:, 0:2048].rearrange("p (s j h t) -> p s j h t", s=2, j=2, h=4)
        att_other = hT_flat[:, 2048:4096].rearrange("p (s j h t) -> p s j h t", s=2, j=2, h=4)
        kst = rows[:, 0:1024].rearrange("p (d f j k) -> p d f j k", d=2, f=2, j=2)
        state = rows[:, 1024:2048].rearrange("p (d f v) -> p d f v", d=2, f=2)
        silu_g = [ar(1024 * b, 1024).rearrange("p (f t) -> p f t", f=2) for b in range(2)]
        hid = [ar(2048 + 1024 * b, 1024).rearrange("p (f t) -> p f t", f=2) for b in range(2)]
        route = ar(4096, 512)
        route_buf = [ar(4608 + 16 * b, 16) for b in range(2)]
        kdup = Z[:, LT * 3632:LT * 3632 + 2048]
        cdup = mix[:, 2:4, :]
        pairs = [rows[:, 512 * b:512 * b + 512].rearrange("p (h m) -> p h m", h=4) for b in range(2)]
        vcmp = rows[:, 1024:2048].rearrange("p (h n) -> p h n", h=4)
        blk = [ar(4096 + 960 * b, 960).rearrange("p (l n) -> p l n", l=16) for b in range(2)]
        hidden = ar(6016, 512)
        hidT_k = ar(6528, 120).rearrange("p (k n) -> p k n", k=2)
        kcmpT = ar(6648, 60)
        cmp_s = ar(6710, 240)
        cmp_p = ar(6950, 512)
        cmpT = ar(7462, 512)
        hidT_v = x[:, 2, :].rearrange("p (k h g n) -> p k h g n", k=2, h=4, g=4)
        gelu_t = x[:, 3, 0:512]
        weighed = hT_spare[:, 1536:2048]

        aq = ar(0, 2048)
        ak = ar(2048, 2048)
        s_ring = [ar(4096 + 768 * b, 768) for b in range(2)] + [scratch[:, 0:768]]
        p_ring = [ar(5632 + 768 * b, 768) for b in range(3)]
        pT_ring = [hT_spare[:, 512 * b:512 * b + 512] for b in range(3)]
        nmax = stat[:, 0:128]
        sums = stat[:, 128:256]
        rsum = stat[:, 256:320]
        head_ss = stat[:, 320:400]
        head_rstd = stat[:, 400:480]
        ss = stat[:, 480:484]
        rstd = stat[:, 484:488]
        esink = stat[:, 488:520]
        comb = stat[:, 520:584].rearrange("p (e t) -> p e t", e=NE)
        lam = stat[:, 584:592]
        gates = stat[:, 592:688]
        coef = stat[:, 688:752]

        block = stack.enter_context(nc.Block())

        @block.scalar
        def _(act):
            seen = Seen(act)

            def drain(*copies, func=ACT.Copy):
                b = A.filled_bank(act)
                for dst, src, scale, bias in copies:
                    f = func if bias is None else ACT.Identity
                    i = nc.scalar.activation(dst, src(b), f, scale=scale, bias=0.0 if bias is None else bias)
                i.then_inc(a_free, 1)

            def cond_silu():
                act.wait_ge(small_loaded, 16)
                nc.scalar.activation(cond[:, :, :], sm("cond", "p (k s) -> p k s", s=2), ACT.Silu).then_inc(cond_ready, 1)

            def sum_squares(src, T, wait):
                for t in range(T):
                    wait(t)
                    nc.scalar.activation(scratch[:, :], src[:, t, :], ACT.Square, accum_out=ss[:, t:t + 1]).then_inc(sumsq_ready, 1)
                    seen.next(sumsq_ready)

            def features(T, scale_bias=None):
                per = 4 // T
                for j in range(KT // per):
                    copies = []
                    for n in range(per):
                        k = j * per + n
                        if scale_bias is None:
                            hT = hT4 if T == 4 else hT2
                            copies.append((hT[:, k, :], lambda b, n=n: b[:, n * T * P:(n + 1) * T * P], 1.0, None))
                            continue
                        for s in range(T // LT):
                            scale, bias = scale_bias(k, s)
                            hT = hT4 if T == 4 else hT2
                            lo = n * T * P + s * S
                            copies.append((hT[:, k, s * S:(s + 1) * S], lambda b, lo=lo: b[:, lo:lo + S], scale, bias))
                    drain(*copies)

            def projected(dst, T, widths):
                col = 0
                for w in widths:
                    for t in range(T):
                        drain((dst[:, t, col:col + w], lambda b, w=w: b[:, 0:w], 1.0, None))
                    col += w

            def q_features(dst, n_ft, T, scale):
                per = 4 // T
                for j in range(n_ft // per):
                    drain((dst[:, j * per * T * P:(j + 1) * per * T * P], lambda b: b[:, :], scale, None))

            def gate_row_copies(T):
                for s in range(T // LT):
                    for h in range(2):
                        drain((gate_rows[:, s, h * 512:(h + 1) * 512], lambda b: b[:, :], 1.0, None))
                whole["gates", T] = A.drains

            def exp_probs(u, src, dst, n, wait=True):
                return nc.scalar.activation(dst, src, ACT.Exp, bias=nmax[:, n:n + 1], accum_out=sums[:, n:n + 1])

            def pT_out(u, width):
                drain((pT_ring[u % 3][:, 0:width], lambda b, w=width: b[:, 0:w], 1.0, None))

            def experts(i):
                T = NT if i == 0 else LT
                N = T * P
                base = NE * i

                def silu(e, parity, first):
                    for f in range(2):
                        act.wait_ge(g_full, e * 2 + f + 1)
                        if f == 0 and not first:
                            act.wait_ge(u_free, e * 2 - 2)
                        nc.scalar.activation(silu_g[parity][:, f, 0:N], bank[f][:, 0:N], ACT.Silu).then_inc(g_free, 1)

                silu(base, 0, i == 0)
                silu(base + 1, 1, i == 0)
                with act.Fori(1, NE // 2) as n:
                    silu(n * 2 + base, 0, False)
                    silu(n * 2 + (base + 1), 1, False)

            def route_exps(i):
                for _ in range(2):
                    seen.next(route_in)
                    src = route_buf[0] if _ == 0 else route_buf[1]
                    T = NT if i == 0 else LT
                    nc.scalar.activation(src[:, 0:4 * T], src[:, 0:4 * T], ACT.Exp).then_inc(route_out, 1)

            def modulate(i, which, T):
                features(T, lambda k, s: (modA[:, which, k, s:s + 1], modT[:, (0 if which == 0 else 24) + k, s:s + 1]))

            def wait_x(t):
                seen.next(x_ready)

            def first_layer(i):
                T = NT if i == 0 else LT
                sum_squares(x, NT, (lambda t: act.wait_ge(x_loaded, 32)) if i == 0 else wait_x)
                seen.next(mod_ready)
                modulate(i, 0, NT)
                if i == 0:
                    projected(zs[0], NT, [512, 512, 512, 512, 256])
                    drain((zs[0][:, :, 2304:2336], lambda b: b[:, 0:NT * 32].rearrange("p (t n) -> p t n", t=NT), 1.0, None))
                else:
                    for t in range(NT):
                        drain((zs[1][:, t, 1024:1280], lambda b: b[:, 0:256], 1.0, None))
                    projected(zs[1], LT, [512, 512])
                whole["z", i] = A.drains
                if i == 0:
                    gla()
                    attention_heads(0)
                else:
                    attention_heads(1)
                features(T)
                gate_row_copies(T)
                projected(zo[T], T, [512, 512])
                whole["y", i] = A.drains
                sum_squares(x, T, wait_x)
                modulate(i, 1, T)
                route_exps(i)
                experts(i)
                gate_row_copies(T)
                whole["gates2", i] = A.drains

            def gla():
                for dst, scale in ((qT, QSCALE), (kT, 1.0)):
                    for f in range(2):
                        drain((dst[:, f, :], lambda b: b[:, :], scale, None))
                drain((lrT[0:32, :], lambda b: b[0:32, :], 1.0, None))
                seen.next(gate_in)
                nc.scalar.activation(X[1], X[1], ACT.Exp).then_inc(gate_soft, 1)
                seen.next(gate_soft)
                nc.scalar.activation(X[1], X[1], ACT.Ln, bias=1.0).then_inc(gate_soft, 1)
                for n in range(len(LEVELS) + 1):
                    seen.next(expo_in)
                    nc.scalar.activation(X[n % 2], X[n % 2], ACT.Exp, scale=1.0 / GLA_GATE_NORM).then_inc(expo_out, 1)
                for d in range(2):
                    drain((kst[:, d].rearrange("p f j k -> p (f j k)"), lambda b: b[:, :], 1.0, None))
                for d in range(2):
                    drain(*[(state[64 * o:64 * o + 64, d].rearrange("p f (o v) -> p f o v", o=2)[:, :, o, :],
                             lambda b, o=o: b[64 * o:64 * o + 64, :].rearrange("p (f o v) -> p f o v", f=2, o=2)[:, :, o, :], 1.0, None)
                            for o in range(2)])
                act.wait_ge(a_free, whole["z", 0])
                for t in range(NT):
                    i = nc.scalar.activation(zs[0][:, t, 1024:1536], zs[0][:, t, 1024:1536], ACT.Silu)
                i.then_inc(z_act_ready, 1)

            def attention_heads(i):
                if i == 0:
                    q_features(aq, 4, NT, QSCALE)
                    for v in range(2):
                        drain((ak[:, v * 512:(v + 1) * 512], lambda b: b[:, :], 1.0, None))
                    for s in range(2):
                        keys = 512 if s == 0 else 256
                        n_u = LT * 8
                        for u in range(n_u + 1):
                            if u < n_u:
                                seen.next(max_ready)
                                b = bank[4 + u % 2]
                                exp_probs(u, b[:, 0:keys], p_ring[u % 3][:, 0:keys], s * 16 + u).then_inc(probs_ready, 1)
                            if u >= 1:
                                pT_out(u - 1, keys)
                else:
                    q_features(aq, 8, LT, QSCALE)
                    for v in range(2):
                        drain((ak[:, v * 512:(v + 1) * 512], lambda b: b[:, :], 1.0, None))
                    n_u = LT * 16
                    for u in range(n_u + 1):
                        if u < n_u:
                            seen.next(max_ready)
                            exp_probs(u, s_ring[u % 3][:, 0:512], p_ring[u % 3][:, 0:512], u)
                            nc.scalar.activation(esink[:, u:u + 1], sm("sink")[:, u % 16:u % 16 + 1], ACT.Exp,
                                                 bias=nmax[:, u:u + 1]).then_inc(probs_ready, 1)
                        if u >= 1:
                            pT_out(u - 1, 512)

            def second_layer(i):
                sum_squares(x, LT, wait_x)
                features(LT, lambda k, s: (sm("norm_pre", "p (l k) -> p l k", l=4)[:, i - 2, k:k + 1], None))
                projected(zs[i], LT, {2: [512] * 5 + [512] * 2, 3: [512] * 8, 4: [512] * 7, 5: [512] * 8}[i])
                if i == 2:
                    drain((zs[2][:, :, 3584:3632], lambda b: b[:, 0:LT * 48].rearrange("p (t n) -> p t n", t=LT), 1.0, None))
                whole["z", i] = A.drains
                {2: sparse, 3: differential, 4: dilated_heads, 5: stick}[i]()
                lo, hi = {2: (2560, 3584), 3: (3072, 4096), 4: (2560, 3584), 5: (3072, 4096)}[i]
                for t in range(LT):
                    n = nc.scalar.activation(zs[i][:, t, lo:hi], zs[i][:, t, lo:hi], ACT.Silu)
                n.then_inc(z_act_ready, 1)
                features(LT)
                projected(zo[2], LT, [512, 512])
                act.wait_ge(a_free, A.drains)
                whole["y", i] = A.drains
                sum_squares(zo[2], LT, lambda t: None)

            def sparse():
                q_features(aq, 8, LT, QSCALE)
                q_features(ak, 8, LT, 1.0)
                for src in range(2):
                    for j in range(2):
                        dst = pairs[src]
                        drain(*[(dst[lo:lo + 64, 2 * j:2 * j + 2, :],
                                 lambda b, lo=lo, o=o: b[lo:lo + 64, :].rearrange("p (h m o) -> p h m o", h=2, o=2)[:, :, :, o],
                                 1.0, None) for o, lo in ((0, 0), (1, 64))])
                whole["pairs"] = A.drains
                act.wait_ge(a_free, whole["z", 2])
                nc.scalar.activation(gates.rearrange("p (t n) -> p t n", t=LT), zs[2][:, :, 3584:3632], ACT.Exp,
                                     scale=-1.0).then_inc(cmp_out, 1)
                seen.next(cmp_in)
                nc.scalar.activation(gelu_t[0:60, :], gelu_t[0:60, :], ACT.Exp, scale=-1.0).then_inc(cmp_out, 1)
                for src in range(2):
                    for kt in range(2):
                        b = A.filled_bank(act)
                        if src == 0:
                            n = nc.scalar.activation(hidT_k[:, kt, :], b[:, 0:60], ACT.Copy)
                        else:
                            for hk in range(4):
                                dst = hidT_v[:, kt, hk, :, 0:CMP_N]
                                n = nc.scalar.activation(dst, b[:, hk * CMP_N:(hk + 1) * CMP_N].unsqueeze(1).broadcast_to([P, 4, CMP_N]), ACT.Copy)
                        n.then_inc(a_free, 1)
                drain((kcmpT[:, :], lambda b: b[:, 0:60], 1.0, None))
                b = A.filled_bank(act)
                for hk in range(4):
                    for g in range(4):
                        n = nc.scalar.activation(vcmp[32 * g:32 * g + 32, hk, g * 64:(g + 1) * 64],
                                                 b[32 * g:32 * g + 32, hk * 64:(hk + 1) * 64], ACT.Copy)
                n.then_inc(a_free, 1)
                for qt in range(LT):
                    seen.next(cmp_in)
                    nc.scalar.activation(cmp_s[:, :], cmp_s[:, :], ACT.Exp).then_inc(cmp_out, 1)
                    drain((cmpT[:, :], lambda b: b[:, :], 1.0, None))
                n_u = LT * 16
                for u in range(n_u + 1):
                    if u < n_u:
                        seen.next(max_ready)
                        nk = P * (u // 16 + 1)
                        exp_probs(u, s_ring[u % 3][:, 0:nk], p_ring[u % 3][:, 0:nk], 2 * u)
                        exp_probs(u, s_ring[u % 3][:, nk:2 * nk], p_ring[u % 3][:, nk:2 * nk], 2 * u + 1).then_inc(probs_ready, 1)
                    if u >= 1:
                        pT_out(u - 1, 2 * P * ((u - 1) // 16 + 1))

            def differential():
                q_features(aq, 8, LT, QSCALE)
                q_features(ak, 8, LT, 1.0)
                seen.next(cmp_in)
                nc.scalar.activation(lam[:, 2:4], lam[:, 0:2], ACT.Exp).then_inc(cmp_out, 1)
                n_u = LT * 8
                for u in range(n_u + 1):
                    if u < n_u:
                        seen.next(max_ready)
                        nk = P * (u // 8 + 1)
                        exp_probs(u, s_ring[u % 3][:, 0:nk], p_ring[u % 3][:, 0:nk], 2 * u)
                        exp_probs(u, s_ring[u % 3][:, nk:2 * nk], p_ring[u % 3][:, nk:2 * nk], 2 * u + 1).then_inc(maps_ready, 1)
                    if u >= 1:
                        pT_out(u - 1, P * ((u - 1) // 8 + 1))

            def dilated_heads():
                q_features(aq, 6, LT, QSCALE)
                q_features(ak, 6, LT, 1.0)
                n_u = LT * 4
                for u in range(n_u + 1):
                    if u < n_u:
                        seen.next(max_ready)
                        nk = P * (u // 4 + 1)
                        exp_probs(u, s_ring[u % 3][:, 0:3 * nk], p_ring[u % 3][:, 0:3 * nk], u).then_inc(maps_ready, 1)
                    if u >= 1:
                        pT_out(u - 1, P * ((u - 1) // 4 + 1))

            def stick():
                q_features(aq, 8, LT, QSCALE)
                q_features(ak, 8, LT, 1.0)
                n_u = LT * 16
                for u in range(n_u + 2):
                    if u < n_u:
                        nk = P * (u // 16 + 1)
                        mag = s_ring[u % 3][:, 512:512 + nk]
                        seen.next(soft_in)
                        nc.scalar.activation(mag, mag, ACT.Exp).then_inc(soft_out, 1)
                        seen.next(soft_out)
                        nc.scalar.activation(mag, mag, ACT.Ln, bias=1.0).then_inc(soft_out, 1)
                        seen.next(soft_out)
                    if 1 <= u <= n_u:
                        nk = P * ((u - 1) // 16 + 1)
                        seen.next(max_ready)
                        nc.scalar.activation(p_ring[(u - 1) % 3][:, 512:512 + nk], p_ring[(u - 1) % 3][:, 256:256 + nk],
                                             ACT.Exp).then_inc(probs_ready, 1)
                    if u >= 2:
                        pT_out(u - 2, P * ((u - 2) // 16 + 1))

            cond_silu()
            for i in range(min(layers, 2)):
                first_layer(i)
            for i in range(2, layers):
                second_layer(i)

        @block.tensor
        def _(pe):
            seen = Seen(pe)
            uses = [0] * SLOTS

            def chunk():
                slot = len(tenancy) % SLOTS
                uses[slot] += 1
                pe.wait_ge(slot_full[slot], 16 * uses[slot])
                tenancy.append([slot, None, None])
                return ring[:, slot, :]

            half_count = [0]

            def chunk_done(ins):
                half_count[0] += 1
                ins.then_inc(chunk_used, 1)
                tenancy[-1][1:] = [chunk_used, half_count[0]]

            def chunk_done_with(pool):
                tenancy[-1][1:] = [pool.full, pool.fills]

            def modulation():
                b = V.take(pe)
                for n in range(12):
                    for kh in range(2):
                        w = chunk().rearrange("p (k n) -> p k n", k=4)
                        for j in range(4):
                            for k in range(4):
                                m = n * 4 + j
                                i = nc.tensor.matmul(b[:, 2 * m:2 * m + 2], w[:, k, j * P:(j + 1) * P], cond[:, 4 * kh + k, :],
                                                     start=(n == 0 and kh == 0 and j == 0 and k == 0),
                                                     stop=(kh == 1 and k == 3), skip_group_check=True)
                        if n == 11 and kh == 1:
                            i.then_inc(v_full, 1)
                            chunk_done_with(V)
                        else:
                            chunk_done(i)

            def transposes(src, T):
                per = 4 // T
                for j in range(KT // per):
                    b = A.take(pe)
                    for n in range(per):
                        for t in range(T):
                            i = nc.tensor.transpose(b[:, (n * T + t) * P:(n * T + t + 1) * P],
                                                    src[:, t, (j * per + n) * P:(j * per + n + 1) * P], ident)
                    i.then_inc(a_full, 1)

            def project(T, n_chunks, quarter=False, wide=None):
                hT = hT4 if wide or T == 4 else hT2
                for n in range(n_chunks):
                    banks = []
                    for kh in range(1 if quarter else 2):
                        kn = 8 if quarter else 4
                        w = chunk().rearrange("p (k n) -> p k n", k=kn)
                        N = HALF // kn
                        last = quarter or kh == 1
                        for t in range(T):
                            if kh == 0:
                                banks.append(A.take(pe))
                            for k in range(kn):
                                i = nc.tensor.matmul(banks[t][:, 0:N], hT[:, kn * kh + k, t * P:(t + 1) * P], w[:, k, :],
                                                     start=(kh == 0 and k == 0), stop=(last and k == kn - 1))
                            if last:
                                i.then_inc(a_full, 1)
                        if last:
                            chunk_done_with(A)
                        else:
                            chunk_done(i)

            def project_small(T, w, N):
                hT = hT4 if T == 4 else hT2
                b = A.take(pe)
                for t in range(T):
                    for k in range(KT):
                        i = nc.tensor.matmul(b[:, t * N:(t + 1) * N], hT[:, k, t * P:(t + 1) * P], w[:, k, :],
                                             start=(k == 0), stop=(k == KT - 1))
                i.then_inc(a_full, 1)

            def gate_row_products(T, which):
                for s in range(T // LT):
                    for h in range(2):
                        b = A.take(pe)
                        for j in range(4):
                            i = nc.tensor.matmul(b[:, j * P:(j + 1) * P],
                                                 modT[:, which * 8 + h * 4 + j, s:s + 1].broadcast_to([P, P]), ident,
                                                 start=True, stop=True)
                        i.then_inc(a_full, 1)

            def head_features(src, n_ft, T):
                per = 4 // T
                for j in range(n_ft // per):
                    b = A.take(pe)
                    for n in range(per):
                        for t in range(T):
                            i = nc.tensor.transpose(b[:, (n * T + t) * P:(n * T + t + 1) * P], src(t, j * per + n), ident)
                    i.then_inc(a_full, 1)

            def attend(n_u, score, turn, weigh, lag_events):
                pT_at = {}
                for step in range(n_u + 2):
                    if step < n_u:
                        score(step)
                    if 1 <= step <= n_u:
                        u = step - 1
                        seen.next(lag_events)
                        b = A.take(pe)
                        turn(u, b).then_inc(a_full, 1)
                        pT_at[u] = A.fills
                    if step >= 2:
                        A.drained(pe, pT_at[step - 2])
                        weigh(step - 2)

            def turn_blocks(src, n, b):
                for j in range(n):
                    i = nc.tensor.transpose(b[:, j * P:(j + 1) * P], src[:, j * P:(j + 1) * P], ident)
                return i

            def gla():
                z = zs[0]
                for col in (0, 256):
                    head_features(lambda t, f: z[:, t, col + f * P:col + (f + 1) * P], 2, NT)
                b = A.take(pe)
                for t in range(NT):
                    i = nc.tensor.transpose(b[0:32, t * P:(t + 1) * P], z[:, t, 2304:2336], ident)
                i.then_inc(a_full, 1)
                A.drained(pe)
                gw = sm("gate_w", "p (d n) -> p d n", d=2)
                for d in range(2):
                    for f in range(2):
                        b = V.take(pe)
                        nc.tensor.matmul(b[:, :], gw[0:32, d, f * P:(f + 1) * P], lrT[0:32, :], start=True,
                                         stop=True).then_inc(v_full, 1)

                def pair_products(blocks):
                    banks = [V.take(pe) for _ in range(2)]
                    for n, (left, right, keys, queries) in enumerate(blocks):
                        for f in range(2):
                            for odd in range(2):
                                r = slice(64 * odd, 64 * odd + 64)
                                o = (n * 2 + f) * P
                                i = nc.tensor.matmul(banks[odd][:, o:o + P], left(f)[r, keys], right(f)[r, queries],
                                                     start=True, stop=True)
                                if n == 1 and f == 1:
                                    i.then_inc(v_full, 1)

                for s in range(2):
                    at = [slice(s * S + j * P, s * S + (j + 1) * P) for j in range(2)]
                    pair_products([(lambda f: kT[:, f, :], lambda f: qT[:, f, :], sl, sl) for sl in at])
                tile = [slice(0, P), slice(P, S)]
                for n, m in enumerate(LEVELS):
                    seen.next(level_ready)
                    xl = X[n % 2].rearrange("p (d f s t) -> p d f s t", d=2, f=2, s=2)

                    def src(d, s):
                        return lambda f: xl[:, d, f, s, :]

                    if m == P:
                        for s in range(2):
                            pair_products([(src(d, s), src(d, s), tile[d], tile[1 - d]) for d in range(2)])
                        continue
                    for d in range(2):
                        for s in range(2):
                            pair_products([(src(d, s), src(d, s), tile[j], tile[j]) for j in range(2)])
                seen.next(level_ready)
                xi = X[len(LEVELS) % 2].rearrange("p (w f t) -> p w f t", w=4, f=2)
                for d in range(2):
                    b = A.take(pe)
                    for f in range(2):
                        for j in range(2):
                            o = (f * 2 + j) * P
                            i = nc.tensor.transpose(b[:, o:o + P], xi[:, d, f, j * P:(j + 1) * P], ident)
                    i.then_inc(a_full, 1)
                A.drained(pe)
                for d in range(2):
                    b = A.take(pe)
                    for f in range(2):
                        for j in range(2):
                            i = nc.tensor.matmul(b[:, f * 256:(f + 1) * 256], kst[:, d, f, j, :],
                                                 z[:, 2 + j, 512 + f * 256:512 + (f + 1) * 256], start=(j == 0), stop=(j == 1))
                    i.then_inc(a_full, 1)
                A.drained(pe)
                V.drained(pe)
                for s in range(2):
                    for j in range(2):
                        b = V.take(pe)
                        if s == LAT:
                            for f in range(2):
                                for d in range(2):
                                    nc.tensor.matmul(b[:, f * 256:(f + 1) * 256], xi[:, 2 + d, f, j * P:(j + 1) * P], state[:, d, f, :],
                                                     start=(f == 0 and d == 0), stop=False, skip_group_check=True)
                        for h in range(GLA_H):
                            for js in range(2):
                                a = att_same if js == j else att_other
                                i = nc.tensor.matmul(b[:, h * P:(h + 1) * P], a[:, s, js, h, :],
                                                     z[:, 2 * s + js, 512 + h * P:512 + (h + 1) * P],
                                                     start=(s == CTX and h == 0 and js == 0), stop=(js == 1), skip_group_check=True)
                        i.then_inc(v_full, 1)

            def rows_of(h):
                return slice(64 * (h % 2), 64 * (h % 2) + 64)

            def first_attention(i):
                if i == 0:
                    z = zs[0]
                    seen.next(heads_ready)
                    head_features(lambda t, f: z[:, t, 1536 + f * P:1536 + (f + 1) * P], 4, NT)
                    head_features(lambda t, f: mix[:, t, 512 + f * P:512 + (f + 1) * P], 2, NT)
                    A.drained(pe)
                    q4 = aq.rearrange("p (f t) -> p f t", f=4)
                    k4 = ak[:, 0:1024].rearrange("p (v t) -> p v t", v=2)
                    for s in range(2):
                        keys = 512 if s == 0 else 256
                        k0 = 0 if s == 0 else S

                        def score(u):
                            h, qt = u % 8, u // 8
                            b = bank[4 + u % 2]
                            nc.tensor.matmul(b[:, 0:keys], q4[rows_of(h), h // 2, s * S + qt * P:s * S + (qt + 1) * P],
                                             k4[rows_of(h), h // 4, k0:512], start=True, stop=True).then_inc(raw_full, 1)

                        def weigh(u):
                            h = u % 8
                            if h == 0:
                                out_bank[0] = V.take(pe)
                            for j in range(keys // P):
                                t = k0 // P + j
                                m = nc.tensor.matmul(out_bank[0][:, h * HD:(h + 1) * HD], pT_ring[u % 3][:, j * P:(j + 1) * P],
                                                     z[:, t, 2176 + (h // 4) * HD:2176 + (h // 4 + 1) * HD],
                                                     start=(j == 0), stop=(j == keys // P - 1))
                            if h == 7:
                                m.then_inc(v_full, 1)

                        attend(LT * 8, score, lambda u, b: turn_blocks(p_ring[u % 3], keys // P, b), weigh, probs_ready)
                else:
                    z = zs[1]
                    seen.next(heads_ready)
                    head_features(lambda t, f: z[:, t, f * P:(f + 1) * P], 8, LT)
                    head_features(lambda t, f: mix[:, t, f * P:(f + 1) * P], 2, NT)
                    A.drained(pe)
                    q8 = aq.rearrange("p (f t) -> p f t", f=8)
                    k4 = ak[:, 0:1024].rearrange("p (v t) -> p v t", v=2)

                    def score(u):
                        h, qt = u % 16, u // 16
                        b = SC.take(pe)
                        nc.tensor.matmul(b[:, :], q8[rows_of(h), h // 2, qt * P:(qt + 1) * P], k4[rows_of(h), h // 8, :],
                                         start=True, stop=True).then_inc(s_full, 1)

                    def weigh(u):
                        h = u % 16
                        if h % 8 == 0:
                            out_bank[0] = V.take(pe)
                        for t in range(NT):
                            m = nc.tensor.matmul(out_bank[0][:, (h % 8) * HD:(h % 8 + 1) * HD], pT_ring[u % 3][:, t * P:(t + 1) * P],
                                                 z[:, t, 1152 + (h // 8) * HD:1152 + (h // 8 + 1) * HD],
                                                 start=(t == 0), stop=(t == NT - 1))
                        if h % 8 == 7:
                            m.then_inc(v_full, 1)

                    attend(LT * 16, score, lambda u, b: turn_blocks(p_ring[u % 3], 4, b), weigh, probs_ready)

            out_bank = [None]

            def router(i, T):
                hT = hT4 if T == 4 else hT2
                w = sm("router_w", "p (l k n) -> p l k n", l=2, k=KT)[:, i]
                b = V.take(pe)
                for t in range(T):
                    for k in range(KT):
                        m = nc.tensor.matmul(b[:, t * 20:(t + 1) * 20], hT[:, k, t * P:(t + 1) * P], w[:, k, :],
                                             start=(k == 0), stop=(k == KT - 1))
                m.then_inc(v_full, 1)

            def experts(i):
                T = NT if i == 0 else LT
                N = T * P
                hT = hT4 if T == 4 else hT2
                base = NE * i
                d_base = 0 if i == 0 else NE * NT * 2
                A.drained(pe)
                SC.drained(pe)
                V.drained(pe)
                slot0 = len(tenancy) % SLOTS
                uses0 = list(uses)
                half0 = half_count[0]
                moe_at[i] = (len(tenancy), half0, d_base)

                def arrive(slot, count):
                    pe.wait_ge(slot_full[slot], count)
                    return ring[:, slot, :]

                def gate_up(e, slots, counts, first):
                    for kh in range(2):
                        w = arrive(slots[kh], counts[kh]).rearrange("p (k n) -> p k n", k=4)
                        for f in range(4):
                            if kh == 0 and not first:
                                pe.wait_ge(g_free if f < 2 else u_free, e * 2 + (f % 2 - 1))
                            for k in range(4):
                                m = nc.tensor.matmul(bank[f][:, 0:N], w[:, k, f * P:(f + 1) * P], hT[:, 4 * kh + k, :],
                                                     start=(kh == 0 and k == 0), stop=(kh == 1 and k == 3))
                            if kh == 1:
                                m.then_inc(g_full if f < 2 else u_full, 1)
                        if kh == 0:
                            m.then_inc(chunk_used, 1)

                def down(e, n, parity, slot, count, first):
                    w = arrive(slot, count).rearrange("p (f n) -> p f n", f=2)
                    pe.wait_ge(u_free, e * 2 + 2)
                    for t in range(T):
                        for h in range(2):
                            c = t * 2 + h
                            if not (first and c < 4):
                                pe.wait_ge(d_free, n + (c - 3))
                            for f in range(2):
                                m = nc.tensor.matmul(bank[4 + c % 4][:, :], hid[parity][:, f, t * P:(t + 1) * P],
                                                     w[:, f, h * 512:(h + 1) * 512], start=(f == 0), stop=(f == 1))
                            m.then_inc(d_full, 1)

                def slot(c):
                    return (slot0 + c) % SLOTS

                def nth(c):
                    return 16 * (uses0[slot(c)] + c // SLOTS + 1)

                per = 2 * T
                gate_up(base, [slot(0), slot(1)], [nth(0), nth(1)], i == 0)
                gate_up(base + 1, [slot(2), slot(3)], [nth(2), nth(3)], False)
                down(base, d_base, 0, slot(4), nth(4), True)
                with pe.Fori(1, NE // 2) as j:
                    c = [slot(5 + q) for q in range(6)]
                    k = [j * 16 + (nth(5 + q) - 16) for q in range(6)]
                    gate_up(j * 2 + base, c[0:2], k[0:2], False)
                    down(j * 2 + (base - 1), j * (2 * per) + (d_base - per), 1, c[2], k[2], False)
                    gate_up(j * 2 + (base + 1), c[3:5], k[3:5], False)
                    down(j * 2 + base, j * (2 * per) + d_base, 0, c[5], k[5], False)
                down(base + NE - 1, d_base + (NE - 1) * per, 1, slot(47), nth(47), False)
                for q in range(3 * NE):
                    uses[slot(q)] += 1
                half_count[0] += NE
                for q in range(3 * NE):
                    tenancy.append([slot(q), d_full, d_base + NE * per])
                pe.wait_ge(g_free, 2 * (base + NE))
                pe.wait_ge(u_free, 2 * (base + NE))
                pe.wait_ge(d_free, d_base + NE * per)

            def first_layer(i):
                T = NT if i == 0 else LT
                modulation()
                seen.next(normed_ready, NT)
                transposes(mix, NT)
                A.drained(pe)
                if i == 0:
                    project(NT, 4)
                    project(NT, 1, quarter=True)
                    project_small(NT, sm("lr_w", "p (k n) -> p k n", k=KT), 32)
                    A.drained(pe)
                    gla()
                else:
                    project(NT, 1, quarter=True)
                    project(LT, 2, wide=True)
                    A.drained(pe)
                first_attention(i)
                V.drained(pe)
                transposes(mix, T)
                seen.next(mod_ready)
                gate_row_products(T, 2)
                A.drained(pe)
                project(T, 2)
                seen.next(normed_ready, T)
                transposes(mix, T)
                A.drained(pe)
                router(i, T)
                experts(i)
                gate_row_products(T, 5)

            def second_layer(i):
                seen.next(normed_ready, LT)
                transposes(mix, LT)
                A.drained(pe)
                project(LT, {2: 7, 3: 8, 4: 7, 5: 8}[i])
                if i == 2:
                    project_small(LT, sm("gl_w", "p (k n) -> p k n", k=KT), 48)
                A.drained(pe)
                {2: sparse, 3: differential, 4: dilated_heads, 5: stick}[i]()
                seen.next(mix_ready, LT)
                transposes(mix, LT)
                A.drained(pe)
                project(LT, 2)

            def sparse():
                z = zs[2]
                head_features(lambda t, f: z[:, t, f * P:(f + 1) * P], 8, LT)
                seen.next(heads_ready)
                kd = kdup.rearrange("p (t f n) -> p t f n", t=LT, f=8)
                head_features(lambda t, f: kd[:, t, f, :], 8, LT)
                cd = cdup
                head_features(lambda t, f: cd[:, t, f * P:(f + 1) * P], 8, LT)
                for src in range(2):
                    b = V.take(pe)
                    seen.next(cmp_blk)
                    for c in range(2):
                        w = chunk().rearrange("p (l n) -> p l n", l=8)
                        for l in range(8):
                            i = nc.tensor.matmul(b[0:60, 0:256], blk[src][:, c * 8 + l, :], w[:, l, :],
                                                 start=(c == 0 and l == 0), stop=(c == 1 and l == 7))
                        if c == 0:
                            chunk_done(i)
                    i.then_inc(v_full, 1)
                    chunk_done_with(V)
                seen.next(cmp_hid)
                for src in range(2):
                    for kt in range(2):
                        b = A.take(pe)
                        nc.tensor.transpose(b[:, 0:60], hidden[0:60, src * 256 + kt * P:src * 256 + (kt + 1) * P],
                                            ident[0:60, 0:60]).then_inc(a_full, 1)
                A.drained(pe)
                w2k = sm("w2_k", "p (k n) -> p k n", k=2)
                w2v = sm("w2_v", "p (k n) -> p k n", k=2)
                b = A.take(pe)
                for kt in range(2):
                    i = nc.tensor.matmul(b[:, 0:60], w2k[:, kt, :], hidT_k[:, kt, :], start=(kt == 0), stop=(kt == 1))
                i.then_inc(a_full, 1)
                b = A.take(pe)
                for hk in range(4):
                    for kt in range(2):
                        i = nc.tensor.matmul(b[:, hk * 64:(hk + 1) * 64], hidT_v[:, kt, hk].rearrange("p g n -> p (g n)"),
                                             w2v[:, kt, :], start=(kt == 0), stop=(kt == 1))
                i.then_inc(a_full, 1)
                A.drained(pe)
                q8 = aq.rearrange("p (f t) -> p f t", f=8)
                for qt in range(LT):
                    banks = [SC.take(pe) for _ in range(2)]
                    for h in range(16):
                        i = nc.tensor.matmul(banks[h % 2][:, (h // 2) * CMP_N:(h // 2 + 1) * CMP_N], q8[rows_of(h), h // 2, qt * P:(qt + 1) * P],
                                             kcmpT[rows_of(h), (h // 4) * CMP_N:(h // 4 + 1) * CMP_N], start=True, stop=True)
                        if h >= 14:
                            i.then_inc(s_full, 1)
                    seen.next(cmp_probs)
                    b = A.take(pe)
                    for hk in range(4):
                        i = nc.tensor.transpose(b[:, hk * P:(hk + 1) * P], cmp_p[:, hk * P:(hk + 1) * P], ident)
                    i.then_inc(a_full, 1)
                    A.drained(pe)
                    for half in range(2):
                        b = V.take(pe)
                        for hk in range(2):
                            i = nc.tensor.matmul(b[:, hk * 256:(hk + 1) * 256],
                                                 cmpT[:, (2 * half + hk) * P:(2 * half + hk + 1) * P], vcmp[:, 2 * half + hk, :],
                                                 start=True, stop=True)
                        i.then_inc(v_full, 1)
                k8 = ak.rearrange("p (b v t) -> p b v t", b=2, v=4)

                def score(u):
                    h, qt = u % 16, u // 16
                    nk = P * (qt + 1)
                    b = SC.take(pe)
                    for br in range(2):
                        i = nc.tensor.matmul(b[:, br * nk:(br + 1) * nk], q8[rows_of(h), h // 2, qt * P:(qt + 1) * P],
                                             k8[rows_of(h), br, h // 4, 0:nk], start=True, stop=True)
                    i.then_inc(s_full, 1)

                def weigh(u):
                    h, qt = u % 16, u // 16
                    if h % 4 == 0:
                        out_bank[0] = V.take(pe)
                    for br in range(2):
                        for j in range(qt + 1):
                            col = 1792 + 512 * br + (h // 4) * HD
                            o = (h % 4) * P + br * HD
                            m = nc.tensor.matmul(out_bank[0][:, o:o + HD], pT_ring[u % 3][:, (br * (qt + 1) + j) * P:(br * (qt + 1) + j + 1) * P],
                                                 z[:, j, col:col + HD], start=(j == 0), stop=(j == qt))
                    if h % 4 == 3:
                        m.then_inc(v_full, 1)

                attend(LT * 16, score, lambda u, b: turn_blocks(p_ring[u % 3], 2 * (u // 16 + 1), b), weigh, probs_ready)

            def differential():
                z = zs[3]
                head_features(lambda t, f: z[:, t, f * P:(f + 1) * P], 8, LT)
                head_features(lambda t, f: z[:, t, 1024 + f * P:1024 + (f + 1) * P], 8, LT)
                A.drained(pe)
                q8 = aq.rearrange("p (f t) -> p f t", f=8)
                k8 = ak.rearrange("p (f t) -> p f t", f=8)

                def score(u):
                    h, qt = u % 8, u // 8
                    nk = P * (qt + 1)
                    for m in range(2):
                        b = SC.take(pe)
                        nc.tensor.matmul(b[:, 0:nk], q8[rows_of(m), h, qt * P:(qt + 1) * P],
                                         k8[rows_of(m), h, 0:nk], start=True, stop=True).then_inc(s_full, 1)

                def weigh(u):
                    h, qt = u % 8, u // 8
                    if h % 4 == 0:
                        out_bank[0] = V.take(pe)
                    for j in range(qt + 1):
                        m = nc.tensor.matmul(out_bank[0][:, (h % 4) * P:(h % 4 + 1) * P], pT_ring[u % 3][:, j * P:(j + 1) * P],
                                             z[:, j, 2048 + h * P:2048 + (h + 1) * P], start=(j == 0), stop=(j == qt))
                    if h % 4 == 3:
                        m.then_inc(v_full, 1)

                attend(LT * 8, score, lambda u, b: turn_blocks(p_ring[u % 3], u // 8 + 1, b), weigh, probs_mixed)

            def dilated_heads():
                z = zs[4]
                head_features(lambda t, f: z[:, t, f * P:(f + 1) * P], 6, LT)
                head_features(lambda t, f: z[:, t, 768 + f * P:768 + (f + 1) * P], 6, LT)
                A.drained(pe)
                q6 = aq[:, 0:1536].rearrange("p (f t) -> p f t", f=6)
                k6 = ak[:, 0:1536].rearrange("p (f t) -> p f t", f=6)

                def score(u):
                    h, qt = u % 4, u // 4
                    nk = P * (qt + 1)
                    for part in ((0, 1), (2,)):
                        b = SC.take(pe)
                        for n, g in enumerate(part):
                            hh = g * 4 + h
                            i = nc.tensor.matmul(b[:, n * nk:(n + 1) * nk], q6[rows_of(hh), hh // 2, qt * P:(qt + 1) * P],
                                                 k6[rows_of(hh), hh // 2, 0:nk], start=True, stop=True)
                        i.then_inc(s_full, 1)

                def weigh(u):
                    h, qt = u % 4, u // 4
                    if h % 2 == 0:
                        out_bank[0] = V.take(pe)
                    for j in range(qt + 1):
                        m = nc.tensor.matmul(out_bank[0][:, (h % 2) * 256:(h % 2 + 1) * 256], pT_ring[u % 3][:, j * P:(j + 1) * P],
                                             z[:, j, 1536 + h * 256:1536 + (h + 1) * 256], start=(j == 0), stop=(j == qt))
                    if h % 2 == 1:
                        m.then_inc(v_full, 1)

                attend(LT * 4, score, lambda u, b: turn_blocks(p_ring[u % 3], u // 4 + 1, b), weigh, probs_mixed)

            def stick():
                z = zs[5]
                head_features(lambda t, f: z[:, t, f * P:(f + 1) * P], 8, LT)
                head_features(lambda t, f: z[:, t, 1024 + f * P:1024 + (f + 1) * P], 8, LT)
                A.drained(pe)
                q8 = aq.rearrange("p (f t) -> p f t", f=8)
                k8 = ak.rearrange("p (f t) -> p f t", f=8)

                def score(u):
                    h, qt = u % 16, u // 16
                    nk = P * (qt + 1)
                    b = SC.take(pe)
                    nc.tensor.matmul(b[:, 0:nk], q8[rows_of(h), h // 2, qt * P:(qt + 1) * P], k8[rows_of(h), h // 2, 0:nk],
                                     start=True, stop=True).then_inc(s_full, 1)

                def weigh(u):
                    h, qt = u % 16, u // 16
                    if h % 8 == 0:
                        out_bank[0] = V.take(pe)
                    for j in range(qt + 1):
                        m = nc.tensor.matmul(out_bank[0][:, (h % 8) * HD:(h % 8 + 1) * HD], pT_ring[u % 3][:, j * P:(j + 1) * P],
                                             z[:, j, 2048 + h * HD:2048 + (h + 1) * HD], start=(j == 0), stop=(j == qt))
                    if h % 8 == 7:
                        m.then_inc(v_full, 1)

                attend(LT * 16, score, lambda u, b: turn_blocks(p_ring[u % 3][:, 512:], u // 16 + 1, b), weigh, probs_ready)

            pe.wait_ge(const_loaded, 32)
            pe.wait_ge(small_loaded, 16)
            seen.next(cond_ready)
            for i in range(min(layers, 2)):
                first_layer(i)
            for i in range(2, layers):
                second_layer(i)

        @block.vector
        def _(dve):
            seen = Seen(dve)
            own = {}
            ve = nc.vector

            def signal(ins, semaphore):
                ins.then_inc(semaphore, 1)
                own[semaphore.name] = own.get(semaphore.name, 0) + 1
                return own[semaphore.name]

            def then(ins, semaphore=dve_step):
                dve.wait_ge(semaphore, signal(ins, semaphore))

            def vbank():
                return V.filled_bank(dve)

            def over(v, n):
                return v.unsqueeze(2).broadcast_to([P, v.shape[1], n])

            def under(v, n):
                return v.unsqueeze(1).broadcast_to([P, n, v.shape[1]])

            def inv_root(dst_n, sums_of_squares, width):
                signal(ve.tensor_scalar(sums_of_squares, sums_of_squares, 1.0 / width, EPS, ALU.mult, ALU.add), meansq_ready)
                seen.next(rstd_ready)

            def norm_rows(T):
                seen.next(sumsq_ready, T)
                inv_root(T, ss[:, 0:T], D)
                for t in range(T):
                    signal(ve.tensor_scalar(mix[:, t, :], x[:, t, :], rstd[:, t:t + 1], None, ALU.mult), normed_ready)

            def modulation(i):
                b = vbank()
                then(ve.tensor_tensor(modT[:, :, :], b[:, 0:96].rearrange("p (m s) -> p m s", s=2),
                                      over(sm("mod_b")[:, i * 48:(i + 1) * 48], 2), ALU.add), v_free)
                for which, col, gain in ((0, 8, "norm_mix"), (1, 32, "norm_ffn")):
                    n = ve.scalar_tensor_tensor(modA[:, which], modT[:, col:col + 8, :], 1.0,
                                                over(sm(gain)[:, i * KT:(i + 1) * KT], 2), ALU.add, ALU.mult)
                signal(n, mod_ready)

            def head_squares(src, H, d, at):
                then(ve.tensor_tensor(scratch2[:, 0:H * d], src, src, ALU.mult))
                then(ve.tensor_reduce(head_ss[:, at:at + H], scratch2[:, 0:H * d].rearrange("p (h d) -> p h d", h=H), AX.X, ALU.add))

            def scale_heads(src, H, d, at):
                v = src.rearrange("p (h d) -> p h d", h=H)
                then(ve.tensor_tensor(v, v, over(head_rstd[:, at:at + H], d), ALU.mult))

            def gain_heads(src, H, gain):
                v = src.rearrange("p (h d) -> p h d", h=H)
                then(ve.tensor_tensor(v, v, under(gain, H), ALU.mult))

            def rotate(src, H, t):
                v = src.rearrange("p (h a b f) -> p h a b f", h=H, a=2, b=2)
                c, s = (rope[:, t, n].unsqueeze(1).broadcast_to([P, H, 2, 16]) for n in range(2))
                x1, x2 = v[:, :, :, 0, :], v[:, :, :, 1, :]
                tmp = [turned[:, H * 32 * n:H * 32 * (n + 1)].rearrange("p (h a f) -> p h a f", h=H, a=2) for n in range(4)]
                for n, (half, by) in enumerate(((x1, c), (x2, s), (x2, c), (x1, s))):
                    m = ve.tensor_tensor(tmp[n], half, by, ALU.mult)
                then(m)
                ve.tensor_tensor(x1, tmp[0], tmp[1], ALU.subtract)
                then(ve.tensor_tensor(x2, tmp[2], tmp[3], ALU.add))

            def twice(dst, src, H):
                return ve.tensor_copy(dst.rearrange("p (h two d) -> p h two d", h=H, two=2),
                                      src.rearrange("p (h d) -> p h d", h=H).unsqueeze(2).broadcast_to([P, H, 2, HD]))

            def heads_first():
                dve.wait_ge(a_free, whole["z", 0])
                z = zs[0]
                for t in range(NT):
                    head_squares(z[:, t, 1536:2176], 10, HD, 10 * t)
                inv_root(40, head_ss[:, 0:40], HD)
                for t in range(NT):
                    scale_heads(z[:, t, 1536:2176], 10, HD, 10 * t)
                    gain_heads(z[:, t, 1536:2048], 8, sm("att_q"))
                    gain_heads(z[:, t, 2048:2176], 2, sm("att_k"))
                    if t < LT:
                        rotate(z[:, t, 1536:2176], 10, t)
                    n = twice(mix[:, t, 512:768], z[:, t, 2048:2176], 2)
                signal(n, heads_ready)

            def heads_second():
                dve.wait_ge(a_free, whole["z", 1])
                z = zs[1]
                for t in range(NT):
                    if t < LT:
                        head_squares(z[:, t, 0:1024], 16, HD, 18 * t)
                    head_squares(z[:, t, 1024:1152], 2, HD, 18 * t + 16 if t < LT else 36 + 2 * (t - LT))
                inv_root(40, head_ss[:, 0:40], HD)
                for t in range(NT):
                    if t < LT:
                        scale_heads(z[:, t, 0:1152], 18, HD, 18 * t)
                        gain_heads(z[:, t, 0:1024], 16, sm("swa_q"))
                    else:
                        scale_heads(z[:, t, 1024:1152], 2, HD, 36 + 2 * (t - LT))
                    gain_heads(z[:, t, 1024:1152], 2, sm("swa_k"))
                    if t < LT:
                        rotate(z[:, t, 0:1152], 18, t)
                    n = twice(mix[:, t, 0:256], z[:, t, 1024:1152], 2)
                signal(n, heads_ready)

            def gla():
                for d in range(2):
                    for f in range(2):
                        b = vbank()
                        at = slice((2 * d + f) * 512, (2 * d + f + 1) * 512)
                        bias = sm("gate_b")[:, 2 * d + f:2 * d + f + 1]
                        ve.tensor_scalar(X[0][:, at], b[:, :], bias, 0.0, ALU.add, ALU.min)
                        then(ve.tensor_scalar(X[1][:, at], b[:, :], bias, None, ALU.add), v_free)
                        ve.scalar_tensor_tensor(X[1][:, at], X[0][:, at], 2.0, X[1][:, at], ALU.mult, ALU.subtract)
                signal(ve.memset(cum[:, :, :, :, 0:1].rearrange("p d f s t -> p (d f s) t"), 0.0), gate_in)
                dve.wait_ge(gate_in, own["gate_in"])
                seen.next(gate_soft, 2)
                for d in range(2):
                    for f in range(2):
                        for s in range(2):
                            lo = (2 * d + f) * 512 + s * S
                            n = ve.tensor_tensor_scan(cum[:, d, f, s, 1:S + 1], X[0][:, lo:lo + S], X[1][:, lo:lo + S], 0.0,
                                                      ALU.add, ALU.subtract)
                then(n)

                def halves(v, m):
                    w = v.rearrange("p g (b two m) -> p g b two m", two=2, m=m)
                    return w[:, :, :, 0, :], w[:, :, :, 1, :]

                def exponents(n):
                    m = LEVELS[n]
                    xl = X[n % 2].rearrange("p (d g t) -> p d g t", d=2, g=4)
                    for d in range(2):
                        c = cum[:, d].rearrange("p f s t -> p (f s) t")
                        mid = c[:, :, m:S + 1:2 * m]
                        mid = mid.unsqueeze(3).broadcast_to([P, 4, S // (2 * m), m])
                        el, er = halves(c[:, :, 1 - d:S + 1 - d], m)
                        ol, orr = halves(xl[:, d], m)
                        ve.tensor_tensor(ol, mid, el, ALU.subtract)
                        i = ve.tensor_tensor(orr, er, mid, ALU.subtract)
                    signal(i, expo_in)

                def decayed(n):
                    m = LEVELS[n]
                    xl = X[n % 2].rearrange("p (d g t) -> p d g t", d=2, g=4)
                    q, k = (v.rearrange("p f (s t) -> p (f s) t", s=2) for v in (qT, kT))
                    seen.next(expo_out)
                    for d in range(2):
                        ol, orr = halves(xl[:, d], m)
                        left, right = (k, q) if d == 0 else (q, k)
                        ve.tensor_tensor(ol, ol, halves(left, m)[0], ALU.mult)
                        i = ve.tensor_tensor(orr, orr, halves(right, m)[1], ALU.mult)
                    signal(i, level_ready)

                def quads(v):
                    return v.rearrange("p (j h t) -> p j h t", j=2, h=2)

                def take_pairs(n):
                    for d in range(1 if n == 0 else 2):
                        for s in range(2):
                            for odd in range(2):
                                b = vbank()
                                if n == 0:
                                    signal(ve.tensor_copy(att_other[:, s, :, odd::2, :], quads(b[:, :])), v_free)
                                else:
                                    mask = gla_masks[:, d, n - 1].unsqueeze(1).unsqueeze(1).broadcast_to([P, 2, 2, P])
                                    signal(ve.copy_predicated(att_same[:, s, :, odd::2, :], mask, quads(b[:, :])), v_free)

                exponents(0)
                ve.memset(rows[:, 1024:2048], 0.0)
                for s in range(2):
                    for odd in range(2):
                        b = vbank()
                        signal(ve.tensor_tensor(att_same[:, s, :, odd::2, :], quads(b[:, :]),
                                                cn("diag2").unsqueeze(1).unsqueeze(1).broadcast_to([P, 2, 2, P]), ALU.mult), v_free)
                dve.wait_ge(v_free, own["v_free"])
                decayed(0)
                for n in range(len(LEVELS)):
                    if n + 1 < len(LEVELS):
                        exponents(n + 1)
                    else:
                        xi = X[len(LEVELS) % 2].rearrange("p (w f t) -> p w f t", w=4, f=2)
                        for w, (d, s) in enumerate(((0, CTX), (1, CTX), (0, LAT), (1, LAT))):
                            c = cum[:, d, :, s, :]
                            el = c[:, :, 1 - d:S + 1 - d]
                            if w in (0, 3):
                                i = ve.tensor_tensor(xi[:, w], c[:, :, S:S + 1].broadcast_to([P, 2, S]), el, ALU.subtract)
                            else:
                                i = ve.tensor_copy(xi[:, w], el)
                        signal(i, expo_in)
                    take_pairs(n)
                    if n + 1 < len(LEVELS):
                        decayed(n + 1)
                seen.next(expo_out)
                for w in range(4):
                    by = kT[:, :, S:2 * S] if w < 2 else qT[:, :, 0:S]
                    i = ve.tensor_tensor(xi[:, w], xi[:, w], by, ALU.mult)
                signal(i, level_ready)
                signal(ve.memset(head_ss[:, 0:1], 0.0), gla_done)
                for t in range(NT):
                    b = vbank()
                    then(ve.tensor_copy(mix[:, t, 0:512], b[:, :]), v_free)
                    head_squares(mix[:, t, 0:512], 4, GLA_DV, 4 * t)
                inv_root(16, head_ss[:, 0:16], GLA_DV)
                seen.next(z_act_ready)
                for t in range(NT):
                    scale_heads(mix[:, t, 0:512], 4, GLA_DV, 4 * t)
                    gain_heads(mix[:, t, 0:512], 4, sm("gla_norm"))
                    then(ve.tensor_tensor(mix[:, t, 0:512], mix[:, t, 0:512], zs[0][:, t, 1024:1536], ALU.mult))

            def attention_first():
                for s in range(2):
                    keys = 512 if s == 0 else 256

                    def out(u):
                        qt = u // 8
                        b = vbank()
                        at = s * 16 + qt * 8
                        then(ve.reciprocal(rsum[:, 0:8], sums[:, at:at + 8]))
                        signal(ve.tensor_tensor(mix[:, 2 * s + qt, 512:1024].rearrange("p (h d) -> p h d", h=8),
                                                b[:, :].rearrange("p (h d) -> p h d", h=8), over(rsum[:, 0:8], HD), ALU.mult), v_free)

                    for u in range(LT * 8 + 3):
                        if u < LT * 8:
                            seen.next(raw_full)
                            signal(ve.tensor_reduce(nmax[:, s * 16 + u:s * 16 + u + 1], bank[4 + u % 2][:, 0:keys], AX.X, ALU.max,
                                                    negate=True), max_ready)
                        if u >= 3 and (u - 3) % 8 == 7:
                            out(u - 3)
                seen.next(probs_ready, 32)

            def reuse(u):
                if u >= 3:
                    seen.next(probs_ready)

            def attention_second():
                dve.wait_ge(late_loaded, 16)
                then(ve.tensor_scalar(neg_sink, sm("sink"), -1.0, None, ALU.mult))

                def out(u):
                    b = vbank()
                    at = u - 7
                    then(ve.tensor_tensor(rsum[:, 0:8], sums[:, at:at + 8], esink[:, at:at + 8], ALU.add))
                    then(ve.reciprocal(rsum[:, 0:8], rsum[:, 0:8]))
                    c = (at % 16) * HD
                    signal(ve.tensor_tensor(mix[:, at // 16, c:c + 512].rearrange("p (h d) -> p h d", h=8),
                                            b[:, :].rearrange("p (h d) -> p h d", h=8), over(rsum[:, 0:8], HD), ALU.mult), v_free)

                n_u = LT * 16
                for u in range(n_u + 3):
                    if u < n_u:
                        reuse(u)
                        b = SC.filled_bank(dve)
                        then(ve.tensor_tensor(s_ring[u % 3][:, 0:512], b[:, :], band[:, u // 16, :], ALU.add), s_free)
                        then(ve.tensor_reduce(lam[:, 0:1], s_ring[u % 3][:, 0:512], AX.X, ALU.max, negate=True))
                        signal(ve.tensor_tensor(nmax[:, u:u + 1], lam[:, 0:1], neg_sink[:, u % 16:u % 16 + 1], ALU.min), max_ready)
                    if u >= 3 and (u - 3) % 8 == 7:
                        out(u - 3)
                seen.next(probs_ready, 3)

            def residual(T, src, gate):
                for t in range(T):
                    then(ve.tensor_tensor(src[:, t, :], src[:, t, :], gate_rows[:, t // LT, :], ALU.mult))
                    signal(ve.tensor_tensor(x[:, t, :], x[:, t, :], src[:, t, :], ALU.add), x_ready)
                dve.wait_ge(x_ready, own["x_ready"])

            def routing(i, T):
                L = route[:, 0:20 * T].rearrange("p (t n) -> p t n", t=T)
                gl, el = L[:, :, 0:4], L[:, :, 4:20]
                at = [96]

                def buf(*shape):
                    n = int(np.prod(shape))
                    v = route[:, at[0]:at[0] + n]
                    at[0] += n
                    if len(shape) == 2:
                        return v.rearrange("p (a b) -> p a b", a=shape[0])
                    if len(shape) == 3:
                        return v.rearrange("p (a b c) -> p a b c", a=shape[0], b=shape[1])
                    return v

                b = vbank()
                bias = sm("router_b")[:, 20 * i:20 * i + 20]
                then(ve.tensor_tensor(L, b[:, 0:20 * T].rearrange("p (t n) -> p t n", t=T), under(bias, T), ALU.add), v_free)
                g_max, taken, total, g_weight, e_max = (buf(T) for _ in range(5))
                is_max, chosen, prob, rank, weight = (buf(T, 4) for _ in range(5))
                picked = buf(T, 4, 4)
                before = buf(T, 4, 4)
                ge, ee = (v[:, 0:4 * T].rearrange("p (t n) -> p t n", t=T) for v in route_buf)
                then(ve.tensor_reduce(g_max, gl, AX.X, ALU.max))
                signal(ve.tensor_tensor(ge, gl, over(g_max, 4), ALU.subtract), route_in)
                then(ve.tensor_tensor(is_max, gl, over(g_max, 4), ALU.is_equal))
                then(ve.memset(taken, 0.0))
                for g in range(4):
                    then(ve.tensor_tensor(chosen[:, :, g], is_max[:, :, g], taken, ALU.is_gt))
                    then(ve.tensor_tensor(taken, taken, is_max[:, :, g], ALU.max))
                then(ve.tensor_tensor(picked, el.rearrange("p t (g e) -> p t g e", g=4),
                                      chosen.unsqueeze(3).broadcast_to([P, T, 4, 4]), ALU.mult))
                then(ve.tensor_reduce(weight, picked.rearrange("p t g e -> p t e g"), AX.X, ALU.add))
                then(ve.tensor_reduce(e_max, weight, AX.X, ALU.max))
                signal(ve.tensor_tensor(ee, weight, over(e_max, 4), ALU.subtract), route_in)
                seen.next(route_out)
                then(ve.tensor_reduce(total, ge, AX.X, ALU.add))
                then(ve.reciprocal(g_weight, total))
                then(ve.memset(before, 0.0))
                seen.next(route_out)
                then(ve.tensor_reduce(total, ee, AX.X, ALU.add))
                then(ve.reciprocal(total, total))
                then(ve.tensor_tensor(prob, ee, over(total, 4), ALU.mult))
                for e in range(4):
                    mine = prob[:, :, e:e + 1]
                    if e:
                        n = ve.tensor_tensor(before[:, :, e, 0:e], prob[:, :, 0:e], mine.broadcast_to([P, T, e]), ALU.is_ge)
                    if e < 3:
                        n = ve.tensor_tensor(before[:, :, e, e + 1:4], prob[:, :, e + 1:4], mine.broadcast_to([P, T, 3 - e]), ALU.is_gt)
                then(n)
                then(ve.tensor_reduce(rank, before, AX.X, ALU.add))
                then(ve.tensor_scalar(rank, rank, 2.0, None, ALU.is_lt))
                then(ve.tensor_tensor(weight, prob, rank, ALU.mult))
                then(ve.tensor_reduce(total, weight, AX.X, ALU.add))
                then(ve.reciprocal(total, total))
                then(ve.tensor_tensor(total, total, g_weight, ALU.mult))
                then(ve.tensor_tensor(weight, weight, over(total, 4), ALU.mult))
                then(ve.tensor_tensor(comb[:, :, 0:T].rearrange("p (g e) t -> p t g e", g=4),
                                      chosen.unsqueeze(3).broadcast_to([P, T, 4, 4]),
                                      weight.unsqueeze(2).broadcast_to([P, T, 4, 4]), ALU.mult))

            def experts(i):
                T = NT if i == 0 else LT
                N = T * P
                base, per = NE * i, 2 * T
                d_base = 0 if i == 0 else NE * NT * 2
                comb_flat = comb.rearrange("p e t -> p (e t)")

                def gate(e, parity):
                    for f in range(2):
                        dve.wait_ge(g_free, e * 2 + (f + 1))
                        dve.wait_ge(u_full, e * 2 + (f + 1))
                        ve.tensor_tensor(hid[parity][:, f, 0:N], silu_g[parity][:, f, 0:N], bank[2 + f][:, 0:N],
                                         ALU.mult).then_inc(u_free, 1)

                def add(e, n, first):
                    for t in range(T):
                        for h in range(2):
                            c = t * 2 + h
                            dst = mix[:, t, h * 512:(h + 1) * 512]
                            w = comb_flat[:, e * 4 + t:e * 4 + t + 1] if isinstance(e, int) else comb_flat[:, bass.ds(e * 4 + t, 1)]
                            dve.wait_ge(d_full, n + (c + 1))
                            src = bank[4 + c % 4][:, :]
                            if first:
                                ve.tensor_scalar(dst, src, w, None, ALU.mult).then_inc(d_free, 1)
                            else:
                                dve.wait_ge(d_free, n + (c + 1 - per))
                                ve.scalar_tensor_tensor(dst, src, w, dst, ALU.mult, ALU.add).then_inc(d_free, 1)

                gate(base, 0)
                gate(base + 1, 1)
                add(0, d_base, True)
                with dve.Fori(1, NE // 2) as j:
                    gate(j * 2 + base, 0)
                    add(j * 2 - 1, j * (2 * per) + (d_base - per), False)
                    gate(j * 2 + (base + 1), 1)
                    add(j * 2, j * (2 * per) + d_base, False)
                add(NE - 1, d_base + (NE - 1) * per, False)
                dve.wait_ge(d_free, d_base + NE * per)

            def first_layer(i):
                T = NT if i == 0 else LT
                norm_rows(NT)
                modulation(i)
                if i == 0:
                    heads_first()
                    gla()
                    attention_first()
                else:
                    heads_second()
                    attention_second()
                dve.wait_ge(a_free, whole["y", i])
                residual(T, zo[T], 0)
                norm_rows(T)
                routing(i, T)
                experts(i)
                dve.wait_ge(a_free, whole["gates2", i])
                residual(T, mix, 1)

            def second_layer(i):
                norm_rows(LT)
                dve.wait_ge(a_free, whole["z", i])
                {2: sparse, 3: differential, 4: dilated_heads, 5: stick}[i]()
                lo, hi = {2: (2560, 3584), 3: (3072, 4096), 4: (2560, 3584), 5: (3072, 4096)}[i]
                seen.next(z_act_ready)
                for t in range(LT):
                    signal(ve.tensor_tensor(mix[:, t, :], mix[:, t, :], zs[i][:, t, lo:hi], ALU.mult), mix_ready)
                seen.next(sumsq_ready, LT)
                inv_root(LT, ss[:, 0:LT], D)
                dve.wait_ge(post_loaded, 16 * (i - 1))
                y = zo[LT]
                for t in range(LT):
                    then(ve.scalar_tensor_tensor(y[:, t, :], y[:, t, :], rstd[:, t:t + 1], post_row[:, :], ALU.mult, ALU.mult))
                    signal(ve.tensor_tensor(x[:, t, :], x[:, t, :], y[:, t, :], ALU.add), x_ready)
                dve.wait_ge(x_ready, own["x_ready"])

            def biased(u, bias, slope, maps, split=False):
                nk = bias.shape[1]
                dst = s_ring[u % 3][:, 0:maps * nk].rearrange("p (m k) -> p m k", m=maps)
                if split:
                    for m in range(maps):
                        b = SC.filled_bank(dve)
                        n = signal(ve.scalar_tensor_tensor(dst[:, m, :], bias, slope, b[:, 0:nk], ALU.mult, ALU.add), s_free)
                    dve.wait_ge(s_free, n)
                else:
                    b = SC.filled_bank(dve)
                    then(ve.scalar_tensor_tensor(dst, under(bias, maps), slope, b[:, 0:maps * nk].rearrange("p (m k) -> p m k", m=maps),
                                                 ALU.mult, ALU.add), s_free)
                signal(ve.tensor_reduce(nmax[:, maps * u:maps * (u + 1)], dst, AX.X, ALU.max, negate=True), max_ready)

            def sparse():
                z = zs[2]
                ve.memset(x[:, 2, :], 0.0)
                ve.memset(rows[:, 1024:2048], 0.0)
                ve.memset(cmp_p, 0.0)
                for t in range(LT):
                    kd = kdup[:, t * 1024:(t + 1) * 1024]
                    twice(kd[:, 0:512], z[:, t, 1536:1792], 4)
                    twice(kd[:, 512:1024], z[:, t, 2048:2304], 4)
                    n = twice(cdup[:, t, :], z[:, t, 1024:1536], 8)
                signal(n, heads_ready)
                seen.next(cmp_out)
                then(ve.tensor_scalar(gates, gates, 1.0, None, ALU.add))
                then(ve.reciprocal(gates, gates))
                gate = gates.rearrange("p (t b h) -> p t b h", t=LT, b=3)
                dve.wait_ge(a_free, whole["pairs"])
                for src, name in ((0, "pos_k"), (1, "pos_v")):
                    v = pairs[src].rearrange("p h (r b) -> p h r b", b=8)
                    o = blk[src].rearrange("p l (h n) -> p l h n", h=4)
                    for half in range(2):
                        pos = sm(name)[:, 8 * half:8 * half + 8]
                        for h in range(4):
                            n = ve.tensor_tensor(o[:, 8 * half:8 * half + 8, h, :],
                                                 v[:, h, half:half + CMP_N, :].rearrange("p n b -> p b n"),
                                                 over(pos, CMP_N), ALU.add)
                    signal(n, cmp_blk)
                for src in range(2):
                    b = vbank()
                    then(ve.tensor_copy(hidden[0:60, src * 256:(src + 1) * 256], b[0:60, 0:256]), v_free)
                h, g = hidden[0:60, :], gelu_t[0:60, :]
                then(ve.tensor_tensor(g, h, h, ALU.mult))
                then(ve.tensor_scalar(g, g, 0.044715, 1.0, ALU.mult, ALU.add))
                signal(ve.scalar_tensor_tensor(g, g, 2.0 * float(np.sqrt(2.0 / np.pi)), h, ALU.mult, ALU.mult), cmp_in)
                seen.next(cmp_out)
                then(ve.tensor_scalar(g, g, 1.0, None, ALU.add))
                then(ve.reciprocal(g, g))
                signal(ve.tensor_tensor(h, h, g, ALU.mult), cmp_hid)
                for qt in range(LT):
                    sc = cmp_s.rearrange("p (h n) -> p h n", h=16)
                    dve.wait_ge(late_loaded, 16)
                    for odd in range(2):
                        b = SC.filled_bank(dve)
                        dst, bias = (v.rearrange("p (h o n) -> p h o n", o=2, n=CMP_N)[:, :, odd, :] for v in (cmp_s, cmp_bias[:, qt, :]))
                        then(ve.tensor_tensor(dst, b[:, 0:120].rearrange("p (h n) -> p h n", h=8), bias, ALU.add), s_free)
                    then(ve.tensor_reduce(rsum[:, 0:16], sc, AX.X, ALU.max))
                    signal(ve.tensor_tensor(sc, sc, over(rsum[:, 0:16], CMP_N), ALU.subtract), cmp_in)
                    seen.next(cmp_out)
                    then(ve.tensor_tensor(sc, sc, under(cmp_valid[:, qt, :], 16), ALU.mult))
                    then(ve.tensor_reduce(rsum[:, 0:16], sc, AX.X, ALU.add))
                    then(ve.tensor_scalar(rsum[:, 0:16], rsum[:, 0:16], TINY, None, ALU.max))
                    then(ve.reciprocal(rsum[:, 0:16], rsum[:, 0:16]))
                    then(ve.tensor_tensor(rsum[:, 0:16], rsum[:, 0:16], gate[:, qt, 0, :], ALU.mult))
                    signal(ve.tensor_tensor(cmp_p.rearrange("p (h n) -> p h n", h=16)[:, :, 0:CMP_N], sc,
                                            over(rsum[:, 0:16], CMP_N), ALU.mult), cmp_probs)
                    for half in range(2):
                        b = vbank()
                        signal(ve.tensor_copy(mix[:, qt, half * 512:(half + 1) * 512], b[:, :]), v_free)
                slopes = alibi(16)

                def out(u):
                    qt, h0 = u // 16, u % 16 - 3
                    b = vbank()
                    then(ve.tensor_scalar(rsum[:, 0:8], sums[:, 2 * u - 6:2 * u + 2], TINY, None, ALU.max))
                    then(ve.reciprocal(rsum[:, 0:8], rsum[:, 0:8]))
                    then(ve.tensor_tensor(coef[:, 0:8].rearrange("p (h b) -> p h b", h=4),
                                          rsum[:, 0:8].rearrange("p (h b) -> p h b", h=4),
                                          gate[:, qt, 1:3, h0:h0 + 4].rearrange("p b h -> p h b"), ALU.mult))
                    then(ve.tensor_tensor(weighed.rearrange("p (m d) -> p m d", m=8), b[:, :].rearrange("p (m d) -> p m d", m=8),
                                          over(coef[:, 0:8], HD), ALU.mult), v_free)
                    dst = mix[:, qt, h0 * HD:(h0 + 4) * HD].rearrange("p (h d) -> p h d", h=4)
                    w = weighed.rearrange("p (h b d) -> p h b d", h=4, b=2)
                    for br in range(2):
                        then(ve.tensor_tensor(dst, dst, w[:, :, br, :], ALU.add))

                n_u = LT * 16
                for u in range(n_u + 3):
                    if u < n_u:
                        reuse(u)
                        biased(u, causal[:, u // 16, 0:P * (u // 16 + 1)], slopes[u % 16], 2)
                    if u >= 3 and (u - 3) % 4 == 3:
                        out(u - 3)
                seen.next(probs_ready, 3)

            def differential():
                lr = sm("lam", "p (a b n) -> p a b n", a=2, b=2)
                prod = scratch[:, 0:128].rearrange("p (a n) -> p a n", a=2)
                then(ve.tensor_tensor(prod, lr[:, :, 0, :], lr[:, :, 1, :], ALU.mult))
                signal(ve.tensor_reduce(lam[:, 0:2], prod, AX.X, ALU.add), cmp_in)
                seen.next(cmp_out)
                then(ve.tensor_tensor(lam[:, 4:5], lam[:, 3:4], lam[:, 2:3], ALU.subtract))
                then(ve.tensor_scalar(lam[:, 5:6], lam[:, 4:5], -LAMBDA_INIT, None, ALU.add))
                slopes = alibi(8)

                def combine(u):
                    nk = P * (u // 8 + 1)
                    seen.next(maps_ready)
                    p = p_ring[u % 3]
                    r = rsum[:, u % 2 * 2:u % 2 * 2 + 2]
                    then(ve.tensor_scalar(r, sums[:, 2 * u:2 * u + 2], TINY, None, ALU.max))
                    then(ve.reciprocal(r, r))
                    then(ve.tensor_scalar(p[:, nk:2 * nk], p[:, nk:2 * nk], r[:, 1:2], lam[:, 5:6], ALU.mult, ALU.mult))
                    signal(ve.scalar_tensor_tensor(p[:, 0:nk], p[:, 0:nk], r[:, 0:1], p[:, nk:2 * nk], ALU.mult, ALU.add), probs_mixed)

                n_u = LT * 8
                for u in range(n_u + 4):
                    if u < n_u:
                        biased(u, causal[:, u // 8, 0:P * (u // 8 + 1)], slopes[u % 8], 2, split=True)
                    if 1 <= u <= n_u:
                        combine(u - 1)
                    if u >= 4 and (u - 4) % 4 == 3:
                        v, b = u - 4, vbank()
                        c = (v % 8 - 3) * P
                        signal(ve.tensor_copy(mix[:, v // 8, c:c + 512], b[:, :]), v_free)
                dve.wait_ge(v_free, own["v_free"])
                for t in range(LT):
                    head_squares(mix[:, t, :], 8, 2 * HD, 8 * t)
                inv_root(16, head_ss[:, 0:16], 2 * HD)
                for t in range(LT):
                    scale_heads(mix[:, t, :], 8, 2 * HD, 8 * t)
                    v = mix[:, t, :].rearrange("p (h d) -> p h d", h=8)
                    then(ve.scalar_tensor_tensor(v, v, 1.0 - LAMBDA_INIT, under(sm("sub_gain"), 8), ALU.mult, ALU.mult))

            def dilated_heads():
                dve.wait_ge(dilated_loaded, 16)
                slopes = alibi(12)

                def soften(u):
                    h, qt = u % 4, u // 4
                    nk = P * (qt + 1)
                    s = s_ring[u % 3][:, 0:3 * nk]
                    for part in ((0, 1), (2,)):
                        b = SC.filled_bank(dve)
                        for n, g in enumerate(part):
                            i = ve.scalar_tensor_tensor(s[:, g * nk:(g + 1) * nk], dilated[:, g, qt, 0:nk], slopes[g * 4 + h],
                                                        b[:, n * nk:(n + 1) * nk], ALU.mult, ALU.add)
                        then(i, s_free)
                    signal(ve.tensor_reduce(nmax[:, u:u + 1], s, AX.X, ALU.max, negate=True), max_ready)

                def combine(u):
                    nk = P * (u // 4 + 1)
                    seen.next(maps_ready)
                    p = p_ring[u % 3]
                    then(ve.tensor_tensor(p[:, 0:nk], p[:, 0:nk], p[:, nk:2 * nk], ALU.add))
                    signal(ve.tensor_tensor(p[:, 0:nk], p[:, 0:nk], p[:, 2 * nk:3 * nk], ALU.add), probs_mixed)

                n_u = LT * 4
                for u in range(n_u + 4):
                    if u < n_u:
                        soften(u)
                    if 1 <= u <= n_u:
                        combine(u - 1)
                    if u >= 4 and (u - 4) % 2 == 1:
                        v, b = u - 4, vbank()
                        r = rsum[:, v // 2 % 2 * 2:v // 2 % 2 * 2 + 2]
                        then(ve.reciprocal(r, sums[:, v - 1:v + 1]))
                        c = (v % 4 - 1) * 256
                        signal(ve.tensor_tensor(mix[:, v // 4, c:c + 512].rearrange("p (h d) -> p h d", h=2),
                                                b[:, :].rearrange("p (h d) -> p h d", h=2), over(r, 256), ALU.mult), v_free)
                dve.wait_ge(v_free, own["v_free"])

            def stick():
                n_u = LT * 16
                for u in range(n_u + 4):
                    if u < n_u:
                        nk = P * (u // 16 + 1)
                        s = s_ring[u % 3]
                        b = SC.filled_bank(dve)
                        then(ve.tensor_tensor(s[:, 0:nk], b[:, 0:nk], strict[:, u // 16, 0:nk], ALU.add), s_free)
                        then(ve.tensor_scalar(s[:, 256:256 + nk], s[:, 0:nk], 0.0, None, ALU.max))
                        signal(ve.scalar_tensor_tensor(s[:, 512:512 + nk], s[:, 256:256 + nk], -2.0, s[:, 0:nk], ALU.mult, ALU.add), soft_in)
                    if 1 <= u <= n_u:
                        v = u - 1
                        nk = P * (v // 16 + 1)
                        s, p = s_ring[v % 3], p_ring[v % 3]
                        seen.next(soft_out, 2)
                        reuse(v)
                        dve.wait_ge(soft_in, own["soft_in"])
                        then(ve.tensor_tensor_scan(p[:, 0:nk][:, ::-1], s[:, 256:256 + nk][:, ::-1], s[:, 512:512 + nk][:, ::-1], 0.0,
                                                   ALU.add, ALU.add))
                        signal(ve.tensor_tensor(p[:, 256:256 + nk], s[:, 0:nk], p[:, 0:nk], ALU.subtract), max_ready)
                    if u >= 4 and (u - 4) % 8 == 7:
                        v, b = u - 4, vbank()
                        c = (v % 16 - 7) * HD
                        signal(ve.tensor_copy(mix[:, v // 16, c:c + 512], b[:, :]), v_free)
                seen.next(probs_ready, 3)
                dve.wait_ge(v_free, own["v_free"])

            scratch2 = scratch
            turned = ar(5632, 2304)
            neg_sink = coef[:, 0:16]
            dve.wait_ge(small_loaded, 16)
            dve.wait_ge(const_loaded, 32)
            for i in range(min(layers, 2)):
                first_layer(i)
            for i in range(2, layers):
                second_layer(i)

        @block.gpsimd
        def _(pool):
            seen = Seen(pool)
            nc.gpsimd.memset(half_neg[:, :], -0.5).then_inc(pool_step, 1)
            pool.wait_ge(pool_step, 1)

            def inv_root(dst, src, n):
                seen.next(meansq_ready)
                nc.gpsimd.tensor_tensor(dst[:, 0:n], src[:, 0:n], half_neg[:, 0:n], ALU.pow).then_inc(rstd_ready, 1)

            def rows_inv_root(T):
                inv_root(rstd, ss, T)

            def load_post(i, x_tiles):
                if x_tiles:
                    pool.wait_ge(x_ready, x_tiles)
                pool.dma_start(post_row[:, :], d_post[i - 2:i - 1, :].broadcast_to([P, D])).then_inc(post_loaded, 16)

            if layers > 2:
                load_post(2, 0)
            rows_inv_root(NT)
            inv_root(head_rstd, head_ss, 40)
            inv_root(head_rstd, head_ss, 16)
            if layers > 1:
                pool.wait_ge(gla_done, 1)
                pool.dma_start(phase[:, 0:N_LATE], d_late).then_inc(late_loaded, 16)
            rows_inv_root(NT)
            if layers > 1:
                rows_inv_root(NT)
                inv_root(head_rstd, head_ss, 40)
                rows_inv_root(LT)
            for i in range(2, layers):
                rows_inv_root(LT)
                if i == 3:
                    inv_root(head_rstd, head_ss, 16)
                rows_inv_root(LT)
                x_tiles = 12 + 2 * (i - 1)
                if i + 1 < layers:
                    load_post(i + 1, x_tiles)
                if i == 2 and layers > 4:
                    pool.dma_start(rows[:, :], d_dilated).then_inc(dilated_loaded, 16)

        @block.sync
        def _(sp):
            sp.dma_start(small[:, :], d_small).then_inc(small_loaded, 16)
            sp.dma_start(x[:, 0:LT, :], d_x.rearrange("(t p) n -> p t n", p=P)).then_inc(x_loaded, 16)
            sp.dma_start(x[:, LT:NT, :], d_ctx.rearrange("(t p) n -> p t n", p=P)).then_inc(x_loaded, 16)
            n_res = N_CONST - 2 * 7 * P
            sp.dma_start(const[:, :], d_const[:, 0:n_res]).then_inc(const_loaded, 16)
            sp.dma_start(phase[:, 0:2 * 7 * P], d_const[:, n_res:N_CONST]).then_inc(const_loaded, 16)

            def load(n):
                slot = tenancy[n][0]
                if n >= SLOTS:
                    sp.wait_ge(*tenancy[n - SLOTS][1:])
                sp.dma_start(ring[:, slot, :], d_w[n]).then_inc(slot_full[slot], 16)

            def expert_loads(i):
                first, half0, d_base = moe_at[i]
                base, per = NE * i, 2 * (NT if i == 0 else LT)

                def slot(c):
                    return (first + c) % SLOTS

                def used(kind, e, kh, k0=0):
                    if kind == "up":
                        return (chunk_used, e + (half0 + 1)) if kh == 0 else (u_full, e * 2 + (2 * base + 2))
                    return d_full, e * per + (d_base + per)

                order = []
                for kind, e in expert_order():
                    order += [(kind, e, 0), (kind, e, 1)] if kind == "up" else [(kind, e, 0)]

                def load_c(c):
                    prev = first + c - SLOTS
                    if c >= SLOTS:
                        sp.wait_ge(*used(*order[c - SLOTS]))
                    elif prev >= 0:
                        sp.wait_ge(*tenancy[prev][1:])
                    sp.dma_start(ring[:, slot(c), :], d_w[first + c]).then_inc(slot_full[slot(c)], 16)

                for c in range(5 + SLOTS):
                    load_c(c)
                with sp.Fori(2, NE // 2) as j:
                    for q, (kind, lead, kh) in enumerate((("up", 0, 0), ("up", 0, 1), ("down", -1, 0),
                                                          ("up", 1, 0), ("up", 1, 1), ("down", 0, 0))):
                        sp.wait_ge(*used(kind, j * 2 + (lead - 2), kh))
                        src = d_w[bass.ds(j * 6 + (first + 5 + q - 6), 1)].rearrange("a p n -> (a p) n")
                        sp.dma_start(ring[:, slot(5 + q), :], src).then_inc(slot_full[slot(5 + q)], 16)
                c = 3 * NE - 1
                sp.wait_ge(*used(*order[c - SLOTS]))
                sp.dma_start(ring[:, slot(c), :], d_w[first + c]).then_inc(slot_full[slot(c)], 16)
                for c in range(3 * NE):
                    kind, e, kh = order[c]
                    tenancy[first + c][1:] = used(kind, e, kh)

            n = 0
            for i in range(min(layers, 2)):
                while n < moe_at[i][0]:
                    load(n)
                    n += 1
                expert_loads(i)
                n += 3 * NE
            while n < len(tenancy):
                load(n)
                n += 1
            sp.wait_ge(x_ready, {1: 8, 2: 12}.get(layers, 12 + 2 * (layers - 2)))
            sp.dma_start(d_out.rearrange("(t p) n -> p t n", p=P), x[:, 0:LT, :]).then_inc(out_done, 16)
            sp.wait_ge(out_done, 16)


def kernel(**inputs):
    import concourse.bacc as bacc
    from concourse.bass_utils import run_bass_kernel_spmd

    nc = bacc.Bacc("TRN2", target_bir_lowering=False, num_devices=1)
    laid = host_layout(inputs)
    arrays, aps = {}, []
    for name in ("x", "ctx", "weights", "small", "norm_post", "const", "late", "dilated"):
        arrays[name + "_dram"] = laid[name]
        aps.append(nc.dram_tensor(name + "_dram", laid[name].shape, F32, kind="ExternalInput").ap())
    aps.append(nc.dram_tensor("out_dram", (S, D), F32, kind="ExternalOutput").ap())
    build_program(nc, *aps)
    r = run_bass_kernel_spmd(nc, [arrays], core_ids=[0])
    return r.results[0]["out_dram"].reshape(1, S, D)
```

```python
from contextlib import ExitStack

import numpy as np

import concourse.bass as bass
from concourse import mybir

F32 = mybir.dt.float32
F32R = mybir.dt.float32r
U32 = mybir.dt.uint32
ACT = mybir.ActivationFunctionType
ALU = mybir.AluOpType
AX = mybir.AxisListType

P = 128
S = 256
D = 1024
KT = D // P
LAT, CTX = 0, 1
NT = 2 * S // P
LT = S // P
HALF = 4 * 512
SLOTS = 3
NEG = -1e30
EPS = 1e-6
TINY = 1e-30
HD = 64
QSCALE = HD ** -0.5

N_MOD = 6
MOD_STEPS = 2 * N_MOD * D // 512
MOD_EARLY = 2 * D // 512
MOD_HEADS, MOD_LEVEL = 5, 3
GLA_H, GLA_DK, GLA_DV = 4, 64, 128
GLA_GATE_NORM = 16.0
GATE_RANK = 16
LEVELS = [128, 64, 32, 16, 8, 4, 2, 1]
NE, NG, EPG = 16, 4, 4
FE = 256
CMP_N, CMP_L, CMP_ST = (S - 32) // 16 + 1, 32, 16
LAMBDA_INIT = 0.8 - 0.6 * float(np.exp(-0.3))
IN_BLOCKS = {2: 7, 3: 8, 4: 7, 5: 8}
C_PATTERNS = ((128, 1), (512, 4), (2048, 16))


def alibi(n):
    return [float(np.float32(2.0 ** (-8.0 * (i + 1) / n))) for i in range(n)]


def fields(table):
    at, out = 0, {}
    for name, width in table:
        out[name] = (at, at + width)
        at += width
    return out, at


SMALL, N_SMALL = fields([
    ("cond", KT * 2), ("mod_b", 2 * 48), ("norm_mix", 2 * KT), ("norm_ffn", 2 * KT), ("norm_pre", 4 * KT),
    ("gate_b", 4), ("att_q", HD), ("att_k", HD), ("swa_q", HD), ("swa_k", HD), ("gla_norm", GLA_DV),
    ("sub_gain", 2 * HD), ("router_b", 2 * 20), ("sink", 16), ("lam", 4 * HD), ("pos_k", 16), ("pos_v", 16),
    ("router_w", 2 * KT * 20), ("lr_w", KT * 32), ("gl_w", KT * 48), ("gate_w", 2 * 256),
    ("w2_k", 2 * 128), ("w2_v", 2 * 64)])
CONST, N_CONST = fields([("ident", P), ("causal", LT * S), ("rope", LT * 64), ("diag2", P),
                         ("gla_masks", 2 * 7 * P)])
LATE, N_LATE = fields([("band", LT * 512), ("cmp_bias", LT * 16 * CMP_N), ("cmp_valid", LT * CMP_N)])
PHASE = max(2 * 7 * P, N_LATE)
DILATED, N_DILATED = fields([("dilated", 3 * LT * S), ("strict", LT * S)])


STREAM, N_CHUNKS = fields(
    [("mod_early", 2 * MOD_EARLY), ("in0", 9), ("mod_late", 2 * (MOD_STEPS - MOD_EARLY)), ("out0", 4), ("experts0", 3 * NE),
     ("in1", 5), ("out1", 4), ("experts1", 3 * NE), ("in2", 2 * IN_BLOCKS[2]), ("compress", 4), ("out2", 4)]
    + [(f"{kind}{i}", 2 * n) for i in (3, 4, 5) for kind, n in (("in", IN_BLOCKS[i]), ("out", 2))])


def const_arrays():
    p = np.arange(P)
    t = np.arange(S).reshape(LT, P)
    k = np.arange(S)
    dist = t[:, :, None] - k[None, None, :]
    causal = np.where(dist >= 0, -dist, NEG)
    inv = (np.float32(10000.0) ** (-np.arange(0, 32, 2, dtype=np.float32) / np.float32(32))).astype(np.float32)
    row, col = (np.arange(S) // 64).astype(np.float32), (np.arange(S) % 64).astype(np.float32)
    ang = np.stack([row[:, None] * inv, col[:, None] * inv], 1)
    rope = np.stack([np.cos(ang), np.sin(ang)], 1).reshape(LT, P, 64)
    masks = np.zeros((2, 7, P, P))
    for n, m in enumerate(LEVELS[1:]):
        blk, right = p // (2 * m), (p // m) % 2
        fwd = (blk[:, None] == blk[None, :]) & (right[:, None] == 0) & (right[None, :] == 1)
        masks[0, n], masks[1, n] = fwd, fwd.T
    band = np.zeros((LT, P, 512))
    band[:, :, :S] = np.where(np.abs(dist) <= 128, 0.0, NEG)
    end = CMP_ST * np.arange(CMP_N) + CMP_L - 1
    cd = t[:, :, None] - end[None, None, :]
    sl = np.array(alibi(16))
    cmp_bias = np.where(cd[:, :, None, :] >= 0, -sl[None, None, :, None] * cd[:, :, None, :], NEG)
    dil = np.stack([np.where((dist >= 0) & (dist <= w) & (dist % d == 0), -dist, NEG) for w, d in C_PATTERNS])

    def pack(a):
        return np.moveaxis(a, -2, 0).reshape(P, -1).astype(np.float32)

    const = np.concatenate([np.eye(P), pack(causal), pack(rope), 2 * np.eye(P), pack(masks)], 1)
    late = np.concatenate([pack(band), np.moveaxis(cmp_bias, 1, 0).reshape(P, -1),
                           pack((cd >= 0).astype(np.float64))], 1)
    dilated = np.concatenate([pack(dil), pack(np.where(dist > 0, 0.0, NEG))], 1)
    return [np.ascontiguousarray(a, np.float32) for a in (const, late, dilated)]


def by_rows(w):
    return w.reshape(-1, P, w.shape[1]).transpose(1, 0, 2)


def chunks_of(w):
    r = by_rows(w)
    out = []
    for n in range(0, w.shape[1], 512):
        if n + 512 <= w.shape[1]:
            out += [r[:, 0:4, n:n + 512], r[:, 4:8, n:n + 512]]
        else:
            out.append(r[:, :, n:n + 256])
    return out


def expert_order():
    out = [("up", 0), ("up", 1), ("down", 0)]
    for i in range(1, NE // 2):
        out += [("up", 2 * i), ("down", 2 * i - 1), ("up", 2 * i + 1), ("down", 2 * i)]
    return out + [("down", NE - 1)]


def expert_chunks(gate, up, down):
    out = []
    for kind, e in expert_order():
        if kind == "up":
            out += chunks_of(np.concatenate([gate[e // EPG, e % EPG], up[e // EPG, e % EPG]], 1))
        else:
            out.append(by_rows(down[e // EPG, e % EPG]))
    return out


def host_layout(a):
    a = {k: np.asarray(v) for k, v in a.items()}
    ev, od, aw, cw = a["ev_w_in"][0], a["od_w_in"][0], a["a_w_in_2"][0], a["c_w_in_2"][0]
    mod = chunks_of(np.concatenate(list(a["mod_w"]), 1))
    w = mod[:2 * MOD_EARLY]
    w += chunks_of(np.concatenate([ev[:, 0:1536], ev[:, 1568:2336]], 1))
    w += mod[2 * MOD_EARLY:]
    w += chunks_of(a["ev_w_out"][0])
    w += expert_chunks(a["exp_w_gate"][0], a["exp_w_up"][0], a["exp_w_down"][0])
    w += chunks_of(od[:, 1024:1280]) + chunks_of(od[:, 0:1024])
    w += chunks_of(a["od_w_out"][0])
    w += expert_chunks(a["exp_w_gate"][1], a["exp_w_up"][1], a["exp_w_down"][1])
    w += chunks_of(np.concatenate([aw[:, 0:2560], aw[:, 2608:3632]], 1))
    for name in ("a_cmp_w1_k_2", "a_cmp_w1_v_2"):
        r = by_rows(a[name][0])
        w += [r[:, 0:8], r[:, 8:16]]
    w += chunks_of(a["a_w_out_2"][0])
    w += chunks_of(a["b_w_in_2"][0]) + chunks_of(a["b_w_out_2"][0])
    w += chunks_of(cw) + chunks_of(a["c_w_out_2"][0])
    w += chunks_of(a["d_w_in_2"][0]) + chunks_of(a["d_w_out_2"][0])
    weights = np.empty((len(w), P, HALF), np.float32)
    for n, c in enumerate(w):
        weights[n] = c.reshape(P, HALF)

    def cols(v):
        v = v.reshape(-1, P)
        return v.T

    def row(v):
        return np.broadcast_to(v.reshape(1, -1), (P, v.size))

    def pos(v):
        return v.reshape(16, P).T

    gate_w = np.zeros((P, 2, 256), np.float32)
    gate_w[0:16, 0], gate_w[16:32, 1] = a["gla_gate_w"][0, 0], a["gla_gate_w"][0, 1]
    cond = np.stack([cols(a["c"]), cols(a["c_ctx"])], 2)
    router_w = np.concatenate([a["router_group_w"], a["router_expert_w"]], 2)
    router_b = np.concatenate([a["router_group_b"], a["router_expert_b"]], 1)
    w2k = by_rows(a["a_cmp_w2_k_2"][0])
    parts = {
        "cond": cond, "mod_b": cols(a["mod_b"]), "norm_mix": cols(a["norm_mix"]), "norm_ffn": cols(a["norm_ffn"]),
        "norm_pre": cols(a["norm_pre_2"]), "gate_b": cols(a["gla_gate_b"][0]),
        "att_q": row(a["att_q_norm"]), "att_k": row(a["att_k_norm"]), "swa_q": row(a["swa_q_norm"]),
        "swa_k": row(a["swa_k_norm"]), "gla_norm": row(a["gla_out_norm"]), "sub_gain": row(a["b_sub_gain_2"]),
        "router_b": row(router_b), "sink": row(a["swa_sink"]), "lam": row(a["b_lambda_2"]),
        "pos_k": pos(a["a_cmp_pos_k_2"]), "pos_v": pos(a["a_cmp_pos_v_2"]),
        "router_w": np.stack([by_rows(router_w[i]) for i in range(2)], 1),
        "lr_w": by_rows(ev[:, 1536:1568]), "gl_w": by_rows(aw[:, 2560:2608]), "gate_w": gate_w,
        "w2_k": np.concatenate([w2k, w2k], 2), "w2_v": by_rows(a["a_cmp_w2_v_2"][0]),
    }
    small = np.empty((P, N_SMALL), np.float32)
    for name, (lo, hi) in SMALL.items():
        small[:, lo:hi] = parts[name].reshape(P, hi - lo)
    const, late, dilated = const_arrays()
    return {
        "x": np.ascontiguousarray(a["x"][0]), "ctx": np.ascontiguousarray(a["ctx"][0]), "weights": weights,
        "small": small, "norm_post": np.ascontiguousarray(a["norm_post_2"]),
        "const": const, "late": late, "dilated": dilated,
    }


class Banks:

    def __init__(self, banks, full, free):
        self.banks, self.full, self.free = banks, full, free
        self.fills = self.drains = 0

    def take(self, pe):
        n = self.fills
        if n >= len(self.banks):
            pe.wait_ge(self.free, n - len(self.banks) + 1)
        self.fills += 1
        return self.banks[n % len(self.banks)]

    def drained(self, pe, fills=None):
        fills = self.fills if fills is None else fills
        if fills:
            pe.wait_ge(self.free, fills)

    def filled_bank(self, eng):
        self.drains += 1
        eng.wait_ge(self.full, self.drains)
        return self.banks[(self.drains - 1) % len(self.banks)]


class Seen:

    def __init__(self, eng):
        self.eng, self.count = eng, {}

    def next(self, semaphore, n=1):
        self.count[semaphore.name] = self.count.get(semaphore.name, 0) + n
        self.eng.wait_ge(semaphore, self.count[semaphore.name])


def build_program(nc, d_x, d_ctx, d_w, d_small, d_post, d_const, d_late, d_dilated, d_out, layers=6):
    with ExitStack() as stack:
        def sb(name, *shape):
            return stack.enter_context(nc.sbuf_tensor(name, [P, *shape], F32))

        def sem(name):
            return stack.enter_context(nc.semaphore(name))

        def shared(dtype):
            return [nc.sbuf_tensor(f"{name}_{dtype.name}", [P, *shape], dtype)
                    for name, shape in (("x", (NT, D)), ("ring", (SLOTS, HALF)), ("hT", (KT * 2 * S,)),
                                        ("Z", (NT * 2336,)), ("mix", (NT, D)))]

        bank = [stack.enter_context(nc.psum_tensor(f"bank{i}", [P, 512], F32)) for i in range(8)]

        with ExitStack() as zone:
            x, ring, hT_flat, Z, mix = (zone.enter_context(t) for t in shared(F32))
        x_r, ring_low, hT_r, Z_r, mix_r = (stack.enter_context(t) for t in shared(F32R))
        ring_high = stack.enter_context(nc.sbuf_tensor("ring_high", [P, SLOTS, HALF], F32R))
        rows = sb("rows", 2 * D)
        const = sb("const", N_CONST - 2 * 7 * P)
        phase = sb("phase", PHASE)
        small = sb("small", N_SMALL)
        post_row = sb("post_row", D)
        arena = sb("arena", 8200)
        scratch = sb("scratch", 1024)
        stat = sb("stat", 768)
        modT = sb("modT", 2 * 48, 2)
        modA = sb("modA", 2, 2, KT, 2)
        cond = sb("cond", KT, 2)
        half_neg = sb("half_neg", 64)

        hT4 = hT_flat[:, :].rearrange("p (k t) -> p k t", k=KT)
        hT2 = hT_flat[:, 0:KT * S].rearrange("p (k t) -> p k t", k=KT)
        hT_spare = hT_flat[:, KT * S:]
        split_at = {"experts": (Z_r[:, 0:KT * 2 * S], Z_r[:, KT * 2 * S:2 * KT * 2 * S]),
                    "project": (x_r[:, LT:NT, :].rearrange("p t n -> p (t n)"), mix_r[:, LT:NT, :].rearrange("p t n -> p (t n)"))}

        def split_views(name, T):
            return [v[:, 0:KT * T * P].rearrange("p (k t) -> p k t", k=KT) for v in split_at[name]]


        def sm(name, pattern=None, **sizes):
            lo, hi = SMALL[name]
            v = small[:, lo:hi]
            return v.rearrange(pattern, **sizes) if pattern else v

        def cn(name):
            lo, hi = CONST[name]
            return const[:, lo:hi]

        ident = cn("ident")
        causal = cn("causal").rearrange("p (t k) -> p t k", t=LT)
        rope = cn("rope").rearrange("p (t c a f) -> p t c a f", t=LT, c=2, a=2)
        gla_masks = phase[:, 0:2 * 7 * P].rearrange("p (d l t) -> p d l t", d=2, l=7).bitcast(U32)

        def late(name):
            lo, hi = LATE[name]
            return phase[:, lo:hi]

        band = late("band").rearrange("p (t k) -> p t k", t=LT)
        cmp_bias = late("cmp_bias").rearrange("p (t n) -> p t n", t=LT)
        cmp_valid = late("cmp_valid").rearrange("p (t n) -> p t n", t=LT)
        dilated = rows[:, 0:3 * LT * S].rearrange("p (g t k) -> p g t k", g=3, t=LT)
        strict = rows[:, 3 * LT * S:4 * LT * S].rearrange("p (t k) -> p t k", t=LT)
        gate_rows = rows[:, :].rearrange("p (s n) -> p s n", s=2)

        x_loaded, small_loaded, const_loaded = sem("x_loaded"), sem("small_loaded"), sem("const_loaded")
        late_loaded, dilated_loaded, post_loaded = sem("late_loaded"), sem("dilated_loaded"), sem("post_loaded")
        slot_full = [sem(f"slot_full{s}") for s in range(SLOTS)]
        high_ready = sem("high_ready")
        low_ready = sem("low_ready")
        act_high = sem("act_high")
        act_low = sem("act_low")
        hid_high_ready = sem("hid_high_ready")
        hid_ready = sem("hid_ready")
        chunk_used = sem("chunk_used")
        a_full, a_free = sem("a_full"), sem("a_free")
        s_full, s_free = sem("s_full"), sem("s_free")
        v_full, v_free = sem("v_full"), sem("v_free")
        masks_loaded = sem("masks_loaded")
        cond_ready = sem("cond_ready")
        mod_full = sem("mod_full")
        mod_copied = sem("mod_copied")
        mod_turned = sem("mod_turned")
        mod_ready = sem("mod_ready")
        sumsq_ready = sem("sumsq_ready")
        meansq_ready = sem("meansq_ready")
        rstd_ready = sem("rstd_ready")
        normed_ready = sem("normed_ready")
        x_ready = sem("x_ready")
        heads_ready = sem("heads_ready")
        mix_ready = sem("mix_ready")
        z_act_ready = sem("z_act_ready")
        gate_in, gate_soft = sem("gate_in"), sem("gate_soft")
        expo_in, expo_out = sem("expo_in"), sem("expo_out")
        level_ready = sem("level_ready")
        gla_done = sem("gla_done")
        max_ready = sem("max_ready")
        probs_ready = sem("probs_ready")
        maps_ready = sem("maps_ready")
        probs_mixed = sem("probs_mixed")
        soft_in, soft_out = sem("soft_in"), sem("soft_out")
        cmp_blk, cmp_hid, cmp_probs = sem("cmp_blk"), sem("cmp_hid"), sem("cmp_probs")
        raw_full = sem("raw_full")
        cmp_in, cmp_out = sem("cmp_in"), sem("cmp_out")
        route_in, route_out = sem("route_in"), sem("route_out")
        g_full, g_free = sem("g_full"), sem("g_free")
        u_full, u_free = sem("u_full"), sem("u_free")
        d_full, d_free = sem("d_full"), sem("d_free")
        dve_step = sem("dve_step")
        pool_step = sem("pool_step")
        out_done = sem("out_done")

        A = Banks(bank[0:4], a_full, a_free)
        SC = Banks(bank[4:6], s_full, s_free)
        V = Banks(bank[6:8], v_full, v_free)

        whole = {}
        tenancy = []
        moe_at = {}

        zs = {0: Z[:, :].rearrange("p (t n) -> p t n", t=NT),
              1: Z[:, 0:NT * 1280].rearrange("p (t n) -> p t n", t=NT),
              2: Z[:, 0:LT * 3632].rearrange("p (t n) -> p t n", t=LT),
              3: Z[:, 0:LT * 4096].rearrange("p (t n) -> p t n", t=LT),
              4: Z[:, 0:LT * 3584].rearrange("p (t n) -> p t n", t=LT),
              5: Z[:, 0:LT * 4096].rearrange("p (t n) -> p t n", t=LT)}
        zo = {T: Z[:, 0:T * D].rearrange("p (t n) -> p t n", t=T) for T in (2, 4)}

        def ar(lo, n):
            return arena[:, lo:lo + n]

        mod_bank, mod_turn_bank = bank[4], bank[5]
        mod_rows_early = scratch[0:2, 0:512].rearrange("p (j n) -> p j n", j=4)
        mod_rows_late = mix[0:2, 0:NT, 768:896]

        qT = ar(0, 1024).rearrange("p (f t) -> p f t", f=2)
        kT = ar(1024, 1024).rearrange("p (f t) -> p f t", f=2)
        cum = ar(2048, 2056).rearrange("p (d f s t) -> p d f s t", d=2, f=2, s=2)
        X = [ar(4104 + 2048 * b, 2048) for b in range(2)]
        lrT = rows[:, 0:512]
        att_same = hT_flat[:, 0:2048].rearrange("p (s j h t) -> p s j h t", s=2, j=2, h=4)
        att_other = hT_flat[:, 2048:4096].rearrange("p (s j h t) -> p s j h t", s=2, j=2, h=4)
        kst = rows[:, 0:1024].rearrange("p (d f j k) -> p d f j k", d=2, f=2, j=2)
        state = rows[:, 1024:2048].rearrange("p (d f v) -> p d f v", d=2, f=2)
        silu_g = [ar(1024 * b, 1024).rearrange("p (f t) -> p f t", f=2) for b in range(2)]
        hid = [ar(2048 + 1024 * b, 1024).rearrange("p (f t) -> p f t", f=2) for b in range(2)]
        hid_high = [hT_r[:, 1024 * b:1024 * (b + 1)].rearrange("p (f t) -> p f t", f=2) for b in range(2)]
        hid_low = [hT_r[:, 1024 * b:1024 * (b + 1)].rearrange("p (f t) -> p f t", f=2) for b in (2, 3)]
        route = ar(4096, 512)
        route_buf = [ar(4608 + 16 * b, 16) for b in range(2)]
        kdup = Z[:, LT * 3632:LT * 3632 + 2048]
        cdup = mix[:, 2:4, :]
        pairs = [rows[:, 512 * b:512 * b + 512].rearrange("p (h m) -> p h m", h=4) for b in range(2)]
        vcmp = rows[:, 1024:2048].rearrange("p (h n) -> p h n", h=4)
        blk = [ar(4096 + 960 * b, 960).rearrange("p (l n) -> p l n", l=16) for b in range(2)]
        hidden = ar(6016, 512)
        hidT_k = ar(6528, 120).rearrange("p (k n) -> p k n", k=2)
        kcmpT = ar(6648, 60)
        cmp_s = ar(6710, 240)
        cmp_p = ar(6950, 512)
        cmpT = ar(7462, 512)
        hidT_v = x[:, 2, :].rearrange("p (k h g n) -> p k h g n", k=2, h=4, g=4)
        gelu_t = x[:, 3, 0:512]
        weighed = hT_spare[:, 1536:2048]

        aq = ar(0, 2048)
        ak = ar(2048, 2048)
        s_ring = [ar(4096 + 768 * b, 768) for b in range(2)] + [scratch[:, 0:768]]
        p_ring = [ar(5632 + 768 * b, 768) for b in range(3)]
        pT_ring = [hT_spare[:, 512 * b:512 * b + 512] for b in range(3)]
        nmax = stat[:, 0:128]
        sums = stat[:, 128:256]
        rsum = stat[:, 256:320]
        head_ss = stat[:, 320:400]
        head_rstd = stat[:, 400:480]
        ss = stat[:, 480:484]
        rstd = stat[:, 484:488]
        esink = stat[:, 488:520]
        comb = stat[:, 520:584].rearrange("p (e t) -> p e t", e=NE)
        lam = stat[:, 584:592]
        gates = stat[:, 592:688]
        coef = stat[:, 688:752]

        block = stack.enter_context(nc.Block())

        @block.scalar
        def _(act):
            seen = Seen(act)

            def drain(*copies, func=ACT.Copy):
                b = A.filled_bank(act)
                for dst, src, scale, bias in copies:
                    f = func if bias is None else ACT.Identity
                    i = nc.scalar.activation(dst, src(b), f, scale=scale, bias=0.0 if bias is None else bias)
                i.then_inc(a_free, 1)

            mod_copies = [0]

            def mod_copy(rows, n=1):
                for _ in range(min(n, MOD_STEPS - mod_copies[0])):
                    mod_copies[0] += 1
                    act.wait_ge(mod_full, mod_copies[0])
                    nc.scalar.activation(rows, mod_bank[0:2, :].rearrange("p (j n) -> p j n", j=4), ACT.Copy).then_inc(mod_copied, 1)

            def cond_silu():
                act.wait_ge(small_loaded, 16)
                nc.scalar.activation(cond[:, :, :], sm("cond", "p (k s) -> p k s", s=2), ACT.Silu).then_inc(cond_ready, 1)

            def chunk_high(n, full=None):
                slot = n % SLOTS
                act.wait_ge(slot_full[slot], 16 * (n // SLOTS + 1) if full is None else full)
                for h in range(2):
                    half = slice(h * HALF // 2, (h + 1) * HALF // 2)
                    nc.scalar.activation(ring_high[:, slot, half], ring[:, slot, half], ACT.Copy).then_inc(high_ready, 1)

            def chunks_high(first, n):
                for c in range(n):
                    chunk_high(first + c)

            def sum_squares(src, T, wait):
                for t in range(T):
                    wait(t)
                    nc.scalar.activation(scratch[:, :], src[:, t, :], ACT.Square, accum_out=ss[:, t:t + 1]).then_inc(sumsq_ready, 1)
                    seen.next(sumsq_ready)

            def features(T, scale_bias=None, split=None):
                per = 4 // T

                def high(j):
                    act.wait_ge(a_free, A.drains - (KT // per - 1 - j))
                    nc.scalar.activation(split_views(split, T)[0][:, j * per:(j + 1) * per, :],
                                         (hT4 if T == 4 else hT2)[:, j * per:(j + 1) * per, :], ACT.Copy).then_inc(act_high, 1)

                for j in range(KT // per):
                    copies = []
                    for n in range(per):
                        k = j * per + n
                        if scale_bias is None:
                            hT = hT4 if T == 4 else hT2
                            copies.append((hT[:, k, :], lambda b, n=n: b[:, n * T * P:(n + 1) * T * P], 1.0, None))
                            continue
                        for s in range(T // LT):
                            scale, bias = scale_bias(k, s)
                            hT = hT4 if T == 4 else hT2
                            lo = n * T * P + s * S
                            copies.append((hT[:, k, s * S:(s + 1) * S], lambda b, lo=lo: b[:, lo:lo + S], scale, bias))
                    drain(*copies)
                if split:
                    for j in range(KT // per):
                        high(j)

            def projected(dst, T, widths, split=None):
                col = 0
                last = 0 if split is None else split + 2 * len(widths)
                for n, w in enumerate(widths):
                    if split is not None and split + 2 * n + 3 < last:
                        chunk_high(split + 2 * n + 3)
                    for t in range(T):
                        drain((dst[:, t, col:col + w], lambda b, w=w: b[:, 0:w], 1.0, None))
                    if split is not None and split + 2 * n + 4 < last:
                        chunk_high(split + 2 * n + 4)
                    col += w

            def q_features(dst, n_ft, T, scale):
                per = 4 // T
                for j in range(n_ft // per):
                    drain((dst[:, j * per * T * P:(j + 1) * per * T * P], lambda b: b[:, :], scale, None))

            def gate_row_copies(T):
                for s in range(T // LT):
                    for h in range(2):
                        drain((gate_rows[:, s, h * 512:(h + 1) * 512], lambda b: b[:, :], 1.0, None))
                whole["gates", T] = A.drains

            def exp_probs(u, src, dst, n, wait=True):
                return nc.scalar.activation(dst, src, ACT.Exp, bias=nmax[:, n:n + 1], accum_out=sums[:, n:n + 1])

            def pT_out(u, width):
                drain((pT_ring[u % 3][:, 0:width], lambda b, w=width: b[:, 0:w], 1.0, None))

            def experts(i):
                T = NT if i == 0 else LT
                N = T * P
                base = NE * i

                def silu(e, parity, first):
                    for f in range(2):
                        act.wait_ge(g_full, e * 2 + f + 1)
                        if f == 0 and not first:
                            act.wait_ge(u_free, e * 2 - 2)
                        nc.scalar.activation(silu_g[parity][:, f, 0:N], bank[f][:, 0:N], ACT.Silu).then_inc(g_free, 1)

                first = STREAM[f"experts{i}"][0]
                chunk_high(first + 3)
                silu(base, 0, i == 0)
                chunk_high(first + 4)
                silu(base + 1, 1, i == 0)
                chunk_high(first + 5)
                chunk_high(first + 6)

                def pair(n, ahead, last=False):
                    ahead(7)
                    silu(n * 2 + base, 0, False)
                    ahead(8)
                    ahead(9)
                    ahead(10)
                    silu(n * 2 + (base + 1), 1, False)
                    if not last:
                        ahead(11)
                        ahead(12)

                per = 6 // SLOTS * 16
                with act.Fori(1, NE // 2 - 1) as n:
                    pair(n, lambda c: chunk_high(first + c, n * per + (16 * ((first + c) // SLOTS + 1) - per)))
                pair(NE // 2 - 1, lambda c: chunk_high(first + c + 6 * (NE // 2 - 2)), last=True)
                chunk_high(first + 3 * NE - 1)

            def route_exps(i):
                for _ in range(2):
                    seen.next(route_in)
                    src = route_buf[0] if _ == 0 else route_buf[1]
                    T = NT if i == 0 else LT
                    nc.scalar.activation(src[:, 0:4 * T], src[:, 0:4 * T], ACT.Exp).then_inc(route_out, 1)

            def modulate(i, which, T, split=None):
                features(T, lambda k, s: (modA[:, i, which, k, s:s + 1], modT[:, 48 * i + 24 * which + k, s:s + 1]), split)

            def wait_x(t):
                seen.next(x_ready)

            def first_layer(i):
                T = NT if i == 0 else LT
                sum_squares(x, NT, (lambda t: act.wait_ge(x_loaded, 32)) if i == 0 else wait_x)
                if i == 0:
                    mod_copy(mod_rows_early, MOD_EARLY)
                    seen.next(mod_ready)
                modulate(i, 0, NT)
                if i == 0:
                    projected(zs[0], NT, [512, 512, 512, 512, 256])
                    drain((zs[0][:, :, 2304:2336], lambda b: b[:, 0:NT * 32].rearrange("p (t n) -> p t n", t=NT), 1.0, None))
                else:
                    for t in range(NT):
                        drain((zs[1][:, t, 1024:1280], lambda b: b[:, 0:256], 1.0, None))
                    projected(zs[1], LT, [512, 512])
                whole["z", i] = A.drains
                if i == 0:
                    gla()
                    attention_heads(0)
                else:
                    attention_heads(1)
                features(T)
                gate_row_copies(T)
                projected(zo[T], T, [512, 512])
                whole["y", i] = A.drains
                chunks_high(STREAM[f"experts{i}"][0], SLOTS)
                sum_squares(x, T, wait_x)
                if i == 0:
                    seen.next(mod_ready)
                modulate(i, 1, T, "experts")
                route_exps(i)
                experts(i)
                gate_row_copies(T)
                whole["gates2", i] = A.drains

            def gla():
                for dst, scale in ((qT, QSCALE), (kT, 1.0)):
                    for f in range(2):
                        drain((dst[:, f, :], lambda b: b[:, :], scale, None))
                drain((lrT[0:32, :], lambda b: b[0:32, :], 1.0, None))
                mod_copy(mod_rows_late, MOD_HEADS)
                seen.next(gate_in)
                nc.scalar.activation(X[1], X[1], ACT.Exp).then_inc(gate_soft, 1)
                seen.next(gate_soft)
                nc.scalar.activation(X[1], X[1], ACT.Ln, bias=1.0).then_inc(gate_soft, 1)
                for n in range(len(LEVELS) + 1):
                    seen.next(expo_in)
                    nc.scalar.activation(X[n % 2], X[n % 2], ACT.Exp, scale=1.0 / GLA_GATE_NORM).then_inc(expo_out, 1)
                    if n >= 2:
                        mod_copy(mod_rows_late, MOD_LEVEL)
                for d in range(2):
                    drain((kst[:, d].rearrange("p f j k -> p (f j k)"), lambda b: b[:, :], 1.0, None))
                for d in range(2):
                    drain(*[(state[64 * o:64 * o + 64, d].rearrange("p f (o v) -> p f o v", o=2)[:, :, o, :],
                             lambda b, o=o: b[64 * o:64 * o + 64, :].rearrange("p (f o v) -> p f o v", f=2, o=2)[:, :, o, :], 1.0, None)
                            for o in range(2)])
                act.wait_ge(a_free, whole["z", 0])
                for t in range(NT):
                    i = nc.scalar.activation(zs[0][:, t, 1024:1536], zs[0][:, t, 1024:1536], ACT.Silu)
                i.then_inc(z_act_ready, 1)

            def attention_heads(i):
                if i == 0:
                    q_features(aq, 4, NT, QSCALE)
                    for v in range(2):
                        drain((ak[:, v * 512:(v + 1) * 512], lambda b: b[:, :], 1.0, None))
                    for s in range(2):
                        keys = 512 if s == 0 else 256
                        n_u = LT * 8
                        for u in range(n_u + 1):
                            if u < n_u:
                                seen.next(max_ready)
                                b = bank[4 + u % 2]
                                exp_probs(u, b[:, 0:keys], p_ring[u % 3][:, 0:keys], s * 16 + u).then_inc(probs_ready, 1)
                            if u >= 1:
                                pT_out(u - 1, keys)
                else:
                    q_features(aq, 8, LT, QSCALE)
                    for v in range(2):
                        drain((ak[:, v * 512:(v + 1) * 512], lambda b: b[:, :], 1.0, None))
                    n_u = LT * 16
                    for u in range(n_u + 1):
                        if u < n_u:
                            seen.next(max_ready)
                            exp_probs(u, s_ring[u % 3][:, 0:512], p_ring[u % 3][:, 0:512], u)
                            nc.scalar.activation(esink[:, u:u + 1], sm("sink")[:, u % 16:u % 16 + 1], ACT.Exp,
                                                 bias=nmax[:, u:u + 1]).then_inc(probs_ready, 1)
                        if u >= 1:
                            pT_out(u - 1, 512)

            def second_layer(i):
                sum_squares(x, LT, wait_x)
                chunks_high(STREAM[f"in{i}"][0], SLOTS)
                features(LT, lambda k, s: (sm("norm_pre", "p (l k) -> p l k", l=4)[:, i - 2, k:k + 1], None), "project")
                projected(zs[i], LT, [512] * IN_BLOCKS[i], STREAM[f"in{i}"][0])
                if i == 2:
                    drain((zs[2][:, :, 3584:3632], lambda b: b[:, 0:LT * 48].rearrange("p (t n) -> p t n", t=LT), 1.0, None))
                whole["z", i] = A.drains
                {2: sparse, 3: differential, 4: dilated_heads, 5: stick}[i]()
                lo, hi = {2: (2560, 3584), 3: (3072, 4096), 4: (2560, 3584), 5: (3072, 4096)}[i]
                for t in range(LT):
                    n = nc.scalar.activation(zs[i][:, t, lo:hi], zs[i][:, t, lo:hi], ACT.Silu)
                n.then_inc(z_act_ready, 1)
                chunks_high(STREAM[f"out{i}"][0], SLOTS)
                features(LT, split="project")
                projected(zo[2], LT, [512, 512], STREAM[f"out{i}"][0])
                act.wait_ge(a_free, A.drains)
                whole["y", i] = A.drains
                sum_squares(zo[2], LT, lambda t: None)

            def sparse():
                q_features(aq, 8, LT, QSCALE)
                q_features(ak, 8, LT, 1.0)
                for src in range(2):
                    for j in range(2):
                        dst = pairs[src]
                        drain(*[(dst[lo:lo + 64, 2 * j:2 * j + 2, :],
                                 lambda b, lo=lo, o=o: b[lo:lo + 64, :].rearrange("p (h m o) -> p h m o", h=2, o=2)[:, :, :, o],
                                 1.0, None) for o, lo in ((0, 0), (1, 64))])
                whole["pairs"] = A.drains
                act.wait_ge(a_free, whole["z", 2])
                nc.scalar.activation(gates.rearrange("p (t n) -> p t n", t=LT), zs[2][:, :, 3584:3632], ACT.Exp,
                                     scale=-1.0).then_inc(cmp_out, 1)
                seen.next(cmp_in)
                nc.scalar.activation(gelu_t[0:60, :], gelu_t[0:60, :], ACT.Exp, scale=-1.0).then_inc(cmp_out, 1)
                for src in range(2):
                    for kt in range(2):
                        b = A.filled_bank(act)
                        if src == 0:
                            n = nc.scalar.activation(hidT_k[:, kt, :], b[:, 0:60], ACT.Copy)
                        else:
                            for hk in range(4):
                                dst = hidT_v[:, kt, hk, :, 0:CMP_N]
                                n = nc.scalar.activation(dst, b[:, hk * CMP_N:(hk + 1) * CMP_N].unsqueeze(1).broadcast_to([P, 4, CMP_N]), ACT.Copy)
                        n.then_inc(a_free, 1)
                drain((kcmpT[:, :], lambda b: b[:, 0:60], 1.0, None))
                b = A.filled_bank(act)
                for hk in range(4):
                    for g in range(4):
                        n = nc.scalar.activation(vcmp[32 * g:32 * g + 32, hk, g * 64:(g + 1) * 64],
                                                 b[32 * g:32 * g + 32, hk * 64:(hk + 1) * 64], ACT.Copy)
                n.then_inc(a_free, 1)
                for qt in range(LT):
                    seen.next(cmp_in)
                    nc.scalar.activation(cmp_s[:, :], cmp_s[:, :], ACT.Exp).then_inc(cmp_out, 1)
                    drain((cmpT[:, :], lambda b: b[:, :], 1.0, None))
                n_u = LT * 16
                for u in range(n_u + 1):
                    if u < n_u:
                        seen.next(max_ready)
                        nk = P * (u // 16 + 1)
                        exp_probs(u, s_ring[u % 3][:, 0:nk], p_ring[u % 3][:, 0:nk], 2 * u)
                        exp_probs(u, s_ring[u % 3][:, nk:2 * nk], p_ring[u % 3][:, nk:2 * nk], 2 * u + 1).then_inc(probs_ready, 1)
                    if u >= 1:
                        pT_out(u - 1, 2 * P * ((u - 1) // 16 + 1))

            def differential():
                q_features(aq, 8, LT, QSCALE)
                q_features(ak, 8, LT, 1.0)
                seen.next(cmp_in)
                nc.scalar.activation(lam[:, 2:4], lam[:, 0:2], ACT.Exp).then_inc(cmp_out, 1)
                n_u = LT * 8
                for u in range(n_u + 1):
                    if u < n_u:
                        seen.next(max_ready)
                        nk = P * (u // 8 + 1)
                        exp_probs(u, s_ring[u % 3][:, 0:nk], p_ring[u % 3][:, 0:nk], 2 * u)
                        exp_probs(u, s_ring[u % 3][:, nk:2 * nk], p_ring[u % 3][:, nk:2 * nk], 2 * u + 1).then_inc(maps_ready, 1)
                    if u >= 1:
                        pT_out(u - 1, P * ((u - 1) // 8 + 1))

            def dilated_heads():
                q_features(aq, 6, LT, QSCALE)
                q_features(ak, 6, LT, 1.0)
                n_u = LT * 4
                for u in range(n_u + 1):
                    if u < n_u:
                        seen.next(max_ready)
                        nk = P * (u // 4 + 1)
                        exp_probs(u, s_ring[u % 3][:, 0:3 * nk], p_ring[u % 3][:, 0:3 * nk], u).then_inc(maps_ready, 1)
                    if u >= 1:
                        pT_out(u - 1, P * ((u - 1) // 4 + 1))

            def stick():
                q_features(aq, 8, LT, QSCALE)
                q_features(ak, 8, LT, 1.0)
                nc.scalar.preload_act_table_set("natural_log_exp_and_others")
                n_u = LT * 16
                for u in range(n_u + 2):
                    if u < n_u:
                        nk = P * (u // 16 + 1)
                        mag = s_ring[u % 3][:, 512:512 + nk]
                        seen.next(soft_in)
                        nc.scalar.activation(mag, mag, ACT.Exp).then_inc(soft_out, 1)
                        seen.next(soft_out)
                        nc.scalar.activation(mag, mag, ACT.Ln, bias=1.0).then_inc(soft_out, 1)
                        seen.next(soft_out)
                    if 1 <= u <= n_u:
                        nk = P * ((u - 1) // 16 + 1)
                        seen.next(max_ready)
                        nc.scalar.activation(p_ring[(u - 1) % 3][:, 512:512 + nk], p_ring[(u - 1) % 3][:, 256:256 + nk],
                                             ACT.Exp).then_inc(probs_ready, 1)
                    if u >= 2:
                        pT_out(u - 2, P * ((u - 2) // 16 + 1))

            cond_silu()
            for i in range(min(layers, 2)):
                first_layer(i)
            for i in range(2, layers):
                second_layer(i)

        @block.tensor
        def _(pe):
            seen = Seen(pe)
            def chunk():
                n = len(tenancy)
                pe.wait_ge(slot_full[n % SLOTS], 16 * (n // SLOTS + 1))
                tenancy.append([n % SLOTS, None, None])
                return ring[:, n % SLOTS, :]

            splits = [0]

            def split_chunk():
                n = len(tenancy)
                splits[0] += 1
                pe.wait_ge(low_ready, 2 * splits[0])
                tenancy.append([n % SLOTS, None, None])
                return [v[:, n % SLOTS, :].rearrange("p (k n) -> p k n", k=4) for v in (ring_high, ring_low)]

            def split_product(out, left, right, start, stop):
                nc.tensor.matmul(out, left[0], right[0], start=start, stop=False)
                nc.tensor.matmul(out, left[0], right[1], start=False, stop=False)
                return nc.tensor.matmul(out, left[1], right[0], start=False, stop=stop)

            half_count = [0]

            def chunk_done(ins):
                half_count[0] += 1
                ins.then_inc(chunk_used, 1)
                tenancy[-1][1:] = [chunk_used, half_count[0]]

            def chunk_done_with(pool):
                tenancy[-1][1:] = [pool.full, pool.fills]

            mod_steps = [0]

            def mod_turn(rows):
                n = mod_steps[0] - 1
                pe.wait_ge(mod_copied, n + 1)
                for j in range(4):
                    m = n * 4 + j
                    i = nc.tensor.matmul(mod_turn_bank[:, 2 * m:2 * m + 2], rows[:, j, :], ident[0:2, 0:2], start=True, stop=True)
                return i

            def mod_step(rows):
                for kh in range(2):
                    w = chunk().rearrange("p (k n) -> p k n", k=4)
                    if kh == 0 and mod_steps[0] not in (0, MOD_EARLY):
                        mod_turn(rows)
                    for k in range(4):
                        i = nc.tensor.matmul(mod_bank[0:2, :], cond[:, 4 * kh + k, :], w[:, k, :],
                                             start=(kh == 0 and k == 0), stop=(kh == 1 and k == 3))
                    if kh == 0:
                        chunk_done(i)
                mod_steps[0] += 1
                i.then_inc(mod_full, 1)
                tenancy[-1][1:] = [mod_full, mod_steps[0]]

            def mod_early():
                for _ in range(MOD_EARLY):
                    mod_step(mod_rows_early)
                mod_turn(mod_rows_early).then_inc(mod_turned, 1)

            def mod_late(n):
                for _ in range(min(n, MOD_STEPS - mod_steps[0])):
                    mod_step(mod_rows_late)

            def transposes(src, T):
                per = 4 // T
                for j in range(KT // per):
                    b = A.take(pe)
                    for n in range(per):
                        for t in range(T):
                            i = nc.tensor.transpose(b[:, (n * T + t) * P:(n * T + t + 1) * P],
                                                    src[:, t, (j * per + n) * P:(j * per + n + 1) * P], ident)
                    i.then_inc(a_full, 1)

            def project(T, n_chunks, quarter=False, wide=None):
                hT = hT4 if wide or T == 4 else hT2
                for n in range(n_chunks):
                    banks = []
                    for kh in range(1 if quarter else 2):
                        kn = 8 if quarter else 4
                        w = chunk().rearrange("p (k n) -> p k n", k=kn)
                        N = HALF // kn
                        last = quarter or kh == 1
                        for t in range(T):
                            if kh == 0:
                                banks.append(A.take(pe))
                            for k in range(kn):
                                i = nc.tensor.matmul(banks[t][:, 0:N], hT[:, kn * kh + k, t * P:(t + 1) * P], w[:, k, :],
                                                     start=(kh == 0 and k == 0), stop=(last and k == kn - 1))
                            if last:
                                i.then_inc(a_full, 1)
                        if last:
                            chunk_done_with(A)
                        else:
                            chunk_done(i)

            def project_split(n_blocks):
                seen.next(act_low, KT // 2)
                hT = split_views("project", LT)
                for n in range(n_blocks):
                    banks = [A.take(pe) for _ in range(LT)]
                    for kh in range(2):
                        w = split_chunk()
                        for t in range(LT):
                            for k in range(4):
                                i = split_product(banks[t][:, :], [v[:, 4 * kh + k, t * P:(t + 1) * P] for v in hT],
                                                  [v[:, k, :] for v in w], kh == 0 and k == 0, kh == 1 and k == 3)
                            if kh == 1:
                                i.then_inc(a_full, 1)
                        if kh == 1:
                            chunk_done_with(A)
                        else:
                            chunk_done(i)

            def project_small(T, w, N):
                hT = hT4 if T == 4 else hT2
                b = A.take(pe)
                for t in range(T):
                    for k in range(KT):
                        i = nc.tensor.matmul(b[:, t * N:(t + 1) * N], hT[:, k, t * P:(t + 1) * P], w[:, k, :],
                                             start=(k == 0), stop=(k == KT - 1))
                i.then_inc(a_full, 1)

            def gate_row_products(i, T, which):
                for s in range(T // LT):
                    for h in range(2):
                        b = A.take(pe)
                        for j in range(4):
                            m = nc.tensor.matmul(b[:, j * P:(j + 1) * P],
                                                 modT[:, 48 * i + which * 8 + h * 4 + j, s:s + 1].broadcast_to([P, P]), ident,
                                                 start=True, stop=True)
                        m.then_inc(a_full, 1)

            def head_features(src, n_ft, T):
                per = 4 // T
                for j in range(n_ft // per):
                    b = A.take(pe)
                    for n in range(per):
                        for t in range(T):
                            i = nc.tensor.transpose(b[:, (n * T + t) * P:(n * T + t + 1) * P], src(t, j * per + n), ident)
                    i.then_inc(a_full, 1)

            def attend(n_u, score, turn, weigh, lag_events):
                pT_at = {}
                for step in range(n_u + 2):
                    if step < n_u:
                        score(step)
                    if 1 <= step <= n_u:
                        u = step - 1
                        seen.next(lag_events)
                        b = A.take(pe)
                        turn(u, b).then_inc(a_full, 1)
                        pT_at[u] = A.fills
                    if step >= 2:
                        A.drained(pe, pT_at[step - 2])
                        weigh(step - 2)

            def turn_blocks(src, n, b):
                for j in range(n):
                    i = nc.tensor.transpose(b[:, j * P:(j + 1) * P], src[:, j * P:(j + 1) * P], ident)
                return i

            def gla():
                z = zs[0]
                for col in (0, 256):
                    head_features(lambda t, f: z[:, t, col + f * P:col + (f + 1) * P], 2, NT)
                b = A.take(pe)
                for t in range(NT):
                    i = nc.tensor.transpose(b[0:32, t * P:(t + 1) * P], z[:, t, 2304:2336], ident)
                i.then_inc(a_full, 1)
                A.drained(pe)
                seen.next(mod_ready)
                gw = sm("gate_w", "p (d n) -> p d n", d=2)
                for d in range(2):
                    if d == 1:
                        mod_late(MOD_HEADS)
                    for f in range(2):
                        b = V.take(pe)
                        nc.tensor.matmul(b[:, :], gw[0:32, d, f * P:(f + 1) * P], lrT[0:32, :], start=True,
                                         stop=True).then_inc(v_full, 1)

                def pair_products(blocks):
                    banks = [V.take(pe) for _ in range(2)]
                    for n, (left, right, keys, queries) in enumerate(blocks):
                        for f in range(2):
                            for odd in range(2):
                                r = slice(64 * odd, 64 * odd + 64)
                                o = (n * 2 + f) * P
                                i = nc.tensor.matmul(banks[odd][:, o:o + P], left(f)[r, keys], right(f)[r, queries],
                                                     start=True, stop=True)
                                if n == 1 and f == 1:
                                    i.then_inc(v_full, 1)

                for s in range(2):
                    at = [slice(s * S + j * P, s * S + (j + 1) * P) for j in range(2)]
                    pair_products([(lambda f: kT[:, f, :], lambda f: qT[:, f, :], sl, sl) for sl in at])
                tile = [slice(0, P), slice(P, S)]
                for n, m in enumerate(LEVELS):
                    seen.next(level_ready)
                    xl = X[n % 2].rearrange("p (d f s t) -> p d f s t", d=2, f=2, s=2)

                    def src(d, s):
                        return lambda f: xl[:, d, f, s, :]

                    if m == P:
                        for s in range(2):
                            pair_products([(src(d, s), src(d, s), tile[d], tile[1 - d]) for d in range(2)])
                        continue
                    for d in range(2):
                        for s in range(2):
                            pair_products([(src(d, s), src(d, s), tile[j], tile[j]) for j in range(2)])
                            if (d, s) != (0, 0):
                                mod_late(1)
                mod_turn(mod_rows_late).then_inc(mod_turned, 1)
                seen.next(level_ready)
                xi = X[len(LEVELS) % 2].rearrange("p (w f t) -> p w f t", w=4, f=2)
                for d in range(2):
                    b = A.take(pe)
                    for f in range(2):
                        for j in range(2):
                            o = (f * 2 + j) * P
                            i = nc.tensor.transpose(b[:, o:o + P], xi[:, d, f, j * P:(j + 1) * P], ident)
                    i.then_inc(a_full, 1)
                A.drained(pe)
                for d in range(2):
                    b = A.take(pe)
                    for f in range(2):
                        for j in range(2):
                            i = nc.tensor.matmul(b[:, f * 256:(f + 1) * 256], kst[:, d, f, j, :],
                                                 z[:, 2 + j, 512 + f * 256:512 + (f + 1) * 256], start=(j == 0), stop=(j == 1))
                    i.then_inc(a_full, 1)
                A.drained(pe)
                V.drained(pe)
                for s in range(2):
                    for j in range(2):
                        b = V.take(pe)
                        if s == LAT:
                            for f in range(2):
                                for d in range(2):
                                    nc.tensor.matmul(b[:, f * 256:(f + 1) * 256], xi[:, 2 + d, f, j * P:(j + 1) * P], state[:, d, f, :],
                                                     start=(f == 0 and d == 0), stop=False, skip_group_check=True)
                        for h in range(GLA_H):
                            for js in range(2):
                                a = att_same if js == j else att_other
                                i = nc.tensor.matmul(b[:, h * P:(h + 1) * P], a[:, s, js, h, :],
                                                     z[:, 2 * s + js, 512 + h * P:512 + (h + 1) * P],
                                                     start=(s == CTX and h == 0 and js == 0), stop=(js == 1), skip_group_check=True)
                        i.then_inc(v_full, 1)

            def rows_of(h):
                return slice(64 * (h % 2), 64 * (h % 2) + 64)

            def first_attention(i):
                if i == 0:
                    z = zs[0]
                    seen.next(heads_ready)
                    head_features(lambda t, f: z[:, t, 1536 + f * P:1536 + (f + 1) * P], 4, NT)
                    head_features(lambda t, f: mix[:, t, 512 + f * P:512 + (f + 1) * P], 2, NT)
                    A.drained(pe)
                    q4 = aq.rearrange("p (f t) -> p f t", f=4)
                    k4 = ak[:, 0:1024].rearrange("p (v t) -> p v t", v=2)
                    for s in range(2):
                        keys = 512 if s == 0 else 256
                        k0 = 0 if s == 0 else S

                        def score(u):
                            h, qt = u % 8, u // 8
                            b = bank[4 + u % 2]
                            nc.tensor.matmul(b[:, 0:keys], q4[rows_of(h), h // 2, s * S + qt * P:s * S + (qt + 1) * P],
                                             k4[rows_of(h), h // 4, k0:512], start=True, stop=True).then_inc(raw_full, 1)

                        def weigh(u):
                            h = u % 8
                            if h == 0:
                                out_bank[0] = V.take(pe)
                            for j in range(keys // P):
                                t = k0 // P + j
                                m = nc.tensor.matmul(out_bank[0][:, h * HD:(h + 1) * HD], pT_ring[u % 3][:, j * P:(j + 1) * P],
                                                     z[:, t, 2176 + (h // 4) * HD:2176 + (h // 4 + 1) * HD],
                                                     start=(j == 0), stop=(j == keys // P - 1))
                            if h == 7:
                                m.then_inc(v_full, 1)

                        attend(LT * 8, score, lambda u, b: turn_blocks(p_ring[u % 3], keys // P, b), weigh, probs_ready)
                else:
                    z = zs[1]
                    seen.next(heads_ready)
                    head_features(lambda t, f: z[:, t, f * P:(f + 1) * P], 8, LT)
                    head_features(lambda t, f: mix[:, t, f * P:(f + 1) * P], 2, NT)
                    A.drained(pe)
                    q8 = aq.rearrange("p (f t) -> p f t", f=8)
                    k4 = ak[:, 0:1024].rearrange("p (v t) -> p v t", v=2)

                    def score(u):
                        h, qt = u % 16, u // 16
                        b = SC.take(pe)
                        nc.tensor.matmul(b[:, :], q8[rows_of(h), h // 2, qt * P:(qt + 1) * P], k4[rows_of(h), h // 8, :],
                                         start=True, stop=True).then_inc(s_full, 1)

                    def weigh(u):
                        h = u % 16
                        if h % 8 == 0:
                            out_bank[0] = V.take(pe)
                        for t in range(NT):
                            m = nc.tensor.matmul(out_bank[0][:, (h % 8) * HD:(h % 8 + 1) * HD], pT_ring[u % 3][:, t * P:(t + 1) * P],
                                                 z[:, t, 1152 + (h // 8) * HD:1152 + (h // 8 + 1) * HD],
                                                 start=(t == 0), stop=(t == NT - 1))
                        if h % 8 == 7:
                            m.then_inc(v_full, 1)

                    attend(LT * 16, score, lambda u, b: turn_blocks(p_ring[u % 3], 4, b), weigh, probs_ready)

            out_bank = [None]

            def router(i, T):
                hT = hT4 if T == 4 else hT2
                w = sm("router_w", "p (l k n) -> p l k n", l=2, k=KT)[:, i]
                b = V.take(pe)
                for t in range(T):
                    for k in range(KT):
                        m = nc.tensor.matmul(b[:, t * 20:(t + 1) * 20], hT[:, k, t * P:(t + 1) * P], w[:, k, :],
                                             start=(k == 0), stop=(k == KT - 1))
                m.then_inc(v_full, 1)

            def experts(i):
                T = NT if i == 0 else LT
                N = T * P
                hT = hT4 if T == 4 else hT2
                base = NE * i
                d_base = 0 if i == 0 else NE * NT * 2
                A.drained(pe)
                SC.drained(pe)
                V.drained(pe)
                half0 = half_count[0]
                first, low0 = len(tenancy), 2 * splits[0]
                moe_at[i] = (first, half0, d_base)
                xT = split_views("experts", T)
                seen.next(act_low, KT * T // 4)

                def slot(c):
                    return (first + c) % SLOTS

                def parts(c, low, k):
                    pe.wait_ge(low_ready, low)
                    return [v[:, slot(c), :].rearrange("p (k n) -> p k n", k=k) for v in (ring_high, ring_low)]

                def gate_up(e, c, low, start):
                    for kh in range(2):
                        w = parts(c + kh, low(c + kh), 4)
                        for f in range(4):
                            if kh == 0 and not start:
                                pe.wait_ge(g_free if f < 2 else u_free, e * 2 + (f % 2 - 1))
                            for k in range(4):
                                m = split_product(bank[f][:, 0:N], [v[:, k, f * P:(f + 1) * P] for v in w],
                                                  [v[:, 4 * kh + k, :] for v in xT], kh == 0 and k == 0, kh == 1 and k == 3)
                            if kh == 1:
                                m.then_inc(g_full if f < 2 else u_full, 1)
                        if kh == 0:
                            m.then_inc(chunk_used, 1)

                def down(e, n, parity, c, low, start):
                    w = parts(c, low(c), 2)
                    pe.wait_ge(hid_ready, e * 2 + 2)
                    hidden_rows = (hid_high[parity], hid_low[parity])
                    for t in range(T):
                        for h in range(2):
                            b = t * 2 + h
                            if not (start and b < 4):
                                pe.wait_ge(d_free, n + (b - 3))
                            for f in range(2):
                                m = split_product(bank[4 + b % 4][:, :], [v[:, f, t * P:(t + 1) * P] for v in hidden_rows],
                                                  [v[:, f, h * 512:(h + 1) * 512] for v in w], f == 0, f == 1)
                            m.then_inc(d_full, 1)

                def low(c):
                    return low0 + 2 * (c + 1)

                per = 2 * T
                gate_up(base, 0, low, i == 0)
                gate_up(base + 1, 2, low, False)
                down(base, d_base, 0, 4, low, True)
                with pe.Fori(1, NE // 2) as j:
                    def low_j(c):
                        return j * 12 + (low(c) - 12)

                    gate_up(j * 2 + base, 5, low_j, False)
                    down(j * 2 + (base - 1), j * (2 * per) + (d_base - per), 1, 7, low_j, False)
                    gate_up(j * 2 + (base + 1), 8, low_j, False)
                    down(j * 2 + base, j * (2 * per) + d_base, 0, 10, low_j, False)
                down(base + NE - 1, d_base + (NE - 1) * per, 1, 3 * NE - 1, low, False)
                splits[0] += 3 * NE
                half_count[0] += NE
                for q in range(3 * NE):
                    tenancy.append([slot(q), d_full, d_base + NE * per])
                pe.wait_ge(g_free, 2 * (base + NE))
                pe.wait_ge(u_free, 2 * (base + NE))
                pe.wait_ge(d_free, d_base + NE * per)

            def first_layer(i):
                T = NT if i == 0 else LT
                if i == 0:
                    mod_early()
                seen.next(normed_ready, NT)
                transposes(mix, NT)
                A.drained(pe)
                if i == 0:
                    project(NT, 4)
                    project(NT, 1, quarter=True)
                    project_small(NT, sm("lr_w", "p (k n) -> p k n", k=KT), 32)
                    A.drained(pe)
                    gla()
                else:
                    project(NT, 1, quarter=True)
                    project(LT, 2, wide=True)
                    A.drained(pe)
                first_attention(i)
                V.drained(pe)
                transposes(mix, T)
                if i == 0:
                    seen.next(mod_ready)
                gate_row_products(i, T, 2)
                A.drained(pe)
                project(T, 2)
                seen.next(normed_ready, T)
                transposes(mix, T)
                A.drained(pe)
                router(i, T)
                experts(i)
                gate_row_products(i, T, 5)

            def second_layer(i):
                seen.next(normed_ready, LT)
                transposes(mix, LT)
                A.drained(pe)
                project_split(IN_BLOCKS[i])
                if i == 2:
                    project_small(LT, sm("gl_w", "p (k n) -> p k n", k=KT), 48)
                A.drained(pe)
                {2: sparse, 3: differential, 4: dilated_heads, 5: stick}[i]()
                seen.next(mix_ready, LT)
                transposes(mix, LT)
                A.drained(pe)
                project_split(2)

            def sparse():
                z = zs[2]
                head_features(lambda t, f: z[:, t, f * P:(f + 1) * P], 8, LT)
                seen.next(heads_ready)
                kd = kdup.rearrange("p (t f n) -> p t f n", t=LT, f=8)
                head_features(lambda t, f: kd[:, t, f, :], 8, LT)
                cd = cdup
                head_features(lambda t, f: cd[:, t, f * P:(f + 1) * P], 8, LT)
                for src in range(2):
                    b = V.take(pe)
                    seen.next(cmp_blk)
                    for c in range(2):
                        w = chunk().rearrange("p (l n) -> p l n", l=8)
                        for l in range(8):
                            i = nc.tensor.matmul(b[0:60, 0:256], blk[src][:, c * 8 + l, :], w[:, l, :],
                                                 start=(c == 0 and l == 0), stop=(c == 1 and l == 7))
                        if c == 0:
                            chunk_done(i)
                    i.then_inc(v_full, 1)
                    chunk_done_with(V)
                seen.next(cmp_hid)
                for src in range(2):
                    for kt in range(2):
                        b = A.take(pe)
                        nc.tensor.transpose(b[:, 0:60], hidden[0:60, src * 256 + kt * P:src * 256 + (kt + 1) * P],
                                            ident[0:60, 0:60]).then_inc(a_full, 1)
                A.drained(pe)
                w2k = sm("w2_k", "p (k n) -> p k n", k=2)
                w2v = sm("w2_v", "p (k n) -> p k n", k=2)
                b = A.take(pe)
                for kt in range(2):
                    i = nc.tensor.matmul(b[:, 0:60], w2k[:, kt, :], hidT_k[:, kt, :], start=(kt == 0), stop=(kt == 1))
                i.then_inc(a_full, 1)
                b = A.take(pe)
                for hk in range(4):
                    for kt in range(2):
                        i = nc.tensor.matmul(b[:, hk * 64:(hk + 1) * 64], hidT_v[:, kt, hk].rearrange("p g n -> p (g n)"),
                                             w2v[:, kt, :], start=(kt == 0), stop=(kt == 1))
                i.then_inc(a_full, 1)
                A.drained(pe)
                q8 = aq.rearrange("p (f t) -> p f t", f=8)
                for qt in range(LT):
                    banks = [SC.take(pe) for _ in range(2)]
                    for h in range(16):
                        i = nc.tensor.matmul(banks[h % 2][:, (h // 2) * CMP_N:(h // 2 + 1) * CMP_N], q8[rows_of(h), h // 2, qt * P:(qt + 1) * P],
                                             kcmpT[rows_of(h), (h // 4) * CMP_N:(h // 4 + 1) * CMP_N], start=True, stop=True)
                        if h >= 14:
                            i.then_inc(s_full, 1)
                    seen.next(cmp_probs)
                    b = A.take(pe)
                    for hk in range(4):
                        i = nc.tensor.transpose(b[:, hk * P:(hk + 1) * P], cmp_p[:, hk * P:(hk + 1) * P], ident)
                    i.then_inc(a_full, 1)
                    A.drained(pe)
                    for half in range(2):
                        b = V.take(pe)
                        for hk in range(2):
                            i = nc.tensor.matmul(b[:, hk * 256:(hk + 1) * 256],
                                                 cmpT[:, (2 * half + hk) * P:(2 * half + hk + 1) * P], vcmp[:, 2 * half + hk, :],
                                                 start=True, stop=True)
                        i.then_inc(v_full, 1)
                k8 = ak.rearrange("p (b v t) -> p b v t", b=2, v=4)

                def score(u):
                    h, qt = u % 16, u // 16
                    nk = P * (qt + 1)
                    b = SC.take(pe)
                    for br in range(2):
                        i = nc.tensor.matmul(b[:, br * nk:(br + 1) * nk], q8[rows_of(h), h // 2, qt * P:(qt + 1) * P],
                                             k8[rows_of(h), br, h // 4, 0:nk], start=True, stop=True)
                    i.then_inc(s_full, 1)

                def weigh(u):
                    h, qt = u % 16, u // 16
                    if h % 4 == 0:
                        out_bank[0] = V.take(pe)
                    for br in range(2):
                        for j in range(qt + 1):
                            col = 1792 + 512 * br + (h // 4) * HD
                            o = (h % 4) * P + br * HD
                            m = nc.tensor.matmul(out_bank[0][:, o:o + HD], pT_ring[u % 3][:, (br * (qt + 1) + j) * P:(br * (qt + 1) + j + 1) * P],
                                                 z[:, j, col:col + HD], start=(j == 0), stop=(j == qt))
                    if h % 4 == 3:
                        m.then_inc(v_full, 1)

                attend(LT * 16, score, lambda u, b: turn_blocks(p_ring[u % 3], 2 * (u // 16 + 1), b), weigh, probs_ready)

            def differential():
                z = zs[3]
                head_features(lambda t, f: z[:, t, f * P:(f + 1) * P], 8, LT)
                head_features(lambda t, f: z[:, t, 1024 + f * P:1024 + (f + 1) * P], 8, LT)
                A.drained(pe)
                q8 = aq.rearrange("p (f t) -> p f t", f=8)
                k8 = ak.rearrange("p (f t) -> p f t", f=8)

                def score(u):
                    h, qt = u % 8, u // 8
                    nk = P * (qt + 1)
                    for m in range(2):
                        b = SC.take(pe)
                        nc.tensor.matmul(b[:, 0:nk], q8[rows_of(m), h, qt * P:(qt + 1) * P],
                                         k8[rows_of(m), h, 0:nk], start=True, stop=True).then_inc(s_full, 1)

                def weigh(u):
                    h, qt = u % 8, u // 8
                    if h % 4 == 0:
                        out_bank[0] = V.take(pe)
                    for j in range(qt + 1):
                        m = nc.tensor.matmul(out_bank[0][:, (h % 4) * P:(h % 4 + 1) * P], pT_ring[u % 3][:, j * P:(j + 1) * P],
                                             z[:, j, 2048 + h * P:2048 + (h + 1) * P], start=(j == 0), stop=(j == qt))
                    if h % 4 == 3:
                        m.then_inc(v_full, 1)

                attend(LT * 8, score, lambda u, b: turn_blocks(p_ring[u % 3], u // 8 + 1, b), weigh, probs_mixed)

            def dilated_heads():
                z = zs[4]
                head_features(lambda t, f: z[:, t, f * P:(f + 1) * P], 6, LT)
                head_features(lambda t, f: z[:, t, 768 + f * P:768 + (f + 1) * P], 6, LT)
                A.drained(pe)
                q6 = aq[:, 0:1536].rearrange("p (f t) -> p f t", f=6)
                k6 = ak[:, 0:1536].rearrange("p (f t) -> p f t", f=6)

                def score(u):
                    h, qt = u % 4, u // 4
                    nk = P * (qt + 1)
                    for part in ((0, 1), (2,)):
                        b = SC.take(pe)
                        for n, g in enumerate(part):
                            hh = g * 4 + h
                            i = nc.tensor.matmul(b[:, n * nk:(n + 1) * nk], q6[rows_of(hh), hh // 2, qt * P:(qt + 1) * P],
                                                 k6[rows_of(hh), hh // 2, 0:nk], start=True, stop=True)
                        i.then_inc(s_full, 1)

                def weigh(u):
                    h, qt = u % 4, u // 4
                    if h % 2 == 0:
                        out_bank[0] = V.take(pe)
                    for j in range(qt + 1):
                        m = nc.tensor.matmul(out_bank[0][:, (h % 2) * 256:(h % 2 + 1) * 256], pT_ring[u % 3][:, j * P:(j + 1) * P],
                                             z[:, j, 1536 + h * 256:1536 + (h + 1) * 256], start=(j == 0), stop=(j == qt))
                    if h % 2 == 1:
                        m.then_inc(v_full, 1)

                attend(LT * 4, score, lambda u, b: turn_blocks(p_ring[u % 3], u // 4 + 1, b), weigh, probs_mixed)

            def stick():
                z = zs[5]
                head_features(lambda t, f: z[:, t, f * P:(f + 1) * P], 8, LT)
                head_features(lambda t, f: z[:, t, 1024 + f * P:1024 + (f + 1) * P], 8, LT)
                A.drained(pe)
                q8 = aq.rearrange("p (f t) -> p f t", f=8)
                k8 = ak.rearrange("p (f t) -> p f t", f=8)

                def score(u):
                    h, qt = u % 16, u // 16
                    nk = P * (qt + 1)
                    b = SC.take(pe)
                    nc.tensor.matmul(b[:, 0:nk], q8[rows_of(h), h // 2, qt * P:(qt + 1) * P], k8[rows_of(h), h // 2, 0:nk],
                                     start=True, stop=True).then_inc(s_full, 1)

                def weigh(u):
                    h, qt = u % 16, u // 16
                    if h % 8 == 0:
                        out_bank[0] = V.take(pe)
                    for j in range(qt + 1):
                        m = nc.tensor.matmul(out_bank[0][:, (h % 8) * HD:(h % 8 + 1) * HD], pT_ring[u % 3][:, j * P:(j + 1) * P],
                                             z[:, j, 2048 + h * HD:2048 + (h + 1) * HD], start=(j == 0), stop=(j == qt))
                    if h % 8 == 7:
                        m.then_inc(v_full, 1)

                attend(LT * 16, score, lambda u, b: turn_blocks(p_ring[u % 3][:, 512:], u // 16 + 1, b), weigh, probs_ready)

            pe.wait_ge(const_loaded, 16)
            pe.wait_ge(small_loaded, 16)
            seen.next(cond_ready)
            for i in range(min(layers, 2)):
                first_layer(i)
            for i in range(2, layers):
                second_layer(i)

        @block.vector
        def _(dve):
            seen = Seen(dve)
            own = {}
            ve = nc.vector

            def signal(ins, semaphore):
                ins.then_inc(semaphore, 1)
                own[semaphore.name] = own.get(semaphore.name, 0) + 1
                return own[semaphore.name]

            def then(ins, semaphore=dve_step):
                dve.wait_ge(semaphore, signal(ins, semaphore))

            def vbank():
                return V.filled_bank(dve)

            def over(v, n):
                return v.unsqueeze(2).broadcast_to([P, v.shape[1], n])

            def under(v, n):
                return v.unsqueeze(1).broadcast_to([P, n, v.shape[1]])

            def inv_root(dst_n, sums_of_squares, width):
                signal(ve.tensor_scalar(sums_of_squares, sums_of_squares, 1.0 / width, EPS, ALU.mult, ALU.add), meansq_ready)
                seen.next(rstd_ready)

            splits = [0]

            def chunk_low(n, ready=None):
                slot = n % SLOTS
                if ready is None:
                    splits[0] += 1
                    ready = 2 * splits[0]
                for h in range(2):
                    half = slice(h * HALF // 2, (h + 1) * HALF // 2)
                    dve.wait_ge(high_ready, ready + (h - 1))
                    ve.tensor_tensor(ring_low[:, slot, half], ring[:, slot, half], ring_high[:, slot, half],
                                     ALU.subtract).then_inc(low_ready, 1)

            def chunks_low(first, n):
                for c in range(n):
                    chunk_low(first + c)

            def features_low(name, T):
                per = 4 // T
                high, low = split_views(name, T)
                for j in range(KT // per):
                    ks = slice(j * per, (j + 1) * per)
                    seen.next(act_high)
                    signal(ve.tensor_tensor(low[:, ks, :], (hT4 if T == 4 else hT2)[:, ks, :], high[:, ks, :], ALU.subtract), act_low)

            def norm_rows(T):
                seen.next(sumsq_ready, T)
                inv_root(T, ss[:, 0:T], D)
                for t in range(T):
                    signal(ve.tensor_scalar(mix[:, t, :], x[:, t, :], rstd[:, t:t + 1], None, ALU.mult), normed_ready)

            def modulation(lo, hi, scaled):
                seen.next(mod_turned)
                then(ve.tensor_tensor(modT[:, lo:hi, :], mod_turn_bank[:, 2 * lo:2 * hi].rearrange("p (m s) -> p m s", s=2),
                                      over(sm("mod_b")[:, lo:hi], 2), ALU.add))
                for i, which in scaled:
                    col = 48 * i + (8, 32)[which]
                    gain = sm(("norm_mix", "norm_ffn")[which])[:, i * KT:(i + 1) * KT]
                    n = ve.scalar_tensor_tensor(modA[:, i, which], modT[:, col:col + 8, :], 1.0, over(gain, 2), ALU.add, ALU.mult)
                signal(n, mod_ready)

            def head_squares(src, H, d, at):
                then(ve.tensor_tensor(scratch2[:, 0:H * d], src, src, ALU.mult))
                then(ve.tensor_reduce(head_ss[:, at:at + H], scratch2[:, 0:H * d].rearrange("p (h d) -> p h d", h=H), AX.X, ALU.add))

            def scale_heads(src, H, d, at):
                v = src.rearrange("p (h d) -> p h d", h=H)
                then(ve.tensor_tensor(v, v, over(head_rstd[:, at:at + H], d), ALU.mult))

            def gain_heads(src, H, gain):
                v = src.rearrange("p (h d) -> p h d", h=H)
                then(ve.tensor_tensor(v, v, under(gain, H), ALU.mult))

            def rotate(src, H, t):
                v = src.rearrange("p (h a b f) -> p h a b f", h=H, a=2, b=2)
                c, s = (rope[:, t, n].unsqueeze(1).broadcast_to([P, H, 2, 16]) for n in range(2))
                x1, x2 = v[:, :, :, 0, :], v[:, :, :, 1, :]
                tmp = [turned[:, H * 32 * n:H * 32 * (n + 1)].rearrange("p (h a f) -> p h a f", h=H, a=2) for n in range(4)]
                for n, (half, by) in enumerate(((x1, c), (x2, s), (x2, c), (x1, s))):
                    m = ve.tensor_tensor(tmp[n], half, by, ALU.mult)
                then(m)
                ve.tensor_tensor(x1, tmp[0], tmp[1], ALU.subtract)
                then(ve.tensor_tensor(x2, tmp[2], tmp[3], ALU.add))

            def twice(dst, src, H):
                return ve.tensor_copy(dst.rearrange("p (h two d) -> p h two d", h=H, two=2),
                                      src.rearrange("p (h d) -> p h d", h=H).unsqueeze(2).broadcast_to([P, H, 2, HD]))

            def heads_first():
                dve.wait_ge(a_free, whole["z", 0])
                z = zs[0]
                for t in range(NT):
                    head_squares(z[:, t, 1536:2176], 10, HD, 10 * t)
                inv_root(40, head_ss[:, 0:40], HD)
                for t in range(NT):
                    scale_heads(z[:, t, 1536:2176], 10, HD, 10 * t)
                    gain_heads(z[:, t, 1536:2048], 8, sm("att_q"))
                    gain_heads(z[:, t, 2048:2176], 2, sm("att_k"))
                    if t < LT:
                        rotate(z[:, t, 1536:2176], 10, t)
                    n = twice(mix[:, t, 512:768], z[:, t, 2048:2176], 2)
                signal(n, heads_ready)

            def heads_second():
                dve.wait_ge(a_free, whole["z", 1])
                z = zs[1]
                for t in range(NT):
                    if t < LT:
                        head_squares(z[:, t, 0:1024], 16, HD, 18 * t)
                    head_squares(z[:, t, 1024:1152], 2, HD, 18 * t + 16 if t < LT else 36 + 2 * (t - LT))
                inv_root(40, head_ss[:, 0:40], HD)
                for t in range(NT):
                    if t < LT:
                        scale_heads(z[:, t, 0:1152], 18, HD, 18 * t)
                        gain_heads(z[:, t, 0:1024], 16, sm("swa_q"))
                    else:
                        scale_heads(z[:, t, 1024:1152], 2, HD, 36 + 2 * (t - LT))
                    gain_heads(z[:, t, 1024:1152], 2, sm("swa_k"))
                    if t < LT:
                        rotate(z[:, t, 0:1152], 18, t)
                    n = twice(mix[:, t, 0:256], z[:, t, 1024:1152], 2)
                signal(n, heads_ready)

            def gla():
                for d in range(2):
                    for f in range(2):
                        b = vbank()
                        at = slice((2 * d + f) * 512, (2 * d + f + 1) * 512)
                        bias = sm("gate_b")[:, 2 * d + f:2 * d + f + 1]
                        ve.tensor_scalar(X[0][:, at], b[:, :], bias, 0.0, ALU.add, ALU.min)
                        then(ve.tensor_scalar(X[1][:, at], b[:, :], bias, None, ALU.add), v_free)
                        ve.scalar_tensor_tensor(X[1][:, at], X[0][:, at], 2.0, X[1][:, at], ALU.mult, ALU.subtract)
                signal(ve.memset(cum[:, :, :, :, 0:1].rearrange("p d f s t -> p (d f s) t"), 0.0), gate_in)
                dve.wait_ge(gate_in, own["gate_in"])
                seen.next(gate_soft, 2)
                for d in range(2):
                    for f in range(2):
                        for s in range(2):
                            lo = (2 * d + f) * 512 + s * S
                            n = ve.tensor_tensor_scan(cum[:, d, f, s, 1:S + 1], X[0][:, lo:lo + S], X[1][:, lo:lo + S], 0.0,
                                                      ALU.add, ALU.subtract)
                then(n)

                def halves(v, m):
                    w = v.rearrange("p g (b two m) -> p g b two m", two=2, m=m)
                    return w[:, :, :, 0, :], w[:, :, :, 1, :]

                def exponents(n):
                    m = LEVELS[n]
                    xl = X[n % 2].rearrange("p (d g t) -> p d g t", d=2, g=4)
                    for d in range(2):
                        c = cum[:, d].rearrange("p f s t -> p (f s) t")
                        mid = c[:, :, m:S + 1:2 * m]
                        mid = mid.unsqueeze(3).broadcast_to([P, 4, S // (2 * m), m])
                        el, er = halves(c[:, :, 1 - d:S + 1 - d], m)
                        ol, orr = halves(xl[:, d], m)
                        ve.tensor_tensor(ol, mid, el, ALU.subtract)
                        i = ve.tensor_tensor(orr, er, mid, ALU.subtract)
                    signal(i, expo_in)

                def decayed(n):
                    m = LEVELS[n]
                    xl = X[n % 2].rearrange("p (d g t) -> p d g t", d=2, g=4)
                    q, k = (v.rearrange("p f (s t) -> p (f s) t", s=2) for v in (qT, kT))
                    seen.next(expo_out)
                    for d in range(2):
                        ol, orr = halves(xl[:, d], m)
                        left, right = (k, q) if d == 0 else (q, k)
                        ve.tensor_tensor(ol, ol, halves(left, m)[0], ALU.mult)
                        i = ve.tensor_tensor(orr, orr, halves(right, m)[1], ALU.mult)
                    signal(i, level_ready)

                def quads(v):
                    return v.rearrange("p (j h t) -> p j h t", j=2, h=2)

                def take_pairs(n):
                    for d in range(1 if n == 0 else 2):
                        for s in range(2):
                            for odd in range(2):
                                b = vbank()
                                if n == 0:
                                    signal(ve.tensor_copy(att_other[:, s, :, odd::2, :], quads(b[:, :])), v_free)
                                else:
                                    mask = gla_masks[:, d, n - 1].unsqueeze(1).unsqueeze(1).broadcast_to([P, 2, 2, P])
                                    signal(ve.copy_predicated(att_same[:, s, :, odd::2, :], mask, quads(b[:, :])), v_free)

                dve.wait_ge(masks_loaded, 16)
                exponents(0)
                ve.memset(rows[:, 1024:2048], 0.0)
                for s in range(2):
                    for odd in range(2):
                        b = vbank()
                        signal(ve.tensor_tensor(att_same[:, s, :, odd::2, :], quads(b[:, :]),
                                                cn("diag2").unsqueeze(1).unsqueeze(1).broadcast_to([P, 2, 2, P]), ALU.mult), v_free)
                dve.wait_ge(v_free, own["v_free"])
                decayed(0)
                for n in range(len(LEVELS)):
                    if n + 1 < len(LEVELS):
                        exponents(n + 1)
                    else:
                        xi = X[len(LEVELS) % 2].rearrange("p (w f t) -> p w f t", w=4, f=2)
                        for w, (d, s) in enumerate(((0, CTX), (1, CTX), (0, LAT), (1, LAT))):
                            c = cum[:, d, :, s, :]
                            el = c[:, :, 1 - d:S + 1 - d]
                            if w in (0, 3):
                                i = ve.tensor_tensor(xi[:, w], c[:, :, S:S + 1].broadcast_to([P, 2, S]), el, ALU.subtract)
                            else:
                                i = ve.tensor_copy(xi[:, w], el)
                        signal(i, expo_in)
                    take_pairs(n)
                    if n + 1 < len(LEVELS):
                        decayed(n + 1)
                seen.next(expo_out)
                for w in range(4):
                    by = kT[:, :, S:2 * S] if w < 2 else qT[:, :, 0:S]
                    i = ve.tensor_tensor(xi[:, w], xi[:, w], by, ALU.mult)
                signal(i, level_ready)
                signal(ve.memset(head_ss[:, 0:1], 0.0), gla_done)
                modulation(4 * MOD_EARLY, 4 * MOD_STEPS, [(0, 1), (1, 0), (1, 1)])
                for t in range(NT):
                    b = vbank()
                    then(ve.tensor_copy(mix[:, t, 0:512], b[:, :]), v_free)
                    head_squares(mix[:, t, 0:512], 4, GLA_DV, 4 * t)
                inv_root(16, head_ss[:, 0:16], GLA_DV)
                seen.next(z_act_ready)
                for t in range(NT):
                    scale_heads(mix[:, t, 0:512], 4, GLA_DV, 4 * t)
                    gain_heads(mix[:, t, 0:512], 4, sm("gla_norm"))
                    then(ve.tensor_tensor(mix[:, t, 0:512], mix[:, t, 0:512], zs[0][:, t, 1024:1536], ALU.mult))

            def attention_first():
                for s in range(2):
                    keys = 512 if s == 0 else 256

                    def out(u):
                        qt = u // 8
                        b = vbank()
                        at = s * 16 + qt * 8
                        then(ve.reciprocal(rsum[:, 0:8], sums[:, at:at + 8]))
                        signal(ve.tensor_tensor(mix[:, 2 * s + qt, 512:1024].rearrange("p (h d) -> p h d", h=8),
                                                b[:, :].rearrange("p (h d) -> p h d", h=8), over(rsum[:, 0:8], HD), ALU.mult), v_free)

                    for u in range(LT * 8 + 3):
                        if u < LT * 8:
                            seen.next(raw_full)
                            signal(ve.tensor_reduce(nmax[:, s * 16 + u:s * 16 + u + 1], bank[4 + u % 2][:, 0:keys], AX.X, ALU.max,
                                                    negate=True), max_ready)
                        if u >= 3 and (u - 3) % 8 == 7:
                            out(u - 3)
                seen.next(probs_ready, 32)

            def reuse(u):
                if u >= 3:
                    seen.next(probs_ready)

            def attention_second():
                dve.wait_ge(late_loaded, 16)
                then(ve.tensor_scalar(neg_sink, sm("sink"), -1.0, None, ALU.mult))

                def out(u):
                    b = vbank()
                    at = u - 7
                    then(ve.tensor_tensor(rsum[:, 0:8], sums[:, at:at + 8], esink[:, at:at + 8], ALU.add))
                    then(ve.reciprocal(rsum[:, 0:8], rsum[:, 0:8]))
                    c = (at % 16) * HD
                    signal(ve.tensor_tensor(mix[:, at // 16, c:c + 512].rearrange("p (h d) -> p h d", h=8),
                                            b[:, :].rearrange("p (h d) -> p h d", h=8), over(rsum[:, 0:8], HD), ALU.mult), v_free)

                n_u = LT * 16
                for u in range(n_u + 3):
                    if u < n_u:
                        reuse(u)
                        b = SC.filled_bank(dve)
                        then(ve.tensor_tensor(s_ring[u % 3][:, 0:512], b[:, :], band[:, u // 16, :], ALU.add), s_free)
                        then(ve.tensor_reduce(lam[:, 0:1], s_ring[u % 3][:, 0:512], AX.X, ALU.max, negate=True))
                        signal(ve.tensor_tensor(nmax[:, u:u + 1], lam[:, 0:1], neg_sink[:, u % 16:u % 16 + 1], ALU.min), max_ready)
                    if u >= 3 and (u - 3) % 8 == 7:
                        out(u - 3)
                seen.next(probs_ready, 3)

            def residual(T, src, gate):
                for t in range(T):
                    then(ve.tensor_tensor(src[:, t, :], src[:, t, :], gate_rows[:, t // LT, :], ALU.mult))
                    signal(ve.tensor_tensor(x[:, t, :], x[:, t, :], src[:, t, :], ALU.add), x_ready)
                dve.wait_ge(x_ready, own["x_ready"])

            def routing(i, T):
                L = route[:, 0:20 * T].rearrange("p (t n) -> p t n", t=T)
                gl, el = L[:, :, 0:4], L[:, :, 4:20]
                at = [96]

                def buf(*shape):
                    n = int(np.prod(shape))
                    v = route[:, at[0]:at[0] + n]
                    at[0] += n
                    if len(shape) == 2:
                        return v.rearrange("p (a b) -> p a b", a=shape[0])
                    if len(shape) == 3:
                        return v.rearrange("p (a b c) -> p a b c", a=shape[0], b=shape[1])
                    return v

                b = vbank()
                bias = sm("router_b")[:, 20 * i:20 * i + 20]
                then(ve.tensor_tensor(L, b[:, 0:20 * T].rearrange("p (t n) -> p t n", t=T), under(bias, T), ALU.add), v_free)
                g_max, taken, total, g_weight, e_max = (buf(T) for _ in range(5))
                is_max, chosen, prob, rank, weight = (buf(T, 4) for _ in range(5))
                picked = buf(T, 4, 4)
                before = buf(T, 4, 4)
                ge, ee = (v[:, 0:4 * T].rearrange("p (t n) -> p t n", t=T) for v in route_buf)
                then(ve.tensor_reduce(g_max, gl, AX.X, ALU.max))
                signal(ve.tensor_tensor(ge, gl, over(g_max, 4), ALU.subtract), route_in)
                then(ve.tensor_tensor(is_max, gl, over(g_max, 4), ALU.is_equal))
                then(ve.memset(taken, 0.0))
                for g in range(4):
                    then(ve.tensor_tensor(chosen[:, :, g], is_max[:, :, g], taken, ALU.is_gt))
                    then(ve.tensor_tensor(taken, taken, is_max[:, :, g], ALU.max))
                then(ve.tensor_tensor(picked, el.rearrange("p t (g e) -> p t g e", g=4),
                                      chosen.unsqueeze(3).broadcast_to([P, T, 4, 4]), ALU.mult))
                then(ve.tensor_reduce(weight, picked.rearrange("p t g e -> p t e g"), AX.X, ALU.add))
                then(ve.tensor_reduce(e_max, weight, AX.X, ALU.max))
                signal(ve.tensor_tensor(ee, weight, over(e_max, 4), ALU.subtract), route_in)
                seen.next(route_out)
                then(ve.tensor_reduce(total, ge, AX.X, ALU.add))
                then(ve.reciprocal(g_weight, total))
                then(ve.memset(before, 0.0))
                seen.next(route_out)
                then(ve.tensor_reduce(total, ee, AX.X, ALU.add))
                then(ve.reciprocal(total, total))
                then(ve.tensor_tensor(prob, ee, over(total, 4), ALU.mult))
                for e in range(4):
                    mine = prob[:, :, e:e + 1]
                    if e:
                        n = ve.tensor_tensor(before[:, :, e, 0:e], prob[:, :, 0:e], mine.broadcast_to([P, T, e]), ALU.is_ge)
                    if e < 3:
                        n = ve.tensor_tensor(before[:, :, e, e + 1:4], prob[:, :, e + 1:4], mine.broadcast_to([P, T, 3 - e]), ALU.is_gt)
                then(n)
                then(ve.tensor_reduce(rank, before, AX.X, ALU.add))
                then(ve.tensor_scalar(rank, rank, 2.0, None, ALU.is_lt))
                then(ve.tensor_tensor(weight, prob, rank, ALU.mult))
                then(ve.tensor_reduce(total, weight, AX.X, ALU.add))
                then(ve.reciprocal(total, total))
                then(ve.tensor_tensor(total, total, g_weight, ALU.mult))
                then(ve.tensor_tensor(weight, weight, over(total, 4), ALU.mult))
                then(ve.tensor_tensor(comb[:, :, 0:T].rearrange("p (g e) t -> p t g e", g=4),
                                      chosen.unsqueeze(3).broadcast_to([P, T, 4, 4]),
                                      weight.unsqueeze(2).broadcast_to([P, T, 4, 4]), ALU.mult))

            def experts(i):
                T = NT if i == 0 else LT
                N = T * P
                base, per = NE * i, 2 * T
                d_base = 0 if i == 0 else NE * NT * 2
                comb_flat = comb.rearrange("p e t -> p (e t)")

                def gate(e, parity):
                    for f in range(2):
                        dve.wait_ge(g_free, e * 2 + (f + 1))
                        dve.wait_ge(u_full, e * 2 + (f + 1))
                        ve.tensor_tensor(hid[parity][:, f, 0:N], silu_g[parity][:, f, 0:N], bank[2 + f][:, 0:N],
                                         ALU.mult).then_inc(u_free, 1)
                    for f in range(2):
                        dve.wait_ge(u_free, e * 2 + (f + 1))
                        ve.tensor_copy(hid_high[parity][:, f, 0:N], hid[parity][:, f, 0:N]).then_inc(hid_high_ready, 1)
                    for f in range(2):
                        dve.wait_ge(hid_high_ready, e * 2 + (f + 1))
                        ve.tensor_tensor(hid_low[parity][:, f, 0:N], hid[parity][:, f, 0:N], hid_high[parity][:, f, 0:N],
                                         ALU.subtract).then_inc(hid_ready, 1)

                def add(e, n, first):
                    for t in range(T):
                        for h in range(2):
                            c = t * 2 + h
                            dst = mix[:, t, h * 512:(h + 1) * 512]
                            w = comb_flat[:, e * 4 + t:e * 4 + t + 1] if isinstance(e, int) else comb_flat[:, bass.ds(e * 4 + t, 1)]
                            dve.wait_ge(d_full, n + (c + 1))
                            src = bank[4 + c % 4][:, :]
                            if first:
                                ve.tensor_scalar(dst, src, w, None, ALU.mult).then_inc(d_free, 1)
                            else:
                                dve.wait_ge(d_free, n + (c + 1 - per))
                                ve.scalar_tensor_tensor(dst, src, w, dst, ALU.mult, ALU.add).then_inc(d_free, 1)

                first = STREAM[f"experts{i}"][0]
                chunk_low(first + 3)
                gate(base, 0)
                chunk_low(first + 4)
                gate(base + 1, 1)
                chunk_low(first + 5)
                add(0, d_base, True)
                chunk_low(first + 6)
                low0 = 2 * splits[0]

                def pair(j, ahead, last=False):
                    ahead(7)
                    gate(j * 2 + base, 0)
                    ahead(8)
                    add(j * 2 - 1, j * (2 * per) + (d_base - per), False)
                    ahead(9)
                    ahead(10)
                    gate(j * 2 + (base + 1), 1)
                    if not last:
                        ahead(11)
                    add(j * 2, j * (2 * per) + d_base, False)
                    if not last:
                        ahead(12)

                with dve.Fori(1, NE // 2 - 1) as j:
                    pair(j, lambda c: chunk_low(first + c, j * 12 + (low0 + 2 * (c - 6) - 12)))
                splits[0] += 6 * (NE // 2 - 2)
                pair(NE // 2 - 1, lambda c: chunk_low(first + c + 6 * (NE // 2 - 2)), last=True)
                chunk_low(first + 3 * NE - 1)
                add(NE - 1, d_base + (NE - 1) * per, False)
                dve.wait_ge(d_free, d_base + NE * per)

            def first_layer(i):
                T = NT if i == 0 else LT
                norm_rows(NT)
                if i == 0:
                    modulation(0, 4 * MOD_EARLY, [(0, 0)])
                    heads_first()
                    gla()
                    attention_first()
                else:
                    heads_second()
                    attention_second()
                dve.wait_ge(a_free, whole["y", i])
                residual(T, zo[T], 0)
                norm_rows(T)
                chunks_low(STREAM[f"experts{i}"][0], SLOTS)
                features_low("experts", T)
                routing(i, T)
                experts(i)
                dve.wait_ge(a_free, whole["gates2", i])
                residual(T, mix, 1)

            def second_layer(i):
                norm_rows(LT)
                chunks_low(STREAM[f"in{i}"][0], SLOTS)
                features_low("project", LT)
                chunks_low(STREAM[f"in{i}"][0] + SLOTS, 2 * IN_BLOCKS[i] - SLOTS)
                dve.wait_ge(a_free, whole["z", i])
                {2: sparse, 3: differential, 4: dilated_heads, 5: stick}[i]()
                lo, hi = {2: (2560, 3584), 3: (3072, 4096), 4: (2560, 3584), 5: (3072, 4096)}[i]
                seen.next(z_act_ready)
                for t in range(LT):
                    signal(ve.tensor_tensor(mix[:, t, :], mix[:, t, :], zs[i][:, t, lo:hi], ALU.mult), mix_ready)
                chunks_low(STREAM[f"out{i}"][0], SLOTS)
                features_low("project", LT)
                chunks_low(STREAM[f"out{i}"][0] + SLOTS, 4 - SLOTS)
                seen.next(sumsq_ready, LT)
                inv_root(LT, ss[:, 0:LT], D)
                dve.wait_ge(post_loaded, 16 * (i - 1))
                y = zo[LT]
                for t in range(LT):
                    then(ve.scalar_tensor_tensor(y[:, t, :], y[:, t, :], rstd[:, t:t + 1], post_row[:, :], ALU.mult, ALU.mult))
                    signal(ve.tensor_tensor(x[:, t, :], x[:, t, :], y[:, t, :], ALU.add), x_ready)
                dve.wait_ge(x_ready, own["x_ready"])

            def biased(u, bias, slope, maps, split=False):
                nk = bias.shape[1]
                dst = s_ring[u % 3][:, 0:maps * nk].rearrange("p (m k) -> p m k", m=maps)
                if split:
                    for m in range(maps):
                        b = SC.filled_bank(dve)
                        n = signal(ve.scalar_tensor_tensor(dst[:, m, :], bias, slope, b[:, 0:nk], ALU.mult, ALU.add), s_free)
                    dve.wait_ge(s_free, n)
                else:
                    b = SC.filled_bank(dve)
                    then(ve.scalar_tensor_tensor(dst, under(bias, maps), slope, b[:, 0:maps * nk].rearrange("p (m k) -> p m k", m=maps),
                                                 ALU.mult, ALU.add), s_free)
                signal(ve.tensor_reduce(nmax[:, maps * u:maps * (u + 1)], dst, AX.X, ALU.max, negate=True), max_ready)

            def sparse():
                z = zs[2]
                ve.memset(x[:, 2, :], 0.0)
                ve.memset(rows[:, 1024:2048], 0.0)
                ve.memset(cmp_p, 0.0)
                for t in range(LT):
                    kd = kdup[:, t * 1024:(t + 1) * 1024]
                    twice(kd[:, 0:512], z[:, t, 1536:1792], 4)
                    twice(kd[:, 512:1024], z[:, t, 2048:2304], 4)
                    n = twice(cdup[:, t, :], z[:, t, 1024:1536], 8)
                signal(n, heads_ready)
                seen.next(cmp_out)
                then(ve.tensor_scalar(gates, gates, 1.0, None, ALU.add))
                then(ve.reciprocal(gates, gates))
                gate = gates.rearrange("p (t b h) -> p t b h", t=LT, b=3)
                dve.wait_ge(a_free, whole["pairs"])
                for src, name in ((0, "pos_k"), (1, "pos_v")):
                    v = pairs[src].rearrange("p h (r b) -> p h r b", b=8)
                    o = blk[src].rearrange("p l (h n) -> p l h n", h=4)
                    for half in range(2):
                        pos = sm(name)[:, 8 * half:8 * half + 8]
                        for h in range(4):
                            n = ve.tensor_tensor(o[:, 8 * half:8 * half + 8, h, :],
                                                 v[:, h, half:half + CMP_N, :].rearrange("p n b -> p b n"),
                                                 over(pos, CMP_N), ALU.add)
                    signal(n, cmp_blk)
                for src in range(2):
                    b = vbank()
                    then(ve.tensor_copy(hidden[0:60, src * 256:(src + 1) * 256], b[0:60, 0:256]), v_free)
                h, g = hidden[0:60, :], gelu_t[0:60, :]
                then(ve.tensor_tensor(g, h, h, ALU.mult))
                then(ve.tensor_scalar(g, g, 0.044715, 1.0, ALU.mult, ALU.add))
                signal(ve.scalar_tensor_tensor(g, g, 2.0 * float(np.sqrt(2.0 / np.pi)), h, ALU.mult, ALU.mult), cmp_in)
                seen.next(cmp_out)
                then(ve.tensor_scalar(g, g, 1.0, None, ALU.add))
                then(ve.reciprocal(g, g))
                signal(ve.tensor_tensor(h, h, g, ALU.mult), cmp_hid)
                for qt in range(LT):
                    sc = cmp_s.rearrange("p (h n) -> p h n", h=16)
                    dve.wait_ge(late_loaded, 16)
                    for odd in range(2):
                        b = SC.filled_bank(dve)
                        dst, bias = (v.rearrange("p (h o n) -> p h o n", o=2, n=CMP_N)[:, :, odd, :] for v in (cmp_s, cmp_bias[:, qt, :]))
                        then(ve.tensor_tensor(dst, b[:, 0:120].rearrange("p (h n) -> p h n", h=8), bias, ALU.add), s_free)
                    then(ve.tensor_reduce(rsum[:, 0:16], sc, AX.X, ALU.max))
                    signal(ve.tensor_tensor(sc, sc, over(rsum[:, 0:16], CMP_N), ALU.subtract), cmp_in)
                    seen.next(cmp_out)
                    then(ve.tensor_tensor(sc, sc, under(cmp_valid[:, qt, :], 16), ALU.mult))
                    then(ve.tensor_reduce(rsum[:, 0:16], sc, AX.X, ALU.add))
                    then(ve.tensor_scalar(rsum[:, 0:16], rsum[:, 0:16], TINY, None, ALU.max))
                    then(ve.reciprocal(rsum[:, 0:16], rsum[:, 0:16]))
                    then(ve.tensor_tensor(rsum[:, 0:16], rsum[:, 0:16], gate[:, qt, 0, :], ALU.mult))
                    signal(ve.tensor_tensor(cmp_p.rearrange("p (h n) -> p h n", h=16)[:, :, 0:CMP_N], sc,
                                            over(rsum[:, 0:16], CMP_N), ALU.mult), cmp_probs)
                    for half in range(2):
                        b = vbank()
                        signal(ve.tensor_copy(mix[:, qt, half * 512:(half + 1) * 512], b[:, :]), v_free)
                slopes = alibi(16)

                def out(u):
                    qt, h0 = u // 16, u % 16 - 3
                    b = vbank()
                    then(ve.tensor_scalar(rsum[:, 0:8], sums[:, 2 * u - 6:2 * u + 2], TINY, None, ALU.max))
                    then(ve.reciprocal(rsum[:, 0:8], rsum[:, 0:8]))
                    then(ve.tensor_tensor(coef[:, 0:8].rearrange("p (h b) -> p h b", h=4),
                                          rsum[:, 0:8].rearrange("p (h b) -> p h b", h=4),
                                          gate[:, qt, 1:3, h0:h0 + 4].rearrange("p b h -> p h b"), ALU.mult))
                    then(ve.tensor_tensor(weighed.rearrange("p (m d) -> p m d", m=8), b[:, :].rearrange("p (m d) -> p m d", m=8),
                                          over(coef[:, 0:8], HD), ALU.mult), v_free)
                    dst = mix[:, qt, h0 * HD:(h0 + 4) * HD].rearrange("p (h d) -> p h d", h=4)
                    w = weighed.rearrange("p (h b d) -> p h b d", h=4, b=2)
                    for br in range(2):
                        then(ve.tensor_tensor(dst, dst, w[:, :, br, :], ALU.add))

                n_u = LT * 16
                for u in range(n_u + 3):
                    if u < n_u:
                        reuse(u)
                        biased(u, causal[:, u // 16, 0:P * (u // 16 + 1)], slopes[u % 16], 2)
                    if u >= 3 and (u - 3) % 4 == 3:
                        out(u - 3)
                seen.next(probs_ready, 3)

            def differential():
                lr = sm("lam", "p (a b n) -> p a b n", a=2, b=2)
                prod = scratch[:, 0:128].rearrange("p (a n) -> p a n", a=2)
                then(ve.tensor_tensor(prod, lr[:, :, 0, :], lr[:, :, 1, :], ALU.mult))
                signal(ve.tensor_reduce(lam[:, 0:2], prod, AX.X, ALU.add), cmp_in)
                seen.next(cmp_out)
                then(ve.tensor_tensor(lam[:, 4:5], lam[:, 3:4], lam[:, 2:3], ALU.subtract))
                then(ve.tensor_scalar(lam[:, 5:6], lam[:, 4:5], -LAMBDA_INIT, None, ALU.add))
                slopes = alibi(8)

                def combine(u):
                    nk = P * (u // 8 + 1)
                    seen.next(maps_ready)
                    p = p_ring[u % 3]
                    r = rsum[:, u % 2 * 2:u % 2 * 2 + 2]
                    then(ve.tensor_scalar(r, sums[:, 2 * u:2 * u + 2], TINY, None, ALU.max))
                    then(ve.reciprocal(r, r))
                    then(ve.tensor_scalar(p[:, nk:2 * nk], p[:, nk:2 * nk], r[:, 1:2], lam[:, 5:6], ALU.mult, ALU.mult))
                    signal(ve.scalar_tensor_tensor(p[:, 0:nk], p[:, 0:nk], r[:, 0:1], p[:, nk:2 * nk], ALU.mult, ALU.add), probs_mixed)

                n_u = LT * 8
                for u in range(n_u + 4):
                    if u < n_u:
                        biased(u, causal[:, u // 8, 0:P * (u // 8 + 1)], slopes[u % 8], 2, split=True)
                    if 1 <= u <= n_u:
                        combine(u - 1)
                    if u >= 4 and (u - 4) % 4 == 3:
                        v, b = u - 4, vbank()
                        c = (v % 8 - 3) * P
                        signal(ve.tensor_copy(mix[:, v // 8, c:c + 512], b[:, :]), v_free)
                dve.wait_ge(v_free, own["v_free"])
                for t in range(LT):
                    head_squares(mix[:, t, :], 8, 2 * HD, 8 * t)
                inv_root(16, head_ss[:, 0:16], 2 * HD)
                for t in range(LT):
                    scale_heads(mix[:, t, :], 8, 2 * HD, 8 * t)
                    v = mix[:, t, :].rearrange("p (h d) -> p h d", h=8)
                    then(ve.scalar_tensor_tensor(v, v, 1.0 - LAMBDA_INIT, under(sm("sub_gain"), 8), ALU.mult, ALU.mult))

            def dilated_heads():
                dve.wait_ge(dilated_loaded, 16)
                slopes = alibi(12)

                def soften(u):
                    h, qt = u % 4, u // 4
                    nk = P * (qt + 1)
                    s = s_ring[u % 3][:, 0:3 * nk]
                    for part in ((0, 1), (2,)):
                        b = SC.filled_bank(dve)
                        for n, g in enumerate(part):
                            i = ve.scalar_tensor_tensor(s[:, g * nk:(g + 1) * nk], dilated[:, g, qt, 0:nk], slopes[g * 4 + h],
                                                        b[:, n * nk:(n + 1) * nk], ALU.mult, ALU.add)
                        then(i, s_free)
                    signal(ve.tensor_reduce(nmax[:, u:u + 1], s, AX.X, ALU.max, negate=True), max_ready)

                def combine(u):
                    nk = P * (u // 4 + 1)
                    seen.next(maps_ready)
                    p = p_ring[u % 3]
                    then(ve.tensor_tensor(p[:, 0:nk], p[:, 0:nk], p[:, nk:2 * nk], ALU.add))
                    signal(ve.tensor_tensor(p[:, 0:nk], p[:, 0:nk], p[:, 2 * nk:3 * nk], ALU.add), probs_mixed)

                n_u = LT * 4
                for u in range(n_u + 4):
                    if u < n_u:
                        soften(u)
                    if 1 <= u <= n_u:
                        combine(u - 1)
                    if u >= 4 and (u - 4) % 2 == 1:
                        v, b = u - 4, vbank()
                        r = rsum[:, v // 2 % 2 * 2:v // 2 % 2 * 2 + 2]
                        then(ve.reciprocal(r, sums[:, v - 1:v + 1]))
                        c = (v % 4 - 1) * 256
                        signal(ve.tensor_tensor(mix[:, v // 4, c:c + 512].rearrange("p (h d) -> p h d", h=2),
                                                b[:, :].rearrange("p (h d) -> p h d", h=2), over(r, 256), ALU.mult), v_free)
                dve.wait_ge(v_free, own["v_free"])

            def stick():
                n_u = LT * 16
                for u in range(n_u + 4):
                    if u < n_u:
                        nk = P * (u // 16 + 1)
                        s = s_ring[u % 3]
                        b = SC.filled_bank(dve)
                        then(ve.tensor_tensor(s[:, 0:nk], b[:, 0:nk], strict[:, u // 16, 0:nk], ALU.add), s_free)
                        then(ve.tensor_scalar(s[:, 256:256 + nk], s[:, 0:nk], 0.0, None, ALU.max))
                        signal(ve.scalar_tensor_tensor(s[:, 512:512 + nk], s[:, 256:256 + nk], -2.0, s[:, 0:nk], ALU.mult, ALU.add), soft_in)
                    if 1 <= u <= n_u:
                        v = u - 1
                        nk = P * (v // 16 + 1)
                        s, p = s_ring[v % 3], p_ring[v % 3]
                        seen.next(soft_out, 2)
                        reuse(v)
                        dve.wait_ge(soft_in, own["soft_in"])
                        then(ve.tensor_tensor_scan(p[:, 0:nk][:, ::-1], s[:, 256:256 + nk][:, ::-1], s[:, 512:512 + nk][:, ::-1], 0.0,
                                                   ALU.add, ALU.add))
                        signal(ve.tensor_tensor(p[:, 256:256 + nk], s[:, 0:nk], p[:, 0:nk], ALU.subtract), max_ready)
                    if u >= 4 and (u - 4) % 8 == 7:
                        v, b = u - 4, vbank()
                        c = (v % 16 - 7) * HD
                        signal(ve.tensor_copy(mix[:, v // 16, c:c + 512], b[:, :]), v_free)
                seen.next(probs_ready, 3)
                dve.wait_ge(v_free, own["v_free"])

            scratch2 = scratch
            turned = ar(5632, 2304)
            neg_sink = coef[:, 0:16]
            dve.wait_ge(small_loaded, 16)
            dve.wait_ge(const_loaded, 16)
            for i in range(min(layers, 2)):
                first_layer(i)
            for i in range(2, layers):
                second_layer(i)

        @block.gpsimd
        def _(pool):
            seen = Seen(pool)
            nc.gpsimd.memset(half_neg[:, :], -0.5).then_inc(pool_step, 1)
            pool.wait_ge(pool_step, 1)

            def inv_root(dst, src, n):
                seen.next(meansq_ready)
                nc.gpsimd.tensor_tensor(dst[:, 0:n], src[:, 0:n], half_neg[:, 0:n], ALU.pow).then_inc(rstd_ready, 1)

            def rows_inv_root(T):
                inv_root(rstd, ss, T)

            def load_post(i, x_tiles):
                if x_tiles:
                    pool.wait_ge(x_ready, x_tiles)
                pool.dma_start(post_row[:, :], d_post[i - 2:i - 1, :].broadcast_to([P, D])).then_inc(post_loaded, 16)

            if layers > 2:
                load_post(2, 0)
            rows_inv_root(NT)
            inv_root(head_rstd, head_ss, 40)
            inv_root(head_rstd, head_ss, 16)
            if layers > 1:
                pool.wait_ge(gla_done, 1)
                pool.dma_start(phase[:, 0:N_LATE], d_late).then_inc(late_loaded, 16)
            rows_inv_root(NT)
            if layers > 1:
                rows_inv_root(NT)
                inv_root(head_rstd, head_ss, 40)
                rows_inv_root(LT)
            for i in range(2, layers):
                rows_inv_root(LT)
                if i == 3:
                    inv_root(head_rstd, head_ss, 16)
                rows_inv_root(LT)
                x_tiles = 12 + 2 * (i - 1)
                if i + 1 < layers:
                    load_post(i + 1, x_tiles)
                if i == 2 and layers > 4:
                    pool.dma_start(rows[:, :], d_dilated).then_inc(dilated_loaded, 16)

        @block.sync
        def _(sp):
            sp.dma_start(small[:, :], d_small).then_inc(small_loaded, 16)
            sp.dma_start(x[:, 0:LT, :], d_x.rearrange("(t p) n -> p t n", p=P)).then_inc(x_loaded, 16)
            sp.dma_start(x[:, LT:NT, :], d_ctx.rearrange("(t p) n -> p t n", p=P)).then_inc(x_loaded, 16)
            n_res = N_CONST - 2 * 7 * P
            sp.dma_start(const[:, :], d_const[:, 0:n_res]).then_inc(const_loaded, 16)

            def load(n):
                if n == 2 * MOD_EARLY:
                    sp.dma_start(phase[:, 0:2 * 7 * P], d_const[:, n_res:N_CONST]).then_inc(masks_loaded, 16)
                slot = tenancy[n][0]
                if n >= SLOTS:
                    sp.wait_ge(*tenancy[n - SLOTS][1:])
                sp.dma_start(ring[:, slot, :], d_w[n]).then_inc(slot_full[slot], 16)

            def expert_loads(i):
                first, half0, d_base = moe_at[i]
                base, per = NE * i, 2 * (NT if i == 0 else LT)

                def slot(c):
                    return (first + c) % SLOTS

                def used(kind, e, kh, k0=0):
                    if kind == "up":
                        return (chunk_used, e + (half0 + 1)) if kh == 0 else (u_full, e * 2 + (2 * base + 2))
                    return d_full, e * per + (d_base + per)

                order = []
                for kind, e in expert_order():
                    order += [(kind, e, 0), (kind, e, 1)] if kind == "up" else [(kind, e, 0)]

                def load_c(c):
                    prev = first + c - SLOTS
                    if c >= SLOTS:
                        sp.wait_ge(*used(*order[c - SLOTS]))
                    elif prev >= 0:
                        sp.wait_ge(*tenancy[prev][1:])
                    sp.dma_start(ring[:, slot(c), :], d_w[first + c]).then_inc(slot_full[slot(c)], 16)

                for c in range(5 + 6):
                    load_c(c)
                with sp.Fori(2, NE // 2) as j:
                    for q in range(6):
                        c = 5 + 6 + q
                        kind, e, kh = order[c - SLOTS]
                        sp.wait_ge(*used(kind, j * 2 + (e - 4), kh))
                        src = d_w[bass.ds(j * 6 + (first + c - 12), 1)].rearrange("a p n -> (a p) n")
                        sp.dma_start(ring[:, slot(c), :], src).then_inc(slot_full[slot(c)], 16)
                load_c(3 * NE - 1)
                for c in range(3 * NE):
                    kind, e, kh = order[c]
                    tenancy[first + c][1:] = used(kind, e, kh)

            n = 0
            for i in range(min(layers, 2)):
                while n < moe_at[i][0]:
                    load(n)
                    n += 1
                expert_loads(i)
                n += 3 * NE
            while n < len(tenancy):
                load(n)
                n += 1
            sp.wait_ge(x_ready, {1: 8, 2: 12}.get(layers, 12 + 2 * (layers - 2)))
            sp.dma_start(d_out.rearrange("(t p) n -> p t n", p=P), x[:, 0:LT, :]).then_inc(out_done, 16)
            sp.wait_ge(out_done, 16)


def kernel(**inputs):
    import concourse.bacc as bacc
    from concourse.bass_utils import run_bass_kernel_spmd

    nc = bacc.Bacc("TRN2", target_bir_lowering=False, num_devices=1)
    laid = host_layout(inputs)
    arrays, aps = {}, []
    for name in ("x", "ctx", "weights", "small", "norm_post", "const", "late", "dilated"):
        arrays[name + "_dram"] = laid[name]
        aps.append(nc.dram_tensor(name + "_dram", laid[name].shape, F32, kind="ExternalInput").ap())
    aps.append(nc.dram_tensor("out_dram", (S, D), F32, kind="ExternalOutput").ap())
    build_program(nc, *aps)
    r = run_bass_kernel_spmd(nc, [arrays], core_ids=[0])
    return r.results[0]["out_dram"].reshape(1, S, D)
```

```python
from contextlib import ExitStack

import numpy as np

import concourse.bass as bass
from concourse import mybir

F32 = mybir.dt.float32
F32R = mybir.dt.float32r
U32 = mybir.dt.uint32
ACT = mybir.ActivationFunctionType
ALU = mybir.AluOpType
AX = mybir.AxisListType

P = 128
S = 256
D = 1024
KT = D // P
LAT, CTX = 0, 1
NT = 2 * S // P
LT = S // P
HALF = 4 * 512
SLOTS = 3
NEG = -1e30
EPS = 1e-6
TINY = 1e-30
HD = 64
QSCALE = HD ** -0.5

N_MOD = 6
MOD_STEPS = 2 * N_MOD * D // 512
MOD_EARLY = 2 * D // 512
MOD_GATES, MOD_START, MOD_LEVEL = 1, 2, 3
GLA_H, GLA_DK, GLA_DV = 4, 64, 128
GLA_GATE_NORM = 16.0
GATE_RANK = 16
LEVELS = [128, 64, 32, 16, 8, 4, 2, 1]
NE, NG, EPG = 16, 4, 4
FE = 256
CMP_N, CMP_L, CMP_ST = (S - 32) // 16 + 1, 32, 16
LAMBDA_INIT = 0.8 - 0.6 * float(np.exp(-0.3))
IN_BLOCKS = {2: 7, 3: 8, 4: 7, 5: 8}
GATE_AT = {2: 2560, 3: 3072, 4: 2560, 5: 3072}
HEADS_AFTER = {2: 5, 3: 6, 4: 5, 5: 6}
Q_ROOTS = 2 * NT
CMP_GELU, CMP_TURN, CMP_KV, CMP_SCORE, CMP_PROBS, CMP_OUT = 2, 5, 8, (10, 16), (13, 19), (15, 21)
C_PATTERNS = ((128, 1), (512, 4), (2048, 16))


def alibi(n):
    return [float(np.float32(2.0 ** (-8.0 * (i + 1) / n))) for i in range(n)]


def fields(table):
    at, out = 0, {}
    for name, width in table:
        out[name] = (at, at + width)
        at += width
    return out, at


SMALL, N_SMALL = fields([
    ("cond", KT * 2), ("mod_b", 2 * 48), ("norm_mix", 2 * KT), ("norm_ffn", 2 * KT), ("norm_pre", 4 * KT),
    ("gate_b", 4), ("att_q", HD), ("att_k", HD), ("swa_q", HD), ("swa_k", HD), ("gla_norm", GLA_DV),
    ("sub_gain", 2 * HD), ("router_b", 2 * 20), ("sink", 16), ("lam", 4 * HD), ("pos_k", 16), ("pos_v", 16),
    ("router_w", 2 * KT * 20), ("lr_w", KT * 32), ("gl_w", KT * 48), ("gate_w", 2 * 256),
    ("w2_k", 2 * 128), ("w2_v", 2 * 64)])
CONST, N_CONST = fields([("ident", P), ("causal", LT * S), ("rope", LT * 64), ("diag2", P), ("pick", 2),
                         ("gla_masks", 2 * 7 * P)])
LATE, N_LATE = fields([("band", LT * 512), ("cmp_bias", LT * 16 * CMP_N), ("cmp_valid", LT * CMP_N)])
PHASE = max(2 * 7 * P, N_LATE)
DILATED, N_DILATED = fields([("dilated", 3 * LT * S), ("strict", LT * S)])


STREAM, N_CHUNKS = fields(
    [("mod_early", 2 * MOD_EARLY), ("in0", 9), ("mod_late", 2 * (MOD_STEPS - MOD_EARLY)), ("out0", 4), ("experts0", 3 * NE),
     ("in1", 5), ("out1", 4), ("experts1", 3 * NE), ("in2", 2 * IN_BLOCKS[2]), ("compress", 4), ("out2", 4)]
    + [(f"{kind}{i}", 2 * n) for i in (3, 4, 5) for kind, n in (("in", IN_BLOCKS[i]), ("out", 2))])


def const_arrays():
    p = np.arange(P)
    t = np.arange(S).reshape(LT, P)
    k = np.arange(S)
    dist = t[:, :, None] - k[None, None, :]
    causal = np.where(dist >= 0, -dist, NEG)
    inv = (np.float32(10000.0) ** (-np.arange(0, 32, 2, dtype=np.float32) / np.float32(32))).astype(np.float32)
    row, col = (np.arange(S) // 64).astype(np.float32), (np.arange(S) % 64).astype(np.float32)
    ang = np.stack([row[:, None] * inv, col[:, None] * inv], 1)
    rope = np.stack([np.cos(ang), np.sin(ang)], 1).reshape(LT, P, 64)
    masks = np.zeros((2, 7, P, P))
    for n, m in enumerate(LEVELS[1:]):
        blk, right = p // (2 * m), (p // m) % 2
        fwd = (blk[:, None] == blk[None, :]) & (right[:, None] == 0) & (right[None, :] == 1)
        masks[0, n], masks[1, n] = fwd, fwd.T
    band = np.zeros((LT, P, 512))
    band[:, :, :S] = np.where(np.abs(dist) <= 128, 0.0, NEG)
    end = CMP_ST * np.arange(CMP_N) + CMP_L - 1
    cd = t[:, :, None] - end[None, None, :]
    sl = np.array(alibi(16))
    cmp_bias = np.where(cd[:, :, None, :] >= 0, -sl[None, None, :, None] * cd[:, :, None, :], NEG)
    dil = np.stack([np.where((dist >= 0) & (dist <= w) & (dist % d == 0), -dist, NEG) for w, d in C_PATTERNS])

    def pack(a):
        return np.moveaxis(a, -2, 0).reshape(P, -1).astype(np.float32)

    pick = (p[:, None] % 32 == np.arange(2)[None, :]).astype(np.float32)
    const = np.concatenate([np.eye(P), pack(causal), pack(rope), 2 * np.eye(P), pick, pack(masks)], 1)
    late = np.concatenate([pack(band), np.moveaxis(cmp_bias, 1, 0).reshape(P, -1),
                           pack((cd >= 0).astype(np.float64))], 1)
    dilated = np.concatenate([pack(dil), pack(np.where(dist > 0, 0.0, NEG))], 1)
    return [np.ascontiguousarray(a, np.float32) for a in (const, late, dilated)]


def by_rows(w):
    return w.reshape(-1, P, w.shape[1]).transpose(1, 0, 2)


def chunks_of(w):
    r = by_rows(w)
    out = []
    for n in range(0, w.shape[1], 512):
        if n + 512 <= w.shape[1]:
            out += [r[:, 0:4, n:n + 512], r[:, 4:8, n:n + 512]]
        else:
            out.append(r[:, :, n:n + 256])
    return out


def gates_first(i, w):
    return np.concatenate([w[:, GATE_AT[i]:GATE_AT[i] + D], w[:, 0:GATE_AT[i]]], 1)


def expert_order():
    out = [("up", 0), ("up", 1), ("down", 0)]
    for i in range(1, NE // 2):
        out += [("up", 2 * i), ("down", 2 * i - 1), ("up", 2 * i + 1), ("down", 2 * i)]
    return out + [("down", NE - 1)]


def expert_chunks(gate, up, down):
    out = []
    for kind, e in expert_order():
        if kind == "up":
            out += chunks_of(np.concatenate([gate[e // EPG, e % EPG], up[e // EPG, e % EPG]], 1))
        else:
            out.append(by_rows(down[e // EPG, e % EPG]))
    return out


def host_layout(a):
    a = {k: np.asarray(v) for k, v in a.items()}
    ev, od, aw, cw = a["ev_w_in"][0], a["od_w_in"][0], a["a_w_in_2"][0], a["c_w_in_2"][0]
    mod = chunks_of(np.concatenate(list(a["mod_w"]), 1))
    w = mod[:2 * MOD_EARLY]
    w += chunks_of(np.concatenate([ev[:, 0:1536], ev[:, 1568:2336]], 1))
    w += mod[2 * MOD_EARLY:]
    w += chunks_of(a["ev_w_out"][0])
    w += expert_chunks(a["exp_w_gate"][0], a["exp_w_up"][0], a["exp_w_down"][0])
    w += chunks_of(od[:, 1024:1280]) + chunks_of(od[:, 0:1024])
    w += chunks_of(a["od_w_out"][0])
    w += expert_chunks(a["exp_w_gate"][1], a["exp_w_up"][1], a["exp_w_down"][1])
    w += chunks_of(gates_first(2, np.concatenate([aw[:, 0:2560], aw[:, 2608:3632]], 1)))
    for name in ("a_cmp_w1_k_2", "a_cmp_w1_v_2"):
        r = by_rows(a[name][0])
        w += [r[:, 0:8], r[:, 8:16]]
    w += chunks_of(a["a_w_out_2"][0])
    w += chunks_of(gates_first(3, a["b_w_in_2"][0])) + chunks_of(a["b_w_out_2"][0])
    w += chunks_of(gates_first(4, cw)) + chunks_of(a["c_w_out_2"][0])
    w += chunks_of(gates_first(5, a["d_w_in_2"][0])) + chunks_of(a["d_w_out_2"][0])
    weights = np.empty((len(w), P, HALF), np.float32)
    for n, c in enumerate(w):
        weights[n] = c.reshape(P, HALF)

    def cols(v):
        v = v.reshape(-1, P)
        return v.T

    def row(v):
        return np.broadcast_to(v.reshape(1, -1), (P, v.size))

    def pos(v):
        return v.reshape(16, P).T

    gate_w = np.zeros((P, 2, 256), np.float32)
    gate_w[0:16, 0], gate_w[16:32, 1] = a["gla_gate_w"][0, 0], a["gla_gate_w"][0, 1]
    cond = np.stack([cols(a["c"]), cols(a["c_ctx"])], 2)
    router_w = np.concatenate([a["router_group_w"], a["router_expert_w"]], 2)
    router_b = np.concatenate([a["router_group_b"], a["router_expert_b"]], 1)
    w2k = by_rows(a["a_cmp_w2_k_2"][0])
    parts = {
        "cond": cond, "mod_b": cols(a["mod_b"]), "norm_mix": cols(a["norm_mix"]), "norm_ffn": cols(a["norm_ffn"]),
        "norm_pre": cols(a["norm_pre_2"]), "gate_b": cols(a["gla_gate_b"][0]),
        "att_q": row(a["att_q_norm"]), "att_k": row(a["att_k_norm"]), "swa_q": row(a["swa_q_norm"]),
        "swa_k": row(a["swa_k_norm"]), "gla_norm": row(a["gla_out_norm"]), "sub_gain": row(a["b_sub_gain_2"]),
        "router_b": row(router_b), "sink": row(a["swa_sink"]), "lam": row(a["b_lambda_2"]),
        "pos_k": pos(a["a_cmp_pos_k_2"]), "pos_v": pos(a["a_cmp_pos_v_2"]),
        "router_w": np.stack([by_rows(router_w[i]) for i in range(2)], 1),
        "lr_w": by_rows(ev[:, 1536:1568]), "gl_w": by_rows(aw[:, 2560:2608]), "gate_w": gate_w,
        "w2_k": np.concatenate([w2k, w2k], 2), "w2_v": by_rows(a["a_cmp_w2_v_2"][0]),
    }
    small = np.empty((P, N_SMALL), np.float32)
    for name, (lo, hi) in SMALL.items():
        small[:, lo:hi] = parts[name].reshape(P, hi - lo)
    const, late, dilated = const_arrays()
    return {
        "x": np.ascontiguousarray(a["x"][0]), "ctx": np.ascontiguousarray(a["ctx"][0]), "weights": weights,
        "small": small, "norm_post": np.ascontiguousarray(a["norm_post_2"]),
        "const": const, "late": late, "dilated": dilated,
    }


class Banks:

    def __init__(self, banks, full, free):
        self.banks, self.full, self.free = banks, full, free
        self.fills = self.drains = 0

    def take(self, pe):
        n = self.fills
        if n >= len(self.banks):
            pe.wait_ge(self.free, n - len(self.banks) + 1)
        self.fills += 1
        return self.banks[n % len(self.banks)]

    def drained(self, pe, fills=None):
        fills = self.fills if fills is None else fills
        if fills:
            pe.wait_ge(self.free, fills)

    def filled_bank(self, eng):
        self.drains += 1
        eng.wait_ge(self.full, self.drains)
        return self.banks[(self.drains - 1) % len(self.banks)]


class Seen:

    def __init__(self, eng):
        self.eng, self.count = eng, {}

    def next(self, semaphore, n=1):
        self.count[semaphore.name] = self.count.get(semaphore.name, 0) + n
        self.eng.wait_ge(semaphore, self.count[semaphore.name])


def early_half(i, u, n_u):
    n, rest = divmod(u - n_u // (4 if i == 0 else 8), max(1, n_u // 12))
    return n if rest == 0 and 0 <= n < 2 * SLOTS else None


def build_program(nc, d_x, d_ctx, d_w, d_small, d_post, d_const, d_late, d_dilated, d_out, layers=6):
    with ExitStack() as stack:
        def sb(name, *shape):
            return stack.enter_context(nc.sbuf_tensor(name, [P, *shape], F32))

        def sem(name):
            return stack.enter_context(nc.semaphore(name))

        def shared(dtype):
            return [nc.sbuf_tensor(f"{name}_{dtype.name}", [P, *shape], dtype)
                    for name, shape in (("x", (NT, D)), ("ring", (SLOTS, HALF)), ("hT", (KT * 2 * S,)),
                                        ("Z", (NT * 2336,)), ("mix", (NT, D)), ("arena", (8200,)))]

        bank = [stack.enter_context(nc.psum_tensor(f"bank{i}", [P, 512], F32)) for i in range(8)]

        with ExitStack() as zone:
            x, ring, hT_flat, Z, mix, arena = (zone.enter_context(t) for t in shared(F32))
        x_r, ring_low, hT_r, Z_r, mix_r, arena_r = (stack.enter_context(t) for t in shared(F32R))
        ring_high = stack.enter_context(nc.sbuf_tensor("ring_high", [P, SLOTS, HALF], F32R))
        rows = sb("rows", 2 * D)
        const = sb("const", N_CONST - 2 * 7 * P)
        phase = sb("phase", PHASE)
        small = sb("small", N_SMALL)
        post_row = sb("post_row", D)
        scratch = sb("scratch", 1024)
        stat = sb("stat", 768)
        half_neg = sb("half_neg", 40)
        modT = sb("modT", 2 * 48, 2)
        modA = sb("modA", 2, 2, KT, 2)
        cond = sb("cond", KT, 2)

        hT4 = hT_flat[:, :].rearrange("p (k t) -> p k t", k=KT)
        hT2 = hT_flat[:, 0:KT * S].rearrange("p (k t) -> p k t", k=KT)
        hT_spare = hT_flat[:, KT * S:]
        split_at = {"first": (arena_r[:, 0:KT * 2 * S], arena_r[:, KT * 2 * S:2 * KT * 2 * S]),
                    "experts": (Z_r[:, 0:KT * 2 * S], Z_r[:, KT * 2 * S:2 * KT * 2 * S]),
                    "project": (x_r[:, LT:NT, :].rearrange("p t n -> p (t n)"), mix_r[:, LT:NT, :].rearrange("p t n -> p (t n)"))}

        def split_views(name, T):
            return [v[:, 0:KT * T * P].rearrange("p (k t) -> p k t", k=KT) for v in split_at[name]]


        def sm(name, pattern=None, **sizes):
            lo, hi = SMALL[name]
            v = small[:, lo:hi]
            return v.rearrange(pattern, **sizes) if pattern else v

        def cn(name):
            lo, hi = CONST[name]
            return const[:, lo:hi]

        ident = cn("ident")
        causal = cn("causal").rearrange("p (t k) -> p t k", t=LT)
        rope = cn("rope").rearrange("p (t c a f) -> p t c a f", t=LT, c=2, a=2)
        gla_masks = phase[:, 0:2 * 7 * P].rearrange("p (d l t) -> p d l t", d=2, l=7).bitcast(U32)

        def late(name):
            lo, hi = LATE[name]
            return phase[:, lo:hi]

        band = late("band").rearrange("p (t k) -> p t k", t=LT)
        cmp_bias = late("cmp_bias").rearrange("p (t n) -> p t n", t=LT)
        cmp_valid = late("cmp_valid").rearrange("p (t n) -> p t n", t=LT)
        dilated = rows[:, 0:3 * LT * S].rearrange("p (g t k) -> p g t k", g=3, t=LT)
        strict = rows[:, 3 * LT * S:4 * LT * S].rearrange("p (t k) -> p t k", t=LT)
        gate_rows = rows[:, :].rearrange("p (s n) -> p s n", s=2)

        x_loaded, small_loaded, const_loaded = sem("x_loaded"), sem("small_loaded"), sem("const_loaded")
        late_loaded, dilated_loaded, post_loaded = sem("late_loaded"), sem("dilated_loaded"), sem("post_loaded")
        slot_full = [sem(f"slot_full{s}") for s in range(SLOTS)]
        high_ready = sem("high_ready")
        low_ready = sem("low_ready")
        act_high = sem("act_high")
        act_low = sem("act_low")
        hid_high_ready = sem("hid_high_ready")
        hid_ready = sem("hid_ready")
        chunk_used = sem("chunk_used")
        a_full, a_free = sem("a_full"), sem("a_free")
        s_full, s_free = sem("s_full"), sem("s_free")
        v_full, v_free = sem("v_full"), sem("v_free")
        masks_loaded = sem("masks_loaded")
        cond_ready = sem("cond_ready")
        mod_cleared = sem("mod_cleared")
        mod_full = sem("mod_full")
        mod_copied = sem("mod_copied")
        mod_turned = sem("mod_turned")
        mod_ready = sem("mod_ready")
        sumsq_ready = sem("sumsq_ready")
        sums_ready = sem("sums_ready")
        half_squares = sem("half_squares")
        mean_ready = sem("mean_ready")
        rstd_ready = sem("rstd_ready")
        scale_ready = sem("scale_ready")
        half_neg_ready = sem("half_neg_ready")
        normed_ready = sem("normed_ready")
        sum_gated = sem("sum_gated")
        sum_added = sem("sum_added")
        x_ready = sem("x_ready")
        heads_ready = sem("heads_ready")
        mix_ready = sem("mix_ready")
        z_act_ready = sem("z_act_ready")
        gate_in, gate_soft = sem("gate_in"), sem("gate_soft")
        expo_in, expo_out = sem("expo_in"), sem("expo_out")
        level_ready = sem("level_ready")
        gla_done = sem("gla_done")
        max_ready = sem("max_ready")
        probs_ready = sem("probs_ready")
        maps_ready = sem("maps_ready")
        probs_mixed = sem("probs_mixed")
        soft_in, soft_out = sem("soft_in"), sem("soft_out")
        cmp_blk, cmp_hid, cmp_probs = sem("cmp_blk"), sem("cmp_hid"), sem("cmp_probs")
        pairs_full, pairs_free = sem("pairs_full"), sem("pairs_free")
        raw_full = sem("raw_full")
        cmp_in, cmp_out = sem("cmp_in"), sem("cmp_out")
        route_in, route_out = sem("route_in"), sem("route_out")
        g_full, g_free = sem("g_full"), sem("g_free")
        u_full, u_free = sem("u_full"), sem("u_free")
        d_full, d_free = sem("d_full"), sem("d_free")
        dve_step = sem("dve_step")
        out_done = sem("out_done")

        A = Banks(bank[0:4], a_full, a_free)
        SC = Banks(bank[4:6], s_full, s_free)
        V = Banks(bank[6:8], v_full, v_free)
        G = Banks(bank[0:4], pairs_full, pairs_free)

        whole = {}
        split_drains = []
        tenancy = []
        moe_at = {}

        zs = {0: Z[:, :].rearrange("p (t n) -> p t n", t=NT),
              1: Z[:, 0:NT * 1280].rearrange("p (t n) -> p t n", t=NT),
              2: Z[:, 0:LT * 3632].rearrange("p (t n) -> p t n", t=LT),
              3: Z[:, 0:LT * 4096].rearrange("p (t n) -> p t n", t=LT),
              4: Z[:, 0:LT * 3584].rearrange("p (t n) -> p t n", t=LT),
              5: Z[:, 0:LT * 4096].rearrange("p (t n) -> p t n", t=LT)}
        q_turned = Z[:, NT * 1280 + 1024:NT * 1280 + 3072].rearrange("p (t n) -> p t n", t=LT)
        q_tables = Z[:, NT * 1280 + 3072:NT * 1280 + 3328].rearrange("p (t n a f) -> p t n a f", t=LT, n=4, a=2)
        zo = {T: Z[:, 0:T * D].rearrange("p (t n) -> p t n", t=T) for T in (2, 4)}

        def ar(lo, n):
            return arena[:, lo:lo + n]

        mod_bank, mod_turn_bank = bank[4], bank[5]
        mod_rows_early = scratch[:, 0:512].rearrange("p (j n) -> p j n", j=4)
        mod_rows_late = mix[:, 0:NT, 768:896]

        qT = ar(0, 1024).rearrange("p (f t) -> p f t", f=2)
        kT = ar(1024, 1024).rearrange("p (f t) -> p f t", f=2)
        cum = ar(2048, 2056).rearrange("p (d f s t) -> p d f s t", d=2, f=2, s=2)
        X = [ar(4104 + 2048 * b, 2048) for b in range(2)]
        lrT = rows[:, 0:512]
        att_same = hT_flat[:, 0:2048].rearrange("p (s j h t) -> p s j h t", s=2, j=2, h=4)
        att_other = hT_flat[:, 2048:4096].rearrange("p (s j h t) -> p s j h t", s=2, j=2, h=4)
        kst = rows[:, 0:1024].rearrange("p (d f j k) -> p d f j k", d=2, f=2, j=2)
        state = rows[:, 1024:2048].rearrange("p (d f v) -> p d f v", d=2, f=2)
        silu_g = [ar(1024 * b, 1024).rearrange("p (f t) -> p f t", f=2) for b in range(2)]
        hid = [ar(2048 + 1024 * b, 1024).rearrange("p (f t) -> p f t", f=2) for b in range(2)]
        hid_high = [hT_r[:, 1024 * b:1024 * (b + 1)].rearrange("p (f t) -> p f t", f=2) for b in range(2)]
        hid_low = [hT_r[:, 1024 * b:1024 * (b + 1)].rearrange("p (f t) -> p f t", f=2) for b in (2, 3)]
        route = ar(4096, 512)
        route_buf = [ar(4608 + 16 * b, 16) for b in range(2)]
        kdup = Z[:, LT * 3632:LT * 3632 + 2048]
        cdup = mix[:, 2:4, :]
        pairs = [rows[:, 512 * b:512 * b + 512].rearrange("p (h m) -> p h m", h=4) for b in range(2)]
        vcmp = rows[:, 1024:2048].rearrange("p (h n) -> p h n", h=4)
        blk = [ar(4096 + 960 * b, 960).rearrange("p (l n) -> p l n", l=16) for b in range(2)]
        hidden = kdup[:, 0:512]
        hidT_k = kdup[:, 512:632].rearrange("p (k n) -> p k n", k=2)
        kcmpT = kdup[:, 632:692]
        cmp_s = kdup[:, 692:932]
        cmp_p = kdup[:, 932:1444]
        cmpT = kdup[:, 1444:1956]
        cmp_rows = mix[:, 2:4, :]
        hidT_v = x[:, 2, :].rearrange("p (k h g n) -> p k h g n", k=2, h=4, g=4)
        gelu_t = x[:, 3, 0:512]
        weighed = hT_spare[:, 1536:2048]

        aq = ar(0, 2048)
        ak = ar(2048, 2048)
        s_ring = [ar(4096 + 768 * b, 768) for b in range(2)] + [scratch[:, 0:768]]
        p_ring = [ar(5632 + 768 * b, 768) for b in range(3)]
        pT_ring = [hT_spare[:, 512 * b:512 * b + 512] for b in range(3)]
        nmax = stat[:, 0:128]
        sums = stat[:, 128:256]
        rsum = stat[:, 256:320]
        head_ss = stat[:, 320:400]
        head_rstd = stat[:, 400:480]
        ss = stat[:, 480:484]
        ss_half = stat[:, 752:756].rearrange("p (t h) -> p t h", t=LT)
        rstd = stat[:, 484:488]
        esink = stat[:, 488:520]
        comb = stat[:, 520:584].rearrange("p (e t) -> p e t", e=NE)
        lam = stat[:, 584:592]
        gates = stat[:, 592:688]
        coef = stat[:, 688:752]

        block = stack.enter_context(nc.Block())

        def down_half(c):
            return c // 2, slice(c % 2 * 512, (c % 2 + 1) * 512)

        @block.scalar
        def _(act):
            seen = Seen(act)

            def drain(*copies, func=ACT.Copy):
                b = A.filled_bank(act)
                for dst, src, scale, bias in copies:
                    f = func if bias is None else ACT.Identity
                    i = nc.scalar.activation(dst, src(b), f, scale=scale, bias=0.0 if bias is None else bias)
                i.then_inc(a_free, 1)

            mod_copies = [0]

            def mod_copy(rows, n=1):
                for _ in range(min(n, MOD_STEPS - mod_copies[0])):
                    mod_copies[0] += 1
                    act.wait_ge(mod_full, mod_copies[0])
                    nc.scalar.activation(rows, mod_bank[:, :].rearrange("p (j n) -> p j n", j=4), ACT.Copy).then_inc(mod_copied, 1)

            tables = [None]

            def log_exp():
                if tables[0] != "log_exp":
                    nc.scalar.preload_act_table_set("natural_log_exp_and_others")
                    tables[0] = "log_exp"

            def silu(dst, src):
                tables[0] = "silu"
                return nc.scalar.activation(dst, src, ACT.Silu)

            def cond_silu():
                act.wait_ge(small_loaded, 16)
                silu(cond[:, :, :], sm("cond", "p (k s) -> p k s", s=2)).then_inc(cond_ready, 1)

            def chunk_high(n, full=None, halves=(0, 1)):
                slot = n % SLOTS
                act.wait_ge(slot_full[slot], 16 * (n // SLOTS + 1) if full is None else full)
                for h in halves:
                    half = slice(h * HALF // 2, (h + 1) * HALF // 2)
                    nc.scalar.activation(ring_high[:, slot, half], ring[:, slot, half], ACT.Copy).then_inc(high_ready, 1)

            def chunks_high(first, n):
                for c in range(n):
                    chunk_high(first + c)

            def out_high(i, u, n_u):
                m = early_half(i, u, n_u)
                if m is not None:
                    chunk_high(STREAM[f"out{i}"][0] + m // 2, halves=(m % 2,))

            def gate_silu(i):
                lo = GATE_AT[i]
                act.wait_ge(a_free, A.drains)
                for t in range(LT):
                    n = silu(zs[i][:, t, lo:lo + D], zs[i][:, t, lo:lo + D])
                n.then_inc(z_act_ready, 1)

            def sum_squares(src, t):
                nc.scalar.activation(scratch[:, :], src[:, t, :], ACT.Square, accum_out=ss[:, t:t + 1]).then_inc(sumsq_ready, 1)
                seen.next(sumsq_ready)

            def normed(t):
                seen.next(scale_ready)
                nc.scalar.activation(mix[:, t, :], x[:, t, :], ACT.Copy, scale=rstd[:, t:t + 1]).then_inc(normed_ready, 1)

            def features(T, scale_bias=None, split=None):
                per = 4 // T
                hT = hT4 if T == 4 else hT2
                for j in range(KT // per):
                    parts = []
                    for n in range(per):
                        for s in range(T // LT):
                            k = j * per + n
                            scale, bias = scale_bias(k, s) if scale_bias else (1.0, None)
                            func = ACT.Copy if bias is None else ACT.Identity
                            bias = 0.0 if bias is None else bias
                            parts.append((k, slice(s * S, (s + 1) * S), n * T * P + s * S, func, scale, bias))
                    b = A.filled_bank(act)
                    if split:
                        split_drains.append(A.drains)
                    for k, at, lo, func, scale, bias in parts:
                        n = nc.scalar.activation(hT[:, k, at], b[:, lo:lo + S], func, scale=scale, bias=bias)
                    n.then_inc(a_free, 1)

            def projected(blocks, first=None, scale=lambda t: 1.0, after=None, between=None):
                n_chunks = sum(w // 256 for _, _, w in blocks)
                start, made = 0, SLOTS
                for n, (dst, T, w) in enumerate(blocks):
                    end = start + w // 256
                    if first is not None and w == 512 and start + SLOTS == made < n_chunks:
                        chunk_high(first + made)
                        made += 1
                    for t in range(T):
                        drain((dst(t), lambda b, w=w: b[:, 0:w], scale(t), None))
                        if after:
                            after(n, t)
                    while first is not None and made < min(end + SLOTS, n_chunks):
                        chunk_high(first + made)
                        made += 1
                    if between:
                        between(n)
                    start = end

            def columns(dst, T, widths):
                at = [sum(widths[:n]) for n in range(len(widths))]
                return [(lambda t, c=c, w=w: dst[:, t, c:c + w], T, w) for c, w in zip(at, widths)]

            def q_features(dst, n_ft, T, scale):
                per = 4 // T
                for j in range(n_ft // per):
                    drain((dst[:, j * per * T * P:(j + 1) * per * T * P], lambda b: b[:, :], scale, None))

            def gate_row_copies(T):
                for s in range(T // LT):
                    for h in range(2):
                        drain((gate_rows[:, s, h * 512:(h + 1) * 512], lambda b: b[:, :], 1.0, None))
                whole["gates", T] = A.drains

            def exp_probs(u, src, dst, n, wait=True):
                return nc.scalar.activation(dst, src, ACT.Exp, bias=nmax[:, n:n + 1], accum_out=sums[:, n:n + 1])

            def pT_out(u, width):
                drain((pT_ring[u % 3][:, 0:width], lambda b, w=width: b[:, 0:w], 1.0, None))

            def experts(i):
                T = NT if i == 0 else LT
                N = T * P
                base = NE * i

                def silu_gate(e, parity, first):
                    for f in range(2):
                        act.wait_ge(g_full, e * 2 + f + 1)
                        if f == 0 and not first:
                            act.wait_ge(u_free, e * 2 - 2)
                        silu(silu_g[parity][:, f, 0:N], bank[f][:, 0:N]).then_inc(g_free, 1)

                first = STREAM[f"experts{i}"][0]
                chunk_high(first + 3)
                silu_gate(base, 0, i == 0)
                chunk_high(first + 4)
                silu_gate(base + 1, 1, i == 0)
                chunk_high(first + 5)
                chunk_high(first + 6)

                def pair(n, ahead, last=False):
                    ahead(7)
                    silu_gate(n * 2 + base, 0, False)
                    ahead(8)
                    ahead(9)
                    ahead(10)
                    silu_gate(n * 2 + (base + 1), 1, False)
                    if not last:
                        ahead(11)
                        ahead(12)

                per = 6 // SLOTS * 16
                with act.Fori(1, NE // 2 - 1) as n:
                    pair(n, lambda c: chunk_high(first + c, n * per + (16 * ((first + c) // SLOTS + 1) - per)))
                pair(NE // 2 - 1, lambda c: chunk_high(first + c + 6 * (NE // 2 - 2)), last=True)
                chunk_high(first + 3 * NE - 1)
                if i + 1 < layers:
                    chunk_high(STREAM[f"in{i + 1}"][0])

            def route_exps(i):
                log_exp()
                for _ in range(2):
                    seen.next(route_in)
                    src = route_buf[0] if _ == 0 else route_buf[1]
                    T = NT if i == 0 else LT
                    nc.scalar.activation(src[:, 0:4 * T], src[:, 0:4 * T], ACT.Exp).then_inc(route_out, 1)

            def modulate(i, which, T, split=None):
                features(T, lambda k, s: (modA[:, i, which, k, s:s + 1], modT[:, 48 * i + 24 * which + k, s:s + 1]), split)

            def first_layer(i):
                T = NT if i == 0 else LT
                for t in range(NT):
                    if i == 0:
                        act.wait_ge(x_loaded, 32)
                    else:
                        seen.next(x_ready)
                    sum_squares(x, t)
                    if t > 0:
                        normed(t - 1)
                normed(NT - 1)
                if i == 0:
                    mod_copy(mod_rows_early, MOD_EARLY)
                    seen.next(mod_ready)
                    chunk_high(STREAM["in0"][0])
                modulate(i, 0, NT, "first")
                chunks_high(STREAM[f"in{i}"][0] + 1, SLOTS - 1)
                if i == 0:
                    projected(columns(zs[0], NT, [512, 512, 512, 512, 256]), STREAM["in0"][0])
                    drain((zs[0][:, :, 2304:2336], lambda b: b[:, 0:NT * 32].rearrange("p (t n) -> p t n", t=NT), 1.0, None))
                else:
                    def after(n, t):
                        if n == 0 and t == NT - 1:
                            whole["k", i] = A.drains
                        if n > 0:
                            whole["q", i, n - 1, t] = A.drains

                    projected([(lambda t: zs[1][:, t, 1024:1280], NT, 256)] + columns(zs[1], LT, [512, 512]), STREAM["in1"][0],
                              after=after)
                whole["z", i] = A.drains
                if i == 0:
                    gla()
                    attention_heads(0)
                else:
                    attention_heads(1)
                features(T, split="first")
                gate_row_copies(T)

                def after(n, t):
                    whole["y", i, n, t] = A.drains
                    if n == 0 and t == T - 1:
                        chunk_high(STREAM[f"experts{i}"][0])
                    if n == 1 and t > 0:
                        seen.next(x_ready)
                        sum_squares(x, t - 1)
                    if n == 1 and t > 1:
                        normed(t - 2)

                projected(columns(zo[T], T, [512, 512]), STREAM[f"out{i}"][0], after=after)
                seen.next(x_ready)
                sum_squares(x, T - 1)
                normed(T - 2)
                normed(T - 1)
                if i == 0:
                    seen.next(mod_ready)
                modulate(i, 1, T, "experts")
                chunk_high(STREAM[f"experts{i}"][0] + 1)
                gate_row_copies(T)
                chunk_high(STREAM[f"experts{i}"][0] + 2)
                whole["gates2", i] = A.drains
                route_exps(i)
                experts(i)

            def gla():
                for dst, scale in ((qT, QSCALE), (kT, 1.0)):
                    for f in range(2):
                        drain((dst[:, f, :], lambda b: b[:, :], scale, None))
                drain((lrT[0:32, :], lambda b: b[0:32, :], 1.0, None))
                mod_copy(mod_rows_late, MOD_GATES)
                seen.next(gate_in)
                log_exp()
                nc.scalar.activation(X[1], X[1], ACT.Exp).then_inc(gate_soft, 1)
                seen.next(gate_soft)
                nc.scalar.activation(X[1], X[1], ACT.Ln, bias=1.0).then_inc(gate_soft, 1)
                mod_copy(mod_rows_late)
                for n in range(len(LEVELS) + 1):
                    seen.next(expo_in)
                    nc.scalar.activation(X[n % 2], X[n % 2], ACT.Exp, scale=1.0 / GLA_GATE_NORM).then_inc(expo_out, 1)
                    if n == 0:
                        mod_copy(mod_rows_late, MOD_START - 1)
                    if n >= 2:
                        mod_copy(mod_rows_late, MOD_LEVEL)
                for d in range(2):
                    drain((kst[:, d].rearrange("p f j k -> p (f j k)"), lambda b: b[:, :], 1.0, None))
                for d in range(2):
                    drain(*[(state[64 * o:64 * o + 64, d].rearrange("p f (o v) -> p f o v", o=2)[:, :, o, :],
                             lambda b, o=o: b[64 * o:64 * o + 64, :].rearrange("p (f o v) -> p f o v", f=2, o=2)[:, :, o, :], 1.0, None)
                            for o in range(2)])
                act.wait_ge(a_free, whole["z", 0])
                for t in range(NT):
                    i = silu(zs[0][:, t, 1024:1536], zs[0][:, t, 1024:1536])
                i.then_inc(z_act_ready, 1)

            def attention_heads(i):
                if i == 0:
                    q_features(aq, 4, NT, QSCALE)
                    for v in range(2):
                        drain((ak[:, v * 512:(v + 1) * 512], lambda b: b[:, :], 1.0, None))
                    for s in range(2):
                        keys = 512 if s == 0 else 256
                        n_u = LT * 8
                        for u in range(n_u + 1):
                            if u < n_u:
                                seen.next(max_ready)
                                b = bank[4 + u % 2]
                                exp_probs(u, b[:, 0:keys], p_ring[u % 3][:, 0:keys], s * 16 + u).then_inc(probs_ready, 1)
                            if u >= 1:
                                pT_out(u - 1, keys)
                            if s == 1:
                                out_high(0, u, n_u)
                else:
                    for v in range(2):
                        drain((ak[:, v * 512:(v + 1) * 512], lambda b: b[:, :], 1.0, None))
                    q_features(aq, 8, LT, QSCALE)
                    n_u = LT * 16
                    for u in range(n_u + 3):
                        if u >= 3:
                            pT_out(u - 3, 512)
                        if u < n_u:
                            seen.next(max_ready)
                            exp_probs(u, s_ring[u % 3][:, 0:512], p_ring[u % 3][:, 0:512], u)
                            nc.scalar.activation(esink[:, u:u + 1], sm("sink")[:, u % 16:u % 16 + 1], ACT.Exp,
                                                 bias=nmax[:, u:u + 1]).then_inc(probs_ready, 1)
                        out_high(1, u, n_u)

            def second_layer(i):
                features(LT, lambda k, s: (sm("norm_pre", "p (l k) -> p l k", l=4)[:, i - 2, k:k + 1], None), "project")
                chunks_high(STREAM[f"in{i}"][0] + 1, SLOTS - 1)
                for t in range(LT):
                    seen.next(x_ready)
                    sum_squares(x, t)
                seen.next(scale_ready)

                def between(n):
                    if n == 1:
                        gate_silu(i)
                        log_exp()
                    if n == HEADS_AFTER[i]:
                        if i == 2:
                            q_features(aq, 8, LT, QSCALE)
                        else:
                            n_ft = 6 if i == 4 else 8
                            q_features(aq, n_ft, LT, QSCALE)
                            q_features(ak, n_ft, LT, 1.0)

                blocks = columns(zs[i], LT, [512] * IN_BLOCKS[i])
                projected(blocks[-2:] + blocks[:-2], STREAM[f"in{i}"][0], lambda t: rstd[:, t:t + 1], between=between)
                if i == 2:
                    drain(*[(zs[2][:, t, 3584:3632], lambda b, t=t: b[:, t * 48:(t + 1) * 48], rstd[:, t:t + 1], None)
                            for t in range(LT)])
                whole["z", i] = A.drains
                {2: sparse, 3: differential, 4: dilated_heads, 5: stick}[i]()
                features(LT, split="project")

                def after(n, t):
                    whole["y", i, n, t] = A.drains
                    act.wait_ge(a_free, A.drains)
                    nc.scalar.activation(scratch[:, 0:512], zo[2][:, t, n * 512:(n + 1) * 512], ACT.Square,
                                         accum_out=ss_half[:, t, n:n + 1]).then_inc(half_squares, 1)
                    seen.next(half_squares)
                    if n == 0 and t == LT - 1 and i + 1 < layers:
                        chunk_high(STREAM[f"in{i + 1}"][0])

                projected(columns(zo[2], LT, [512, 512]), STREAM[f"out{i}"][0], after=after)

            def sparse():
                q_features(ak, 8, LT, 1.0)
                for src in range(2):
                    for j in range(2):
                        dst = pairs[src]
                        drain(*[(dst[lo:lo + 64, 2 * j:2 * j + 2, :],
                                 lambda b, lo=lo, o=o: b[lo:lo + 64, :].rearrange("p (h m o) -> p h m o", h=2, o=2)[:, :, :, o],
                                 1.0, None) for o, lo in ((0, 0), (1, 64))])
                whole["pairs"] = A.drains
                act.wait_ge(a_free, whole["z", 2])
                nc.scalar.activation(gates.rearrange("p (t n) -> p t n", t=LT), zs[2][:, :, 3584:3632], ACT.Exp,
                                     scale=-1.0).then_inc(cmp_out, 1)
                def gelu_exp(src):
                    g = gelu_t[0:60, src * 256:(src + 1) * 256]
                    seen.next(cmp_in)
                    nc.scalar.activation(g, g, ACT.Exp, scale=-1.0).then_inc(cmp_out, 1)

                gelu_exp(0)

                def compressed(u):
                    if u == CMP_GELU:
                        gelu_exp(1)
                    if u == CMP_TURN:
                        for src in range(2):
                            for kt in range(2):
                                b = A.filled_bank(act)
                                if src == 0:
                                    n = nc.scalar.activation(hidT_k[:, kt, :], b[:, 0:60], ACT.Copy)
                                else:
                                    for hk in range(4):
                                        dst = hidT_v[:, kt, hk, :, 0:CMP_N]
                                        n = nc.scalar.activation(dst, b[:, hk * CMP_N:(hk + 1) * CMP_N].unsqueeze(1).broadcast_to([P, 4, CMP_N]), ACT.Copy)
                                n.then_inc(a_free, 1)
                    if u == CMP_KV:
                        drain((kcmpT[:, :], lambda b: b[:, 0:60], 1.0, None))
                        b = A.filled_bank(act)
                        for hk in range(4):
                            for g in range(4):
                                n = nc.scalar.activation(vcmp[32 * g:32 * g + 32, hk, g * 64:(g + 1) * 64],
                                                         b[32 * g:32 * g + 32, hk * 64:(hk + 1) * 64], ACT.Copy)
                        n.then_inc(a_free, 1)
                    if u in CMP_SCORE:
                        seen.next(cmp_in)
                        nc.scalar.activation(cmp_s[:, :], cmp_s[:, :], ACT.Exp).then_inc(cmp_out, 1)
                    if u in CMP_PROBS:
                        drain((cmpT[:, :], lambda b: b[:, :], 1.0, None))
                    if u in CMP_OUT:
                        qt = CMP_OUT.index(u)
                        for half in range(2):
                            drain((cmp_rows[:, qt, half * 512:(half + 1) * 512], lambda b: b[:, :], 1.0, None))
                        whole["cmp", qt] = A.drains

                n_u = LT * 16
                for u in range(n_u + 3):
                    if u >= 3:
                        pT_out(u - 3, 2 * P * ((u - 3) // 16 + 1))
                    if u < n_u:
                        seen.next(max_ready)
                        nk = P * (u // 16 + 1)
                        exp_probs(u, s_ring[u % 3][:, 0:nk], p_ring[u % 3][:, 0:nk], 2 * u)
                        exp_probs(u, s_ring[u % 3][:, nk:2 * nk], p_ring[u % 3][:, nk:2 * nk], 2 * u + 1).then_inc(probs_ready, 1)
                        compressed(u)
                        out_high(2, u, n_u)

            def differential():
                seen.next(cmp_in)
                nc.scalar.activation(lam[:, 2:4], lam[:, 0:2], ACT.Exp).then_inc(cmp_out, 1)
                n_u = LT * 8
                for u in range(n_u + 3):
                    if u >= 3:
                        pT_out(u - 3, P * ((u - 3) // 8 + 1))
                    if u < n_u:
                        seen.next(max_ready)
                        nk = P * (u // 8 + 1)
                        exp_probs(u, s_ring[u % 3][:, 0:nk], p_ring[u % 3][:, 0:nk], 2 * u)
                        exp_probs(u, s_ring[u % 3][:, nk:2 * nk], p_ring[u % 3][:, nk:2 * nk], 2 * u + 1).then_inc(maps_ready, 1)
                        out_high(3, u, n_u)

            def dilated_heads():
                n_u = LT * 4
                for u in range(n_u + 3):
                    if u >= 3:
                        pT_out(u - 3, P * ((u - 3) // 4 + 1))
                    if u < n_u:
                        seen.next(max_ready)
                        nk = P * (u // 4 + 1)
                        exp_probs(u, s_ring[u % 3][:, 0:3 * nk], p_ring[u % 3][:, 0:3 * nk], u).then_inc(maps_ready, 1)
                        out_high(4, u, n_u)

            def stick():
                n_u = LT * 16
                for u in range(n_u + 3):
                    if u >= 3:
                        pT_out(u - 3, P * ((u - 3) // 16 + 1))
                    if u < n_u:
                        nk = P * (u // 16 + 1)
                        mag = s_ring[u % 3][:, 512:512 + nk]
                        seen.next(soft_in)
                        nc.scalar.activation(mag, mag, ACT.Exp).then_inc(soft_out, 1)
                        seen.next(soft_out)
                        nc.scalar.activation(mag, mag, ACT.Ln, bias=1.0).then_inc(soft_out, 1)
                        seen.next(soft_out)
                    if 1 <= u <= n_u:
                        nk = P * ((u - 1) // 16 + 1)
                        seen.next(max_ready)
                        nc.scalar.activation(p_ring[(u - 1) % 3][:, 512:512 + nk], p_ring[(u - 1) % 3][:, 256:256 + nk],
                                             ACT.Exp).then_inc(probs_ready, 1)
                        out_high(5, u - 1, n_u)

            cond_silu()
            for i in range(min(layers, 2)):
                first_layer(i)
            for i in range(2, layers):
                second_layer(i)

        @block.tensor
        def _(pe):
            seen = Seen(pe)
            def chunk():
                n = len(tenancy)
                pe.wait_ge(slot_full[n % SLOTS], 16 * (n // SLOTS + 1))
                tenancy.append([n % SLOTS, None, None])
                return ring[:, n % SLOTS, :]

            splits = [0]

            def split_chunk(rows_per):
                n = len(tenancy)
                splits[0] += 1
                pe.wait_ge(low_ready, 2 * splits[0])
                tenancy.append([n % SLOTS, None, None])
                return [v[:, n % SLOTS, :].rearrange("p (k n) -> p k n", k=rows_per) for v in (ring_high, ring_low)]

            def split_product(out, left, right, start, stop):
                nc.tensor.matmul(out, left[0], right[0], start=start, stop=False)
                nc.tensor.matmul(out, left[0], right[1], start=False, stop=False)
                return nc.tensor.matmul(out, left[1], right[0], start=False, stop=stop)

            half_count = [0]

            def chunk_done(ins):
                half_count[0] += 1
                ins.then_inc(chunk_used, 1)
                tenancy[-1][1:] = [chunk_used, half_count[0]]

            def chunk_done_with(pool):
                tenancy[-1][1:] = [pool.full, pool.fills]

            mod_steps = [0]

            def mod_turn(rows):
                n = mod_steps[0] - 1
                pe.wait_ge(mod_copied, n + 1)
                for j in range(4):
                    m = n * 4 + j
                    i = nc.tensor.matmul(mod_turn_bank[:, 2 * m:2 * m + 2], rows[:, j, :], cn("pick"), start=True, stop=True)
                return i

            def mod_step(rows):
                for kh in range(2):
                    w = chunk().rearrange("p (k n) -> p k n", k=4)
                    if kh == 0 and mod_steps[0] not in (0, MOD_EARLY):
                        mod_turn(rows)
                    for k in range(4):
                        i = nc.tensor.matmul(mod_bank[32 * k:32 * k + 2, :], cond[:, 4 * kh + k, :], w[:, k, :],
                                             start=(kh == 0), stop=(kh == 1), tile_position=(0, 32 * k))
                    if kh == 0:
                        chunk_done(i)
                mod_steps[0] += 1
                i.then_inc(mod_full, 1)
                tenancy[-1][1:] = [mod_full, mod_steps[0]]

            def mod_early():
                pe.wait_ge(mod_cleared, 1)
                for _ in range(MOD_EARLY):
                    mod_step(mod_rows_early)
                mod_turn(mod_rows_early).then_inc(mod_turned, 1)

            def mod_late(n):
                for _ in range(min(n, MOD_STEPS - mod_steps[0])):
                    mod_step(mod_rows_late)

            def transposes(src, T, half_ready=None):
                per = 4 // T
                for j in range(KT // per):
                    if half_ready and j % (KT // per // 2) == 0:
                        half_ready(j // (KT // per // 2))
                    b = A.take(pe)
                    for n in range(per):
                        for t in range(T):
                            i = nc.tensor.transpose(b[:, (n * T + t) * P:(n * T + t + 1) * P],
                                                    src[:, t, (j * per + n) * P:(j * per + n + 1) * P], ident)
                    i.then_inc(a_full, 1)

            def project(name, T, blocks, between=None):
                hT = split_views(name, T)
                low0 = seen.count.get("act_low", 0)
                for n, (tiles, w) in enumerate(blocks):
                    banks = [A.take(pe) for _ in range(tiles)]
                    rows_per = KT // (w // 256)
                    for k0 in range(0, KT, rows_per):
                        last = k0 + rows_per == KT
                        high, low = split_chunk(rows_per)
                        for t in range(tiles):
                            for k in range(rows_per):
                                ready = low0 + (k0 + k) * T // 4 + 1
                                if n == 0 and t == 0 and ready > seen.count.get("act_low", 0):
                                    seen.next(act_low)
                                i = split_product(banks[t][:, 0:w], [v[:, k0 + k, t * P:(t + 1) * P] for v in hT],
                                                  (high[:, k, :], low[:, k, :]), k0 + k == 0, k0 + k == KT - 1)
                            if last:
                                i.then_inc(a_full, 1)
                        if last:
                            chunk_done_with(A)
                        else:
                            chunk_done(i)
                    if between:
                        between(n)

            def project_small(T, w, N):
                hT = hT4 if T == 4 else hT2
                b = A.take(pe)
                for t in range(T):
                    for k in range(KT):
                        i = nc.tensor.matmul(b[:, t * N:(t + 1) * N], hT[:, k, t * P:(t + 1) * P], w[:, k, :],
                                             start=(k == 0), stop=(k == KT - 1))
                i.then_inc(a_full, 1)

            def gate_row_products(i, T, which):
                for s in range(T // LT):
                    for h in range(2):
                        b = A.take(pe)
                        for j in range(4):
                            m = nc.tensor.matmul(b[:, j * P:(j + 1) * P],
                                                 modT[:, 48 * i + which * 8 + h * 4 + j, s:s + 1].broadcast_to([P, P]), ident,
                                                 start=True, stop=True)
                        m.then_inc(a_full, 1)

            def head_features(src, n_ft, T):
                per = 4 // T
                for j in range(n_ft // per):
                    b = A.take(pe)
                    for n in range(per):
                        for t in range(T):
                            i = nc.tensor.transpose(b[:, (n * T + t) * P:(n * T + t + 1) * P], src(t, j * per + n), ident)
                    i.then_inc(a_full, 1)

            def attend(n_u, score, turn, weigh, lag_events, lead=2, between=None):
                pT_at = {}
                for step in range(n_u + lead + 1):
                    if step < n_u:
                        if between:
                            between(step)
                        score(step)
                    if lead <= step < n_u + lead:
                        u = step - lead
                        seen.next(lag_events)
                        b = A.take(pe)
                        turn(u, b).then_inc(a_full, 1)
                        pT_at[u] = A.fills
                    if step > lead:
                        A.drained(pe, pT_at[step - lead - 1])
                        weigh(step - lead - 1)

            def turn_blocks(src, n, b):
                for j in range(n):
                    i = nc.tensor.transpose(b[:, j * P:(j + 1) * P], src[:, j * P:(j + 1) * P], ident)
                return i

            def gla():
                z = zs[0]
                for col in (0, 256):
                    head_features(lambda t, f: z[:, t, col + f * P:col + (f + 1) * P], 2, NT)
                b = A.take(pe)
                for t in range(NT):
                    i = nc.tensor.transpose(b[0:32, t * P:(t + 1) * P], z[:, t, 2304:2336], ident)
                i.then_inc(a_full, 1)
                A.drained(pe)
                seen.next(mod_ready)
                gw = sm("gate_w", "p (d n) -> p d n", d=2)
                for d in range(2):
                    if d == 1:
                        mod_late(MOD_GATES)
                    for f in range(2):
                        b = V.take(pe)
                        nc.tensor.matmul(b[:, :], gw[0:32, d, f * P:(f + 1) * P], lrT[0:32, :], start=True,
                                         stop=True).then_inc(v_full, 1)

                def pair_products(blocks):
                    banks = [G.take(pe) for _ in range(2)]
                    for n, (left, right, keys, queries) in enumerate(blocks):
                        for f in range(2):
                            for odd in range(2):
                                r = slice(64 * odd, 64 * odd + 64)
                                o = (n * 2 + f) * P
                                i = nc.tensor.matmul(banks[odd][:, o:o + P], left(f)[r, keys], right(f)[r, queries],
                                                     start=True, stop=True)
                                if n == 1 and f == 1:
                                    i.then_inc(pairs_full, 1)

                for s in range(2):
                    at = [slice(s * S + j * P, s * S + (j + 1) * P) for j in range(2)]
                    pair_products([(lambda f: kT[:, f, :], lambda f: qT[:, f, :], sl, sl) for sl in at])
                mod_late(MOD_START)
                tile = [slice(0, P), slice(P, S)]
                for n, m in enumerate(LEVELS):
                    seen.next(level_ready)
                    xl = X[n % 2].rearrange("p (d f s t) -> p d f s t", d=2, f=2, s=2)

                    def src(d, s):
                        return lambda f: xl[:, d, f, s, :]

                    if m == P:
                        for s in range(2):
                            pair_products([(src(d, s), src(d, s), tile[d], tile[1 - d]) for d in range(2)])
                        continue
                    for d in range(2):
                        for s in range(2):
                            pair_products([(src(d, s), src(d, s), tile[j], tile[j]) for j in range(2)])
                            if (d, s) != (0, 0):
                                mod_late(1)
                mod_turn(mod_rows_late).then_inc(mod_turned, 1)
                G.drained(pe)
                seen.next(level_ready)
                xi = X[len(LEVELS) % 2].rearrange("p (w f t) -> p w f t", w=4, f=2)
                for d in range(2):
                    b = A.take(pe)
                    for f in range(2):
                        for j in range(2):
                            o = (f * 2 + j) * P
                            i = nc.tensor.transpose(b[:, o:o + P], xi[:, d, f, j * P:(j + 1) * P], ident)
                    i.then_inc(a_full, 1)
                A.drained(pe)
                for d in range(2):
                    b = A.take(pe)
                    for f in range(2):
                        for j in range(2):
                            i = nc.tensor.matmul(b[:, f * 256:(f + 1) * 256], kst[:, d, f, j, :],
                                                 z[:, 2 + j, 512 + f * 256:512 + (f + 1) * 256], start=(j == 0), stop=(j == 1))
                    i.then_inc(a_full, 1)
                A.drained(pe)
                V.drained(pe)
                for s in range(2):
                    for j in range(2):
                        b = V.take(pe)
                        if s == LAT:
                            for f in range(2):
                                for d in range(2):
                                    nc.tensor.matmul(b[:, f * 256:(f + 1) * 256], xi[:, 2 + d, f, j * P:(j + 1) * P], state[:, d, f, :],
                                                     start=(f == 0 and d == 0), stop=False, skip_group_check=True)
                        for h in range(GLA_H):
                            for js in range(2):
                                a = att_same if js == j else att_other
                                i = nc.tensor.matmul(b[:, h * P:(h + 1) * P], a[:, s, js, h, :],
                                                     z[:, 2 * s + js, 512 + h * P:512 + (h + 1) * P],
                                                     start=(s == CTX and h == 0 and js == 0), stop=(js == 1), skip_group_check=True)
                        i.then_inc(v_full, 1)

            def rows_of(h):
                return slice(64 * (h % 2), 64 * (h % 2) + 64)

            def first_attention(i):
                if i == 0:
                    z = zs[0]
                    seen.next(heads_ready)
                    head_features(lambda t, f: z[:, t, 1536 + f * P:1536 + (f + 1) * P], 4, NT)
                    head_features(lambda t, f: mix[:, t, 512 + f * P:512 + (f + 1) * P], 2, NT)
                    A.drained(pe)
                    q4 = aq.rearrange("p (f t) -> p f t", f=4)
                    k4 = ak[:, 0:1024].rearrange("p (v t) -> p v t", v=2)
                    for s in range(2):
                        keys = 512 if s == 0 else 256
                        k0 = 0 if s == 0 else S

                        def score(u):
                            h, qt = u % 8, u // 8
                            b = bank[4 + u % 2]
                            nc.tensor.matmul(b[:, 0:keys], q4[rows_of(h), h // 2, s * S + qt * P:s * S + (qt + 1) * P],
                                             k4[rows_of(h), h // 4, k0:512], start=True, stop=True).then_inc(raw_full, 1)

                        def weigh(u):
                            h = u % 8
                            if h == 0:
                                out_bank[0] = V.take(pe)
                            for j in range(keys // P):
                                t = k0 // P + j
                                m = nc.tensor.matmul(out_bank[0][:, h * HD:(h + 1) * HD], pT_ring[u % 3][:, j * P:(j + 1) * P],
                                                     z[:, t, 2176 + (h // 4) * HD:2176 + (h // 4 + 1) * HD],
                                                     start=(j == 0), stop=(j == keys // P - 1))
                            if h == 7:
                                m.then_inc(v_full, 1)

                        attend(LT * 8, score, lambda u, b: turn_blocks(p_ring[u % 3], keys // P, b), weigh, probs_ready,
                               lead=1)
                else:
                    z = zs[1]
                    seen.next(heads_ready)
                    head_features(lambda t, f: mix[:, t, f * P:(f + 1) * P], 2, NT)
                    for half in range(2):
                        seen.next(heads_ready)
                        head_features(lambda t, f: q_turned[:, t, (4 * half + f) * P:(4 * half + f + 1) * P], 4, LT)
                    A.drained(pe)
                    q8 = aq.rearrange("p (f t) -> p f t", f=8)
                    k4 = ak[:, 0:1024].rearrange("p (v t) -> p v t", v=2)

                    def score(u):
                        h, qt = u % 16, u // 16
                        b = SC.take(pe)
                        nc.tensor.matmul(b[:, :], q8[rows_of(h), h // 2, qt * P:(qt + 1) * P], k4[rows_of(h), h // 8, :],
                                         start=True, stop=True).then_inc(s_full, 1)

                    def weigh(u):
                        h = u % 16
                        if h % 8 == 0:
                            out_bank[0] = V.take(pe)
                        for t in range(NT):
                            m = nc.tensor.matmul(out_bank[0][:, (h % 8) * HD:(h % 8 + 1) * HD], pT_ring[u % 3][:, t * P:(t + 1) * P],
                                                 z[:, t, 1152 + (h // 8) * HD:1152 + (h // 8 + 1) * HD],
                                                 start=(t == 0), stop=(t == NT - 1))
                        if h % 8 == 7:
                            m.then_inc(v_full, 1)

                    attend(LT * 16, score, lambda u, b: turn_blocks(p_ring[u % 3], 4, b), weigh, probs_ready)

            out_bank = [None]

            def router(i, T):
                hT = hT4 if T == 4 else hT2
                w = sm("router_w", "p (l k n) -> p l k n", l=2, k=KT)[:, i]
                b = V.take(pe)
                for t in range(T):
                    for k in range(KT):
                        m = nc.tensor.matmul(b[:, t * 20:(t + 1) * 20], hT[:, k, t * P:(t + 1) * P], w[:, k, :],
                                             start=(k == 0), stop=(k == KT - 1))
                m.then_inc(v_full, 1)

            def experts(i):
                T = NT if i == 0 else LT
                N = T * P
                hT = hT4 if T == 4 else hT2
                base = NE * i
                d_base = 0 if i == 0 else NE * NT * 2
                A.drained(pe)
                SC.drained(pe)
                V.drained(pe)
                half0 = half_count[0]
                first, low0 = len(tenancy), 2 * splits[0]
                moe_at[i] = (first, half0, d_base)
                xT = split_views("experts", T)
                low_seen = seen.count["act_low"]

                def slot(c):
                    return (first + c) % SLOTS

                def parts(c, low, k):
                    pe.wait_ge(low_ready, low)
                    return [v[:, slot(c), :].rearrange("p (k n) -> p k n", k=k) for v in (ring_high, ring_low)]

                def gate_up(e, c, low, start, start_of_layer=False):
                    for kh in range(2):
                        w = parts(c + kh, low(c + kh), 4)
                        for f in range(4):
                            if kh == 0 and not start:
                                pe.wait_ge(g_free if f < 2 else u_free, e * 2 + (f % 2 - 1))
                            for k in range(4):
                                if start_of_layer and f == 0 and low_seen + (4 * kh + k) * T // 4 + 1 > seen.count["act_low"]:
                                    seen.next(act_low)
                                m = split_product(bank[f][:, 0:N], [v[:, k, f * P:(f + 1) * P] for v in w],
                                                  [v[:, 4 * kh + k, :] for v in xT], kh == 0 and k == 0, kh == 1 and k == 3)
                            if kh == 1:
                                m.then_inc(g_full if f < 2 else u_full, 1)
                        if kh == 0:
                            m.then_inc(chunk_used, 1)

                def down(e, n, parity, c, low, start):
                    w = parts(c, low(c), 2)
                    pe.wait_ge(hid_ready, e * 2 + 2)
                    hidden_rows = (hid_high[parity], hid_low[parity])
                    for t in range(T):
                        for h in range(2):
                            b = t * 2 + h
                            if not (start and b < 4):
                                pe.wait_ge(d_free, n + (b - 3))
                            for f in range(2):
                                m = split_product(bank[4 + b % 4][:, :], [v[:, f, t * P:(t + 1) * P] for v in hidden_rows],
                                                  [v[:, f, h * 512:(h + 1) * 512] for v in w], f == 0, f == 1)
                            m.then_inc(d_full, 1)

                def low(c):
                    return low0 + 2 * (c + 1)

                per = 2 * T
                gate_up(base, 0, low, i == 0, True)
                gate_up(base + 1, 2, low, False)
                down(base, d_base, 0, 4, low, True)
                with pe.Fori(1, NE // 2) as j:
                    def low_j(c):
                        return j * 12 + (low(c) - 12)

                    gate_up(j * 2 + base, 5, low_j, False)
                    down(j * 2 + (base - 1), j * (2 * per) + (d_base - per), 1, 7, low_j, False)
                    gate_up(j * 2 + (base + 1), 8, low_j, False)
                    down(j * 2 + base, j * (2 * per) + d_base, 0, 10, low_j, False)
                down(base + NE - 1, d_base + (NE - 1) * per, 1, 3 * NE - 1, low, False)
                splits[0] += 3 * NE
                half_count[0] += NE
                for q in range(3 * NE):
                    tenancy.append([slot(q), d_full, d_base + NE * per])
                pe.wait_ge(g_free, 2 * (base + NE))
                pe.wait_ge(u_free, 2 * (base + NE))
                pe.wait_ge(d_free, d_base + NE * per)

            def first_layer(i):
                T = NT if i == 0 else LT
                if i == 0:
                    mod_early()
                seen.next(normed_ready, NT)
                transposes(mix, NT)
                if i == 0:
                    project("first", NT, [(NT, 512)] * 4 + [(NT, 256)])
                    pe.wait_ge(small_loaded, 32)
                    project_small(NT, sm("lr_w", "p (k n) -> p k n", k=KT), 32)
                    A.drained(pe)
                    gla()
                else:
                    project("first", NT, [(NT, 256)] + [(LT, 512)] * 2)
                    A.drained(pe)
                first_attention(i)
                V.drained(pe)
                transposes(mix, T)
                if i == 0:
                    seen.next(mod_ready)
                gate_row_products(i, T, 2)
                project("first", T, [(T, 512)] * 2)
                seen.next(normed_ready, T)
                transposes(mix, T)
                A.drained(pe)
                router(i, T)
                gate_row_products(i, T, 5)
                experts(i)

            heads_turned = [0]

            def second_layer(i):
                pe.wait_ge(x_ready, 12 + LT * (i - 2))
                transposes(x, LT)

                def between(n):
                    if n == HEADS_AFTER[i]:
                        A.drained(pe, A.fills - LT)
                        n_ft = 6 if i == 4 else 8
                        for at in (0,) if i == 2 else (0, n_ft * P):
                            head_features(lambda t, f: zs[i][:, t, at + f * P:at + (f + 1) * P], n_ft, LT)
                        heads_turned[0] = A.fills

                project("project", LT, [(LT, 512)] * IN_BLOCKS[i], between)
                if i == 2:
                    project_small(LT, sm("gl_w", "p (k n) -> p k n", k=KT), 48)
                    A.drained(pe)
                else:
                    A.drained(pe, heads_turned[0])
                {2: sparse, 3: differential, 4: dilated_heads, 5: stick}[i]()
                if i == 5:
                    transposes(mix, LT, lambda half: V.drained(pe, V.fills - 1 + half))
                else:
                    transposes(mix, LT, lambda half: seen.next(mix_ready))
                project("project", LT, [(LT, 512)] * 2)

            def sparse():
                z = zs[2]
                seen.next(heads_ready)
                kd = kdup.rearrange("p (t f n) -> p t f n", t=LT, f=8)
                head_features(lambda t, f: kd[:, t, f, :], 8, LT)
                cd = cdup
                head_features(lambda t, f: cd[:, t, f * P:(f + 1) * P], 8, LT)
                for src in range(2):
                    b = V.take(pe)
                    seen.next(cmp_blk)
                    for c in range(2):
                        w = chunk().rearrange("p (l n) -> p l n", l=8)
                        for l in range(8):
                            i = nc.tensor.matmul(b[0:60, 0:256], blk[src][:, c * 8 + l, :], w[:, l, :],
                                                 start=(c == 0 and l == 0), stop=(c == 1 and l == 7))
                        if c == 0:
                            chunk_done(i)
                    i.then_inc(v_full, 1)
                    chunk_done_with(V)
                w2k = sm("w2_k", "p (k n) -> p k n", k=2)
                w2v = sm("w2_v", "p (k n) -> p k n", k=2)
                q8 = aq.rearrange("p (f t) -> p f t", f=8)
                fills = {}

                def compressed(u):
                    if u == CMP_TURN:
                        for src in range(2):
                            seen.next(cmp_hid)
                            for kt in range(2):
                                b = A.take(pe)
                                nc.tensor.transpose(b[:, 0:60], hidden[0:60, src * 256 + kt * P:src * 256 + (kt + 1) * P],
                                                    ident[0:60, 0:60]).then_inc(a_full, 1)
                        fills["hidden"] = A.fills
                    if u == CMP_KV:
                        A.drained(pe, fills["hidden"])
                        b = A.take(pe)
                        for kt in range(2):
                            i = nc.tensor.matmul(b[:, 0:60], w2k[:, kt, :], hidT_k[:, kt, :], start=(kt == 0), stop=(kt == 1))
                        i.then_inc(a_full, 1)
                        b = A.take(pe)
                        for hk in range(4):
                            for kt in range(2):
                                i = nc.tensor.matmul(b[:, hk * 64:(hk + 1) * 64], hidT_v[:, kt, hk].rearrange("p g n -> p (g n)"),
                                                     w2v[:, kt, :], start=(kt == 0), stop=(kt == 1))
                        i.then_inc(a_full, 1)
                        fills["kv"] = A.fills
                    if u in CMP_SCORE:
                        qt = CMP_SCORE.index(u)
                        A.drained(pe, fills["kv"])
                        banks = [SC.take(pe) for _ in range(2)]
                        for h in range(16):
                            i = nc.tensor.matmul(banks[h % 2][:, (h // 2) * CMP_N:(h // 2 + 1) * CMP_N],
                                                 q8[rows_of(h), h // 2, qt * P:(qt + 1) * P],
                                                 kcmpT[rows_of(h), (h // 4) * CMP_N:(h // 4 + 1) * CMP_N], start=True, stop=True)
                            if h >= 14:
                                i.then_inc(s_full, 1)
                    if u in CMP_PROBS:
                        seen.next(cmp_probs)
                        b = A.take(pe)
                        for hk in range(4):
                            i = nc.tensor.transpose(b[:, hk * P:(hk + 1) * P], cmp_p[:, hk * P:(hk + 1) * P], ident)
                        i.then_inc(a_full, 1)
                        fills["probs"] = A.fills
                    if u in CMP_OUT:
                        A.drained(pe, fills["probs"])
                        for half in range(2):
                            b = A.take(pe)
                            for hk in range(2):
                                i = nc.tensor.matmul(b[:, hk * 256:(hk + 1) * 256],
                                                     cmpT[:, (2 * half + hk) * P:(2 * half + hk + 1) * P], vcmp[:, 2 * half + hk, :],
                                                     start=True, stop=True)
                            i.then_inc(a_full, 1)

                k8 = ak.rearrange("p (b v t) -> p b v t", b=2, v=4)

                def score(u):
                    h, qt = u % 16, u // 16
                    nk = P * (qt + 1)
                    b = SC.take(pe)
                    for br in range(2):
                        i = nc.tensor.matmul(b[:, br * nk:(br + 1) * nk], q8[rows_of(h), h // 2, qt * P:(qt + 1) * P],
                                             k8[rows_of(h), br, h // 4, 0:nk], start=True, stop=True)
                    i.then_inc(s_full, 1)

                def weigh(u):
                    h, qt = u % 16, u // 16
                    if h % 4 == 0:
                        out_bank[0] = V.take(pe)
                    for br in range(2):
                        for j in range(qt + 1):
                            col = 1792 + 512 * br + (h // 4) * HD
                            o = (h % 4) * P + br * HD
                            m = nc.tensor.matmul(out_bank[0][:, o:o + HD], pT_ring[u % 3][:, (br * (qt + 1) + j) * P:(br * (qt + 1) + j + 1) * P],
                                                 z[:, j, col:col + HD], start=(j == 0), stop=(j == qt))
                    if h % 4 == 3:
                        m.then_inc(v_full, 1)

                attend(LT * 16, score, lambda u, b: turn_blocks(p_ring[u % 3], 2 * (u // 16 + 1), b), weigh, probs_ready,
                       between=compressed)

            def differential():
                z = zs[3]
                q8 = aq.rearrange("p (f t) -> p f t", f=8)
                k8 = ak.rearrange("p (f t) -> p f t", f=8)

                def score(u):
                    h, qt = u % 8, u // 8
                    nk = P * (qt + 1)
                    for m in range(2):
                        b = SC.take(pe)
                        nc.tensor.matmul(b[:, 0:nk], q8[rows_of(m), h, qt * P:(qt + 1) * P],
                                         k8[rows_of(m), h, 0:nk], start=True, stop=True).then_inc(s_full, 1)

                def weigh(u):
                    h, qt = u % 8, u // 8
                    if h % 4 == 0:
                        out_bank[0] = V.take(pe)
                    for j in range(qt + 1):
                        m = nc.tensor.matmul(out_bank[0][:, (h % 4) * P:(h % 4 + 1) * P], pT_ring[u % 3][:, j * P:(j + 1) * P],
                                             z[:, j, 2048 + h * P:2048 + (h + 1) * P], start=(j == 0), stop=(j == qt))
                    if h % 4 == 3:
                        m.then_inc(v_full, 1)

                attend(LT * 8, score, lambda u, b: turn_blocks(p_ring[u % 3], u // 8 + 1, b), weigh, probs_mixed)

            def dilated_heads():
                z = zs[4]
                q6 = aq[:, 0:1536].rearrange("p (f t) -> p f t", f=6)
                k6 = ak[:, 0:1536].rearrange("p (f t) -> p f t", f=6)

                def score(u):
                    h, qt = u % 4, u // 4
                    nk = P * (qt + 1)
                    for part in ((0, 1), (2,)):
                        b = SC.take(pe)
                        for n, g in enumerate(part):
                            hh = g * 4 + h
                            i = nc.tensor.matmul(b[:, n * nk:(n + 1) * nk], q6[rows_of(hh), hh // 2, qt * P:(qt + 1) * P],
                                                 k6[rows_of(hh), hh // 2, 0:nk], start=True, stop=True)
                        i.then_inc(s_full, 1)

                def weigh(u):
                    h, qt = u % 4, u // 4
                    if h % 2 == 0:
                        out_bank[0] = V.take(pe)
                    for j in range(qt + 1):
                        m = nc.tensor.matmul(out_bank[0][:, (h % 2) * 256:(h % 2 + 1) * 256], pT_ring[u % 3][:, j * P:(j + 1) * P],
                                             z[:, j, 1536 + h * 256:1536 + (h + 1) * 256], start=(j == 0), stop=(j == qt))
                    if h % 2 == 1:
                        m.then_inc(v_full, 1)

                attend(LT * 4, score, lambda u, b: turn_blocks(p_ring[u % 3], u // 4 + 1, b), weigh, probs_mixed)

            def stick():
                z = zs[5]
                q8 = aq.rearrange("p (f t) -> p f t", f=8)
                k8 = ak.rearrange("p (f t) -> p f t", f=8)

                def score(u):
                    h, qt = u % 16, u // 16
                    nk = P * (qt + 1)
                    b = SC.take(pe)
                    nc.tensor.matmul(b[:, 0:nk], q8[rows_of(h), h // 2, qt * P:(qt + 1) * P], k8[rows_of(h), h // 2, 0:nk],
                                     start=True, stop=True).then_inc(s_full, 1)

                def weigh(u):
                    h, qt = u % 16, u // 16
                    if h % 8 == 0:
                        out_bank[0] = V.take(pe)
                    for j in range(qt + 1):
                        m = nc.tensor.matmul(out_bank[0][:, (h % 8) * HD:(h % 8 + 1) * HD], pT_ring[u % 3][:, j * P:(j + 1) * P],
                                             z[:, j, 2048 + h * HD:2048 + (h + 1) * HD], start=(j == 0), stop=(j == qt))
                    if h % 8 == 7:
                        m.then_inc(v_full, 1)

                attend(LT * 16, score, lambda u, b: turn_blocks(p_ring[u % 3][:, 512:], u // 16 + 1, b), weigh, probs_ready)

            pe.wait_ge(const_loaded, 16)
            pe.wait_ge(small_loaded, 16)
            seen.next(cond_ready)
            for i in range(min(layers, 2)):
                first_layer(i)
            for i in range(2, layers):
                second_layer(i)

        @block.vector
        def _(dve):
            seen = Seen(dve)
            own = {}
            ve = nc.vector

            def signal(ins, semaphore):
                ins.then_inc(semaphore, 1)
                own[semaphore.name] = own.get(semaphore.name, 0) + 1
                return own[semaphore.name]

            def then(ins, semaphore=dve_step):
                dve.wait_ge(semaphore, signal(ins, semaphore))

            def vbank():
                return V.filled_bank(dve)

            def over(v, n):
                return v.unsqueeze(2).broadcast_to([P, v.shape[1], n])

            def under(v, n):
                return v.unsqueeze(1).broadcast_to([P, n, v.shape[1]])

            def inv_root():
                seen.next(rstd_ready)

            splits = [0]

            def chunk_low(n, ready=None, halves=(0, 1)):
                slot = n % SLOTS
                if ready is None:
                    if 0 in halves:
                        splits[0] += 1
                    ready = 2 * splits[0]
                for h in halves:
                    half = slice(h * HALF // 2, (h + 1) * HALF // 2)
                    dve.wait_ge(high_ready, ready + (h - 1))
                    ve.tensor_tensor(ring_low[:, slot, half], ring[:, slot, half], ring_high[:, slot, half],
                                     ALU.subtract).then_inc(low_ready, 1)

            def chunks_low(first, n):
                for c in range(n):
                    chunk_low(first + c)

            def out_low(i, u, n_u):
                m = early_half(i, u - 3, n_u)
                if m is not None:
                    chunk_low(STREAM[f"out{i}"][0] + m // 2, halves=(m % 2,))

            features_split = [0]

            def features_low(name, T):
                per = 4 // T
                high, low = split_views(name, T)
                hT = hT4 if T == 4 else hT2
                for j in range(KT // per + 1):
                    if j < KT // per:
                        ks = slice(j * per, (j + 1) * per)
                        dve.wait_ge(a_free, split_drains[features_split[0]])
                        features_split[0] += 1
                        n = signal(ve.tensor_copy(high[:, ks, :], hT[:, ks, :]), act_high)
                    if j:
                        ks = slice((j - 1) * per, j * per)
                        dve.wait_ge(act_high, n - (j < KT // per))
                        signal(ve.tensor_tensor(low[:, ks, :], hT[:, ks, :], high[:, ks, :], ALU.subtract), act_low)

            def modulation(lo, hi, scaled):
                seen.next(mod_turned)
                then(ve.tensor_tensor(modT[:, lo:hi, :], mod_turn_bank[:, 2 * lo:2 * hi].rearrange("p (m s) -> p m s", s=2),
                                      over(sm("mod_b")[:, lo:hi], 2), ALU.add))
                for i, which in scaled:
                    col = 48 * i + (8, 32)[which]
                    gain = sm(("norm_mix", "norm_ffn")[which])[:, i * KT:(i + 1) * KT]
                    n = ve.scalar_tensor_tensor(modA[:, i, which], modT[:, col:col + 8, :], 1.0, over(gain, 2), ALU.add, ALU.mult)
                signal(n, mod_ready)

            def head_squares(src, H, d, at, last=False):
                then(ve.tensor_tensor(scratch2[:, 0:H * d], src, src, ALU.mult))
                then(ve.tensor_reduce(head_ss[:, at:at + H], scratch2[:, 0:H * d].rearrange("p (h d) -> p h d", h=H), AX.X, ALU.add),
                     sums_ready if last else dve_step)

            def scale_heads(src, H, d, at):
                v = src.rearrange("p (h d) -> p h d", h=H)
                then(ve.tensor_tensor(v, v, over(head_rstd[:, at:at + H], d), ALU.mult))

            def gain_heads(src, H, gain):
                v = src.rearrange("p (h d) -> p h d", h=H)
                then(ve.tensor_tensor(v, v, under(gain, H), ALU.mult))

            def rotate(src, H, t, turned):
                v = src.rearrange("p (h a b f) -> p h a b f", h=H, a=2, b=2)
                c, s = (rope[:, t, n].unsqueeze(1).broadcast_to([P, H, 2, 16]) for n in range(2))
                x1, x2 = v[:, :, :, 0, :], v[:, :, :, 1, :]
                tmp = [turned[:, n, 0:H * 32].rearrange("p (h a f) -> p h a f", h=H, a=2) for n in range(4)]
                for n, (half, by) in enumerate(((x1, c), (x2, s), (x2, c), (x1, s))):
                    m = ve.tensor_tensor(tmp[n], half, by, ALU.mult)
                then(m)
                ve.tensor_tensor(x1, tmp[0], tmp[1], ALU.subtract)
                then(ve.tensor_tensor(x2, tmp[2], tmp[3], ALU.add))

            def twice(dst, src, H):
                return ve.tensor_copy(dst.rearrange("p (h two d) -> p h two d", h=H, two=2),
                                      src.rearrange("p (h d) -> p h d", h=H).unsqueeze(2).broadcast_to([P, H, 2, HD]))

            def heads_first_squares(t):
                head_squares(zs[0][:, t, 1536:2176], 10, HD, 10 * t, t == NT - 1)

            def heads_first(t):
                z = zs[0]
                if t == 0:
                    inv_root()
                scale_heads(z[:, t, 1536:2176], 10, HD, 10 * t)
                gain_heads(z[:, t, 1536:2048], 8, sm("att_q"))
                gain_heads(z[:, t, 2048:2176], 2, sm("att_k"))
                if t < LT:
                    rotate(z[:, t, 1536:2176], 10, t, mix[:, :, 0:512])
                n = twice(mix[:, t, 512:768], z[:, t, 2048:2176], 2)
                if t == NT - 1:
                    signal(n, heads_ready)

            def heads_second(first):
                z = zs[1]
                turned = Z[:, NT * 1280:NT * 1280 + 1024].rearrange("p (n m) -> p n m", n=4)
                gain = sm("swa_q", "p (a b f) -> p a b f", a=2, b=2)
                for t in range(LT):
                    for n, (half, by) in enumerate(((0, 0), (1, 1), (1, 0), (0, 1))):
                        m = ve.tensor_tensor(q_tables[:, t, n], rope[:, t, by], gain[:, :, half, :], ALU.mult)
                then(m)
                dve.wait_ge(a_free, whole["k", 1])
                for t in range(NT):
                    head_squares(z[:, t, 1024:1152], 2, HD, 2 * t, t == NT - 1)
                chunk_low(first + SLOTS)
                inv_root()
                for t in range(NT):
                    k = z[:, t, 1024:1152]
                    scale_heads(k, 2, HD, 2 * t)
                    gain_heads(k, 2, sm("swa_k"))
                    if t < LT:
                        rotate(k, 2, t, turned)
                    n = twice(mix[:, t, 0:256], k, 2)
                signal(n, heads_ready)
                chunk_low(first + SLOTS + 1)
                for half in range(2):
                    at = slice(512 * half, 512 * (half + 1))
                    for t in range(LT):
                        dve.wait_ge(a_free, whole["q", 1, half, t])
                        src, dst = (v[:, t, at].rearrange("p (h a b f) -> p h a b f", h=8, a=2, b=2) for v in (z, q_turned))
                        tmp = [turned[:, n, :].rearrange("p (h a f) -> p h a f", h=8, a=2) for n in range(4)]
                        for n, b in enumerate((0, 1, 1, 0)):
                            m = ve.tensor_tensor(tmp[n], src[:, :, :, b, :],
                                                 q_tables[:, t, n].unsqueeze(1).broadcast_to([P, 8, 2, 16]), ALU.mult)
                        then(m)
                        ve.tensor_tensor(dst[:, :, :, 0, :], tmp[0], tmp[1], ALU.subtract)
                        m = ve.tensor_tensor(dst[:, :, :, 1, :], tmp[2], tmp[3], ALU.add)
                        dve.wait_ge(heads_ready if t == LT - 1 else dve_step, signal(m, heads_ready if t == LT - 1 else dve_step))
                    for t in range(LT):
                        head_squares(z[:, t, at], 8, HD, Q_ROOTS + 16 * half + 8 * t, t == LT - 1)

            def gla():
                dve.wait_ge(small_loaded, 32)
                for d in range(2):
                    for f in range(2):
                        b = vbank()
                        at = slice((2 * d + f) * 512, (2 * d + f + 1) * 512)
                        bias = sm("gate_b")[:, 2 * d + f:2 * d + f + 1]
                        ve.tensor_scalar(X[0][:, at], b[:, :], bias, 0.0, ALU.add, ALU.min)
                        then(ve.tensor_scalar(X[1][:, at], b[:, :], bias, None, ALU.add), v_free)
                        ve.scalar_tensor_tensor(X[1][:, at], X[0][:, at], 2.0, X[1][:, at], ALU.mult, ALU.subtract)
                signal(ve.memset(cum[:, :, :, :, 0:1].rearrange("p d f s t -> p (d f s) t"), 0.0), gate_in)
                ve.memset(rows[:, 1024:2048], 0.0)
                dve.wait_ge(gate_in, own["gate_in"])
                seen.next(gate_soft, 2)
                for d in range(2):
                    for f in range(2):
                        for s in range(2):
                            lo = (2 * d + f) * 512 + s * S
                            n = ve.tensor_tensor_scan(cum[:, d, f, s, 1:S + 1], X[0][:, lo:lo + S], X[1][:, lo:lo + S], 0.0,
                                                      ALU.add, ALU.subtract)
                then(n)

                def halves(v, m):
                    w = v.rearrange("p g (b two m) -> p g b two m", two=2, m=m)
                    return w[:, :, :, 0, :], w[:, :, :, 1, :]

                def exponents(n):
                    m = LEVELS[n]
                    xl = X[n % 2].rearrange("p (d g t) -> p d g t", d=2, g=4)
                    for d in range(2):
                        c = cum[:, d].rearrange("p f s t -> p (f s) t")
                        mid = c[:, :, m:S + 1:2 * m]
                        mid = mid.unsqueeze(3).broadcast_to([P, 4, S // (2 * m), m])
                        el, er = halves(c[:, :, 1 - d:S + 1 - d], m)
                        ol, orr = halves(xl[:, d], m)
                        ve.tensor_tensor(ol, mid, el, ALU.subtract)
                        i = ve.tensor_tensor(orr, er, mid, ALU.subtract)
                    signal(i, expo_in)

                def decayed(n):
                    m = LEVELS[n]
                    xl = X[n % 2].rearrange("p (d g t) -> p d g t", d=2, g=4)
                    q, k = (v.rearrange("p f (s t) -> p (f s) t", s=2) for v in (qT, kT))
                    seen.next(expo_out)
                    for d in range(2):
                        ol, orr = halves(xl[:, d], m)
                        left, right = (k, q) if d == 0 else (q, k)
                        ve.tensor_tensor(ol, ol, halves(left, m)[0], ALU.mult)
                        i = ve.tensor_tensor(orr, orr, halves(right, m)[1], ALU.mult)
                    signal(i, level_ready)

                def quads(v):
                    return v.rearrange("p (j h t) -> p j h t", j=2, h=2)

                def take_pairs(n, d):
                    for s in range(2):
                        for odd in range(2):
                            b = G.filled_bank(dve)
                            if n == 0:
                                signal(ve.tensor_copy(att_other[:, s, :, odd::2, :], quads(b[:, :])), pairs_free)
                            else:
                                mask = gla_masks[:, d, n - 1].unsqueeze(1).unsqueeze(1).broadcast_to([P, 2, 2, P])
                                signal(ve.copy_predicated(att_same[:, s, :, odd::2, :], mask, quads(b[:, :])), pairs_free)

                dve.wait_ge(masks_loaded, 16)
                dve.wait_ge(a_free, whole["z", 0])
                exponents(0)
                for s in range(2):
                    for odd in range(2):
                        b = G.filled_bank(dve)
                        signal(ve.tensor_tensor(att_same[:, s, :, odd::2, :], quads(b[:, :]),
                                                cn("diag2").unsqueeze(1).unsqueeze(1).broadcast_to([P, 2, 2, P]), ALU.mult), pairs_free)
                dve.wait_ge(pairs_free, own["pairs_free"])
                decayed(0)
                for n in range(len(LEVELS)):
                    if n + 1 < len(LEVELS):
                        exponents(n + 1)
                    else:
                        xi = X[len(LEVELS) % 2].rearrange("p (w f t) -> p w f t", w=4, f=2)
                        for w, (d, s) in enumerate(((0, CTX), (1, CTX), (0, LAT), (1, LAT))):
                            c = cum[:, d, :, s, :]
                            el = c[:, :, 1 - d:S + 1 - d]
                            if w in (0, 3):
                                i = ve.tensor_tensor(xi[:, w], c[:, :, S:S + 1].broadcast_to([P, 2, S]), el, ALU.subtract)
                            else:
                                i = ve.tensor_copy(xi[:, w], el)
                        signal(i, expo_in)
                    take_pairs(n, 0)
                    if n + 1 < len(LEVELS):
                        decayed(n + 1)
                    if n > 0:
                        take_pairs(n, 1)
                    if n < NT:
                        heads_first_squares(n)
                    else:
                        heads_first(n - NT)
                seen.next(expo_out)
                for w in range(4):
                    by = kT[:, :, S:2 * S] if w < 2 else qT[:, :, 0:S]
                    i = ve.tensor_tensor(xi[:, w], xi[:, w], by, ALU.mult)
                signal(i, level_ready)
                signal(ve.memset(head_ss[:, 0:1], 0.0), gla_done)
                modulation(4 * MOD_EARLY, 4 * MOD_STEPS, [(0, 1), (1, 0), (1, 1)])
                for t in range(NT):
                    b = vbank()
                    then(ve.tensor_copy(mix[:, t, 0:512], b[:, :]), v_free)
                    head_squares(mix[:, t, 0:512], 4, GLA_DV, 4 * t, t == NT - 1)

            def gla_output(t):
                if t == 0:
                    inv_root()
                    seen.next(z_act_ready)
                scale_heads(mix[:, t, 0:512], 4, GLA_DV, 4 * t)
                gain_heads(mix[:, t, 0:512], 4, sm("gla_norm"))
                then(ve.tensor_tensor(mix[:, t, 0:512], mix[:, t, 0:512], zs[0][:, t, 1024:1536], ALU.mult))

            def attention_first():
                for s in range(2):
                    keys = 512 if s == 0 else 256

                    def out(u):
                        qt = u // 8
                        b = vbank()
                        at = s * 16 + qt * 8
                        then(ve.reciprocal(rsum[:, 0:8], sums[:, at:at + 8]))
                        signal(ve.tensor_tensor(mix[:, 2 * s + qt, 512:1024].rearrange("p (h d) -> p h d", h=8),
                                                b[:, :].rearrange("p (h d) -> p h d", h=8), over(rsum[:, 0:8], HD), ALU.mult), v_free)

                    for u in range(LT * 8 + 3):
                        if u < LT * 8:
                            seen.next(raw_full)
                            signal(ve.tensor_reduce(nmax[:, s * 16 + u:s * 16 + u + 1], bank[4 + u % 2][:, 0:keys], AX.X, ALU.max,
                                                    negate=True), max_ready)
                        if s == 0 and u % 3 == 1 and u // 3 < NT:
                            gla_output(u // 3)
                        if s == 1:
                            out_low(0, u, LT * 8)
                        if u >= 3 and (u - 3) % 8 == 7:
                            out(u - 3)
                seen.next(probs_ready, 32)

            def reuse(u):
                if u >= 3:
                    seen.next(probs_ready)

            def attention_second():
                dve.wait_ge(late_loaded, 16)
                then(ve.tensor_scalar(neg_sink, sm("sink"), -1.0, None, ALU.mult))

                def out(u):
                    b = vbank()
                    at = u - 7
                    then(ve.tensor_tensor(rsum[:, 0:8], sums[:, at:at + 8], esink[:, at:at + 8], ALU.add))
                    then(ve.reciprocal(rsum[:, 0:8], rsum[:, 0:8]))
                    c = (at % 16) * HD
                    signal(ve.tensor_tensor(mix[:, at // 16, c:c + 512].rearrange("p (h d) -> p h d", h=8),
                                            b[:, :].rearrange("p (h d) -> p h d", h=8), over(rsum[:, 0:8], HD), ALU.mult), v_free)

                n_u = LT * 16
                for u in range(n_u + 5):
                    if u < n_u:
                        reuse(u)
                        if u in (0, 8):
                            inv_root()
                        root = Q_ROOTS + 16 * (u % 16 // 8) + 8 * (u // 16) + u % 8
                        b = SC.filled_bank(dve)
                        then(ve.scalar_tensor_tensor(s_ring[u % 3][:, 0:512], b[:, :], head_rstd[:, root:root + 1], band[:, u // 16, :],
                                                     ALU.mult, ALU.add), s_free)
                        then(ve.tensor_reduce(lam[:, 0:1], s_ring[u % 3][:, 0:512], AX.X, ALU.max, negate=True))
                        signal(ve.tensor_tensor(nmax[:, u:u + 1], lam[:, 0:1], neg_sink[:, u % 16:u % 16 + 1], ALU.min), max_ready)
                    out_low(1, u, n_u)
                    if u >= 5 and (u - 5) % 8 == 7:
                        out(u - 5)
                seen.next(probs_ready, 3)

            def residual_mix(i, T):
                for n in range(2):
                    half = slice(n * 512, (n + 1) * 512)
                    for t in range(T):
                        dve.wait_ge(a_free, whole["y", i, n, t])
                        y = zo[T][:, t, half]
                        then(ve.tensor_tensor(y, y, gate_rows[:, t // LT, half], ALU.mult))
                        m = ve.tensor_tensor(x[:, t, half], x[:, t, half], y, ALU.add)
                        if n == 1:
                            signal(m, x_ready)
                    if n == 0:
                        chunk_low(STREAM[f"experts{i}"][0])
                dve.wait_ge(x_ready, own["x_ready"])

            def routing(i, T):
                L = route[:, 0:20 * T].rearrange("p (t n) -> p t n", t=T)
                gl, el = L[:, :, 0:4], L[:, :, 4:20]
                at = [96]

                def buf(*shape):
                    n = int(np.prod(shape))
                    v = route[:, at[0]:at[0] + n]
                    at[0] += n
                    if len(shape) == 2:
                        return v.rearrange("p (a b) -> p a b", a=shape[0])
                    if len(shape) == 3:
                        return v.rearrange("p (a b c) -> p a b c", a=shape[0], b=shape[1])
                    return v

                b = vbank()
                bias = sm("router_b")[:, 20 * i:20 * i + 20]
                then(ve.tensor_tensor(L, b[:, 0:20 * T].rearrange("p (t n) -> p t n", t=T), under(bias, T), ALU.add), v_free)
                g_max, taken, total, g_weight, e_max = (buf(T) for _ in range(5))
                is_max, chosen, prob, rank, weight = (buf(T, 4) for _ in range(5))
                picked = buf(T, 4, 4)
                before = buf(T, 4, 4)
                ge, ee = (v[:, 0:4 * T].rearrange("p (t n) -> p t n", t=T) for v in route_buf)
                then(ve.tensor_reduce(g_max, gl, AX.X, ALU.max))
                signal(ve.tensor_tensor(ge, gl, over(g_max, 4), ALU.subtract), route_in)
                then(ve.tensor_tensor(is_max, gl, over(g_max, 4), ALU.is_equal))
                then(ve.memset(taken, 0.0))
                for g in range(4):
                    then(ve.tensor_tensor(chosen[:, :, g], is_max[:, :, g], taken, ALU.is_gt))
                    then(ve.tensor_tensor(taken, taken, is_max[:, :, g], ALU.max))
                then(ve.tensor_tensor(picked, el.rearrange("p t (g e) -> p t g e", g=4),
                                      chosen.unsqueeze(3).broadcast_to([P, T, 4, 4]), ALU.mult))
                then(ve.tensor_reduce(weight, picked.rearrange("p t g e -> p t e g"), AX.X, ALU.add))
                then(ve.tensor_reduce(e_max, weight, AX.X, ALU.max))
                signal(ve.tensor_tensor(ee, weight, over(e_max, 4), ALU.subtract), route_in)
                yield
                seen.next(route_out)
                then(ve.tensor_reduce(total, ge, AX.X, ALU.add))
                then(ve.reciprocal(g_weight, total))
                then(ve.memset(before, 0.0))
                seen.next(route_out)
                then(ve.tensor_reduce(total, ee, AX.X, ALU.add))
                then(ve.reciprocal(total, total))
                then(ve.tensor_tensor(prob, ee, over(total, 4), ALU.mult))
                for e in range(4):
                    mine = prob[:, :, e:e + 1]
                    if e:
                        n = ve.tensor_tensor(before[:, :, e, 0:e], prob[:, :, 0:e], mine.broadcast_to([P, T, e]), ALU.is_ge)
                    if e < 3:
                        n = ve.tensor_tensor(before[:, :, e, e + 1:4], prob[:, :, e + 1:4], mine.broadcast_to([P, T, 3 - e]), ALU.is_gt)
                then(n)
                then(ve.tensor_reduce(rank, before, AX.X, ALU.add))
                then(ve.tensor_scalar(rank, rank, 2.0, None, ALU.is_lt))
                then(ve.tensor_tensor(weight, prob, rank, ALU.mult))
                then(ve.tensor_reduce(total, weight, AX.X, ALU.add))
                then(ve.reciprocal(total, total))
                then(ve.tensor_tensor(total, total, g_weight, ALU.mult))
                then(ve.tensor_tensor(weight, weight, over(total, 4), ALU.mult))
                then(ve.tensor_tensor(comb[:, :, 0:T].rearrange("p (g e) t -> p t g e", g=4),
                                      chosen.unsqueeze(3).broadcast_to([P, T, 4, 4]),
                                      weight.unsqueeze(2).broadcast_to([P, T, 4, 4]), ALU.mult))
                yield

            def experts(i, route_parts):
                T = NT if i == 0 else LT
                N = T * P
                base, per = NE * i, 2 * T
                d_base = 0 if i == 0 else NE * NT * 2
                comb_flat = comb.rearrange("p e t -> p (e t)")

                def gate(e, parity):
                    for f in range(2):
                        dve.wait_ge(g_free, e * 2 + (f + 1))
                        dve.wait_ge(u_full, e * 2 + (f + 1))
                        ve.tensor_tensor(hid[parity][:, f, 0:N], silu_g[parity][:, f, 0:N], bank[2 + f][:, 0:N],
                                         ALU.mult).then_inc(u_free, 1)
                    for f in range(2):
                        dve.wait_ge(u_free, e * 2 + (f + 1))
                        ve.tensor_copy(hid_high[parity][:, f, 0:N], hid[parity][:, f, 0:N]).then_inc(hid_high_ready, 1)
                    for f in range(2):
                        dve.wait_ge(hid_high_ready, e * 2 + (f + 1))
                        ve.tensor_tensor(hid_low[parity][:, f, 0:N], hid[parity][:, f, 0:N], hid_high[parity][:, f, 0:N],
                                         ALU.subtract).then_inc(hid_ready, 1)

                def add(e, n, first):
                    for c in range(2 * T):
                        t, half = down_half(c)
                        dst = mix[:, t, half]
                        w = comb_flat[:, e * 4 + t:e * 4 + t + 1] if isinstance(e, int) else comb_flat[:, bass.ds(e * 4 + t, 1)]
                        dve.wait_ge(d_full, n + (c + 1))
                        src = bank[4 + c % 4][:, :]
                        if first:
                            ve.tensor_scalar(dst, src, w, None, ALU.mult).then_inc(d_free, 1)
                        else:
                            dve.wait_ge(d_free, n + (c + 1 - per))
                            ve.scalar_tensor_tensor(dst, src, w, dst, ALU.mult, ALU.add).then_inc(d_free, 1)

                def add_last(n):
                    for c in range(2 * T):
                        t, half = down_half(c)
                        seen.next(sum_added)
                        dve.wait_ge(d_full, n + (c + 1))
                        w = comb_flat[:, (NE - 1) * 4 + t:(NE - 1) * 4 + t + 1]
                        ve.scalar_tensor_tensor(mix[:, t, half], bank[4 + c % 4][:, :], w, gate_rows[:, t // LT, half],
                                                ALU.mult, ALU.mult).then_inc(d_free, 1)
                        dve.wait_ge(d_free, n + (c + 1))
                        m = ve.tensor_tensor(x[:, t, half], x[:, t, half], mix[:, t, half], ALU.add)
                        if c % 2:
                            signal(m, x_ready)

                first = STREAM[f"experts{i}"][0]
                next(route_parts)
                chunk_low(first + 3)
                gate(base, 0)
                chunk_low(first + 4)
                next(route_parts)
                gate(base + 1, 1)
                chunk_low(first + 5)
                add(0, d_base, True)
                chunk_low(first + 6)
                low0 = 2 * splits[0]

                def pair(j, ahead, last=False):
                    ahead(7)
                    gate(j * 2 + base, 0)
                    ahead(8)
                    add(j * 2 - 1, j * (2 * per) + (d_base - per), False)
                    ahead(9)
                    ahead(10)
                    gate(j * 2 + (base + 1), 1)
                    if not last:
                        ahead(11)
                    add(j * 2, j * (2 * per) + d_base, False)
                    if not last:
                        ahead(12)

                with dve.Fori(1, NE // 2 - 1) as j:
                    pair(j, lambda c: chunk_low(first + c, j * 12 + (low0 + 2 * (c - 6) - 12)))
                splits[0] += 6 * (NE // 2 - 2)
                pair(NE // 2 - 1, lambda c: chunk_low(first + c + 6 * (NE // 2 - 2)), last=True)
                chunk_low(first + 3 * NE - 1)
                if i + 1 < layers:
                    chunk_low(STREAM[f"in{i + 1}"][0])
                add_last(d_base + (NE - 1) * per)
                dve.wait_ge(x_ready, own["x_ready"])

            def first_layer(i):
                T = NT if i == 0 else LT
                if i == 0:
                    modulation(0, 4 * MOD_EARLY, [(0, 0)])
                first = STREAM[f"in{i}"][0]
                if i == 0:
                    chunk_low(first)
                features_low("first", NT)
                chunks_low(first + 1, SLOTS - 1)
                if i == 0:
                    chunks_low(first + SLOTS, 9 - SLOTS)
                    gla()
                    attention_first()
                else:
                    heads_second(first)
                    attention_second()
                features_low("first", T)
                chunks_low(STREAM[f"out{i}"][0] + SLOTS, 4 - SLOTS)
                residual_mix(i, T)
                features_low("experts", T)
                chunks_low(STREAM[f"experts{i}"][0] + 1, SLOTS - 1)
                experts(i, routing(i, T))

            def second_layer(i):
                features_low("project", LT)
                chunks_low(STREAM[f"in{i}"][0] + 1, 2 * IN_BLOCKS[i] - 1)
                if i == 2:
                    dve.wait_ge(a_free, whole["z", i])
                {2: sparse, 3: differential, 4: dilated_heads, 5: stick}[i]()
                features_low("project", LT)
                chunks_low(STREAM[f"out{i}"][0] + SLOTS, 4 - SLOTS)
                dve.wait_ge(post_loaded, 16 * (i - 1))
                y = mix[:, 0:LT, :]
                for n in range(2):
                    half = slice(n * 512, (n + 1) * 512)
                    for t in range(LT):
                        dve.wait_ge(a_free, whole["y", i, n, t])
                        m = signal(ve.tensor_tensor(y[:, t, half], zo[LT][:, t, half], post_row[:, half], ALU.mult), dve_step)
                        if n == 1:
                            inv_root()
                            dve.wait_ge(dve_step, m)
                            signal(ve.scalar_tensor_tensor(x[:, t, :], y[:, t, :], rstd[:, t:t + 1], x[:, t, :], ALU.mult, ALU.add), x_ready)
                    if n == 0 and i + 1 < layers:
                        chunk_low(STREAM[f"in{i + 1}"][0])
                dve.wait_ge(x_ready, own["x_ready"])

            def gate(i, t, c, width, last):
                at = slice(c, c + width)
                z = zs[i][:, t, GATE_AT[i] + c:GATE_AT[i] + c + width]
                signal(ve.tensor_tensor(mix[:, t, at], mix[:, t, at], z, ALU.mult), mix_ready if last else dve_step)

            def biased(u, bias, slope, maps, split=False):
                nk = bias.shape[1]
                dst = s_ring[u % 3][:, 0:maps * nk].rearrange("p (m k) -> p m k", m=maps)
                if split:
                    for m in range(maps):
                        b = SC.filled_bank(dve)
                        n = signal(ve.scalar_tensor_tensor(dst[:, m, :], bias, slope, b[:, 0:nk], ALU.mult, ALU.add), s_free)
                    dve.wait_ge(s_free, n)
                else:
                    b = SC.filled_bank(dve)
                    then(ve.scalar_tensor_tensor(dst, under(bias, maps), slope, b[:, 0:maps * nk].rearrange("p (m k) -> p m k", m=maps),
                                                 ALU.mult, ALU.add), s_free)
                signal(ve.tensor_reduce(nmax[:, maps * u:maps * (u + 1)], dst, AX.X, ALU.max, negate=True), max_ready)

            def sparse():
                z = zs[2]
                for t in range(LT):
                    kd = kdup[:, t * 1024:(t + 1) * 1024]
                    twice(kd[:, 0:512], z[:, t, 1536:1792], 4)
                    twice(kd[:, 512:1024], z[:, t, 2048:2304], 4)
                    n = twice(cdup[:, t, :], z[:, t, 1024:1536], 8)
                signal(n, heads_ready)
                ve.memset(x[:, 2, :], 0.0)
                ve.memset(rows[:, 1024:2048], 0.0)
                dve.wait_ge(a_free, whole["pairs"])
                for src, name in ((0, "pos_k"), (1, "pos_v")):
                    v = pairs[src].rearrange("p h (r b) -> p h r b", b=8)
                    o = blk[src].rearrange("p l (h n) -> p l h n", h=4)
                    for half in range(2):
                        pos = sm(name)[:, 8 * half:8 * half + 8]
                        for h in range(4):
                            n = ve.tensor_tensor(o[:, 8 * half:8 * half + 8, h, :],
                                                 v[:, h, half:half + CMP_N, :].rearrange("p n b -> p b n"),
                                                 over(pos, CMP_N), ALU.add)
                    signal(n, cmp_blk)
                seen.next(cmp_out)
                then(ve.tensor_scalar(gates, gates, 1.0, None, ALU.add))
                then(ve.reciprocal(gates, gates))
                branch = gates.rearrange("p (t b h) -> p t b h", t=LT, b=3)
                ve.memset(cmp_p, 0.0)
                parts = [[v[0:60, src * 256:(src + 1) * 256] for v in (hidden, gelu_t)] for src in range(2)]

                def gelu_exponent(src):
                    h, g = parts[src]
                    b = vbank()
                    then(ve.tensor_copy(h, b[0:60, 0:256]), v_free)
                    then(ve.tensor_tensor(g, h, h, ALU.mult))
                    then(ve.tensor_scalar(g, g, 0.044715, 1.0, ALU.mult, ALU.add))
                    signal(ve.scalar_tensor_tensor(g, g, 2.0 * float(np.sqrt(2.0 / np.pi)), h, ALU.mult, ALU.mult), cmp_in)

                def gelu(src):
                    h, g = parts[src]
                    seen.next(cmp_out)
                    then(ve.tensor_scalar(g, g, 1.0, None, ALU.add))
                    then(ve.reciprocal(g, g))
                    signal(ve.tensor_tensor(h, h, g, ALU.mult), cmp_hid)

                gelu_exponent(0)
                gelu(0)

                def compressed(u):
                    sc = cmp_s.rearrange("p (h n) -> p h n", h=16)
                    if u == CMP_GELU:
                        gelu_exponent(1)
                    if u == CMP_GELU + 1:
                        gelu(1)
                    if u in CMP_SCORE:
                        qt = CMP_SCORE.index(u)
                        dve.wait_ge(late_loaded, 16)
                        for odd in range(2):
                            b = SC.filled_bank(dve)
                            dst, bias = (v.rearrange("p (h o n) -> p h o n", o=2, n=CMP_N)[:, :, odd, :] for v in (cmp_s, cmp_bias[:, qt, :]))
                            then(ve.tensor_tensor(dst, b[:, 0:120].rearrange("p (h n) -> p h n", h=8), bias, ALU.add), s_free)
                        then(ve.tensor_reduce(rsum[:, 0:16], sc, AX.X, ALU.max))
                        signal(ve.tensor_tensor(sc, sc, over(rsum[:, 0:16], CMP_N), ALU.subtract), cmp_in)
                    if u - 1 in CMP_SCORE:
                        qt = CMP_SCORE.index(u - 1)
                        seen.next(cmp_out)
                        then(ve.tensor_tensor(sc, sc, under(cmp_valid[:, qt, :], 16), ALU.mult))
                        then(ve.tensor_reduce(rsum[:, 0:16], sc, AX.X, ALU.add))
                        then(ve.tensor_scalar(rsum[:, 0:16], rsum[:, 0:16], TINY, None, ALU.max))
                        then(ve.reciprocal(rsum[:, 0:16], rsum[:, 0:16]))
                        then(ve.tensor_tensor(rsum[:, 0:16], rsum[:, 0:16], branch[:, qt, 0, :], ALU.mult))
                        if qt > 0:
                            dve.wait_ge(a_free, whole["cmp", qt - 1])
                        signal(ve.tensor_tensor(cmp_p.rearrange("p (h n) -> p h n", h=16)[:, :, 0:CMP_N], sc,
                                                over(rsum[:, 0:16], CMP_N), ALU.mult), cmp_probs)

                slopes = alibi(16)
                seen.next(z_act_ready)

                def out(u):
                    qt, h0 = u // 16, u % 16 - 3
                    b = vbank()
                    then(ve.tensor_scalar(rsum[:, 0:8], sums[:, 2 * u - 6:2 * u + 2], TINY, None, ALU.max))
                    then(ve.reciprocal(rsum[:, 0:8], rsum[:, 0:8]))
                    then(ve.tensor_tensor(coef[:, 0:8].rearrange("p (h b) -> p h b", h=4),
                                          rsum[:, 0:8].rearrange("p (h b) -> p h b", h=4),
                                          branch[:, qt, 1:3, h0:h0 + 4].rearrange("p b h -> p h b"), ALU.mult))
                    then(ve.tensor_tensor(weighed.rearrange("p (m d) -> p m d", m=8), b[:, :].rearrange("p (m d) -> p m d", m=8),
                                          over(coef[:, 0:8], HD), ALU.mult), v_free)
                    dst = mix[:, qt, h0 * HD:(h0 + 4) * HD].rearrange("p (h d) -> p h d", h=4)
                    w = weighed.rearrange("p (h b d) -> p h b d", h=4, b=2)
                    if qt == 0:
                        then(ve.tensor_tensor(dst, w[:, :, 0, :], w[:, :, 1, :], ALU.add))
                        return
                    cmp = cmp_rows[:, qt, h0 * HD:(h0 + 4) * HD].rearrange("p (h d) -> p h d", h=4)
                    dve.wait_ge(a_free, whole["cmp", qt])
                    for first, branch_rows in ((cmp, w[:, :, 0, :]), (dst, w[:, :, 1, :])):
                        then(ve.tensor_tensor(dst, first, branch_rows, ALU.add))
                    gate(2, qt, h0 * HD, 4 * HD, h0 in (4, 12))

                n_u = LT * 16
                for u in range(n_u + 5):
                    if u < n_u:
                        reuse(u)
                        compressed(u)
                        biased(u, causal[:, u // 16, 0:P * (u // 16 + 1)], slopes[u % 16], 2)
                    if u == 16 + 5:
                        dve.wait_ge(a_free, whole["cmp", 0])
                        then(ve.tensor_tensor(mix[:, 0, :], mix[:, 0, :], cmp_rows[:, 0, :], ALU.add))
                        gate(2, 0, 0, D, False)
                    out_low(2, u, n_u)
                    if u >= 5 and (u - 5) % 4 == 3:
                        out(u - 5)
                seen.next(probs_ready, 3)

            def differential():
                lr = sm("lam", "p (a b n) -> p a b n", a=2, b=2)
                prod = scratch[:, 0:128].rearrange("p (a n) -> p a n", a=2)
                then(ve.tensor_tensor(prod, lr[:, :, 0, :], lr[:, :, 1, :], ALU.mult))
                signal(ve.tensor_reduce(lam[:, 0:2], prod, AX.X, ALU.add), cmp_in)
                seen.next(cmp_out)
                then(ve.tensor_tensor(lam[:, 4:5], lam[:, 3:4], lam[:, 2:3], ALU.subtract))
                then(ve.tensor_scalar(lam[:, 5:6], lam[:, 4:5], -LAMBDA_INIT, None, ALU.add))
                slopes = alibi(8)

                def combine(u):
                    nk = P * (u // 8 + 1)
                    seen.next(maps_ready)
                    p = p_ring[u % 3]
                    s, r = sums[:, 2 * u:2 * u + 2], rsum[:, u % 2 * 2:u % 2 * 2 + 2]
                    then(ve.tensor_scalar(s, s, TINY, None, ALU.max))
                    then(ve.reciprocal(r[:, 1:2], s[:, 1:2]))
                    then(ve.scalar_tensor_tensor(r[:, 0:1], s[:, 0:1], lam[:, 5:6], r[:, 1:2], ALU.mult, ALU.mult))
                    signal(ve.scalar_tensor_tensor(p[:, 0:nk], p[:, nk:2 * nk], r[:, 0:1], p[:, 0:nk], ALU.mult, ALU.add), probs_mixed)

                def group(g):
                    return mix[:, g // 2, g % 2 * 512:g % 2 * 512 + 512]

                def squares(g):
                    b = vbank()
                    then(ve.reciprocal(rsum[:, 8:12], sums[:, 8 * g:8 * g + 8:2]))
                    then(ve.tensor_tensor(group(g).rearrange("p (h d) -> p h d", h=4), b[:, :].rearrange("p (h d) -> p h d", h=4),
                                          over(rsum[:, 8:12], 2 * HD), ALU.mult), v_free)
                    then(ve.tensor_tensor(weighed, group(g), group(g), ALU.mult))
                    signal(ve.tensor_reduce(head_ss[:, 4 * g:4 * g + 4], weighed.rearrange("p (h d) -> p h d", h=4), AX.X, ALU.add),
                           sums_ready)

                def normed(g):
                    inv_root()
                    scale_heads(group(g), 4, 2 * HD, 4 * g)
                    v = group(g).rearrange("p (h d) -> p h d", h=4)
                    then(ve.scalar_tensor_tensor(v, v, 1.0 - LAMBDA_INIT, under(sm("sub_gain"), 4), ALU.mult, ALU.mult))
                    if g == 0:
                        seen.next(z_act_ready)
                    gate(3, g // 2, g % 2 * 512, 512, g // 2 == LT - 1)

                n_u = LT * 8
                for u in range(n_u + 5):
                    if u < n_u:
                        biased(u, causal[:, u // 8, 0:P * (u // 8 + 1)], slopes[u % 8], 2, split=True)
                    if 1 <= u <= n_u:
                        combine(u - 1)
                    out_low(3, u, n_u)
                    if u >= 5 and (u - 5) % 4 == 3:
                        squares((u - 5) // 4)
                    if u >= 7 and (u - 7) % 4 == 3:
                        normed((u - 7) // 4)
                normed(n_u // 4 - 1)

            def dilated_heads():
                dve.wait_ge(dilated_loaded, 16)
                slopes = alibi(12)

                def soften(u):
                    h, qt = u % 4, u // 4
                    nk = P * (qt + 1)
                    s = s_ring[u % 3][:, 0:3 * nk]
                    for part in ((0, 1), (2,)):
                        b = SC.filled_bank(dve)
                        for n, g in enumerate(part):
                            i = ve.scalar_tensor_tensor(s[:, g * nk:(g + 1) * nk], dilated[:, g, qt, 0:nk], slopes[g * 4 + h],
                                                        b[:, n * nk:(n + 1) * nk], ALU.mult, ALU.add)
                        then(i, s_free)
                    signal(ve.tensor_reduce(nmax[:, u:u + 1], s, AX.X, ALU.max, negate=True), max_ready)

                def combine(u):
                    nk = P * (u // 4 + 1)
                    seen.next(maps_ready)
                    p = p_ring[u % 3]
                    then(ve.tensor_tensor(p[:, 0:nk], p[:, 0:nk], p[:, nk:2 * nk], ALU.add))
                    signal(ve.tensor_tensor(p[:, 0:nk], p[:, 0:nk], p[:, 2 * nk:3 * nk], ALU.add), probs_mixed)

                n_u = LT * 4
                for u in range(n_u + 5):
                    if u < n_u:
                        soften(u)
                    if 1 <= u <= n_u:
                        combine(u - 1)
                    out_low(4, u, n_u)
                    if u >= 5 and (u - 5) % 2 == 1:
                        v, b = u - 5, vbank()
                        r = rsum[:, v // 2 % 2 * 2:v // 2 % 2 * 2 + 2]
                        then(ve.reciprocal(r, sums[:, v - 1:v + 1]))
                        c = (v % 4 - 1) * 256
                        then(ve.tensor_tensor(mix[:, v // 4, c:c + 512].rearrange("p (h d) -> p h d", h=2),
                                              b[:, :].rearrange("p (h d) -> p h d", h=2), over(r, 256), ALU.mult), v_free)
                        if v == 1:
                            seen.next(z_act_ready)
                        gate(4, v // 4, c, 512, v // 4 == LT - 1)

            def stick():
                n_u = LT * 16
                for u in range(n_u + 5):
                    if u < n_u:
                        nk = P * (u // 16 + 1)
                        s = s_ring[u % 3]
                        b = SC.filled_bank(dve)
                        then(ve.tensor_tensor(s[:, 0:nk], b[:, 0:nk], strict[:, u // 16, 0:nk], ALU.add), s_free)
                        then(ve.tensor_scalar(s[:, 256:256 + nk], s[:, 0:nk], 0.0, None, ALU.max))
                        signal(ve.scalar_tensor_tensor(s[:, 512:512 + nk], s[:, 256:256 + nk], -2.0, s[:, 0:nk], ALU.mult, ALU.add), soft_in)
                    if 1 <= u <= n_u:
                        v = u - 1
                        nk = P * (v // 16 + 1)
                        s, p = s_ring[v % 3], p_ring[v % 3]
                        seen.next(soft_out, 2)
                        reuse(v)
                        dve.wait_ge(soft_in, own["soft_in"])
                        then(ve.tensor_tensor_scan(p[:, 0:nk][:, ::-1], s[:, 256:256 + nk][:, ::-1], s[:, 512:512 + nk][:, ::-1], 0.0,
                                                   ALU.add, ALU.add))
                        signal(ve.tensor_tensor(p[:, 256:256 + nk], s[:, 0:nk], p[:, 0:nk], ALU.subtract), max_ready)
                    out_low(5, u, n_u)
                    if u >= 5 and (u - 5) % 8 == 7:
                        v, b = u - 5, vbank()
                        if v == 7:
                            seen.next(z_act_ready)
                        c = (v % 16 - 7) * HD
                        z = zs[5][:, v // 16, GATE_AT[5] + c:GATE_AT[5] + c + 512]
                        signal(ve.tensor_tensor(mix[:, v // 16, c:c + 512], b[:, :], z, ALU.mult), v_free)
                seen.next(probs_ready, 3)

            scratch2 = scratch
            neg_sink = coef[:, 0:16]
            signal(ve.memset(mod_bank[:, :], 0.0), mod_cleared)
            dve.wait_ge(small_loaded, 16)
            dve.wait_ge(const_loaded, 16)
            for i in range(min(layers, 2)):
                first_layer(i)
            for i in range(2, layers):
                second_layer(i)

        @block.gpsimd
        def _(pool):
            seen = Seen(pool)
            nc.gpsimd.memset(half_neg[:, :], -0.5).then_inc(half_neg_ready, 1)
            pool.wait_ge(half_neg_ready, 1)

            def inv_root(dst, src, n, width, done=rstd_ready):
                nc.gpsimd.tensor_scalar(src[:, 0:n], src[:, 0:n], 1.0 / width, EPS, ALU.mult, ALU.add).then_inc(mean_ready, 1)
                seen.next(mean_ready)
                nc.gpsimd.tensor_tensor(dst[:, 0:n], src[:, 0:n], half_neg[:, 0:n], ALU.pow).then_inc(done, 1)

            def of_rows(T, done=rstd_ready):
                seen.next(sumsq_ready, T)
                inv_root(rstd, ss, T, D, done)

            def of_tiles(T):
                for t in range(T):
                    seen.next(sumsq_ready)
                    inv_root(rstd[:, t:t + 1], ss[:, t:t + 1], 1, D, scale_ready)

            def of_heads(lo, hi, width):
                seen.next(sums_ready)
                inv_root(head_rstd[:, lo:hi], head_ss[:, lo:hi], hi - lo, width)

            def add_sums(i):
                T = NT if i == 0 else LT
                pool.wait_ge(a_free, whole["gates2", i])
                for c in range(2 * T):
                    t, half = down_half(c)
                    pool.wait_ge(d_free, (0 if i == 0 else NE * NT * 2) + (NE - 2) * 2 * T + c + 1)
                    nc.gpsimd.tensor_tensor(mix[:, t, half], mix[:, t, half], gate_rows[:, t // LT, half], ALU.mult).then_inc(sum_gated, 1)
                    seen.next(sum_gated)
                    nc.gpsimd.tensor_tensor(x[:, t, half], x[:, t, half], mix[:, t, half], ALU.add).then_inc(sum_added, 1)

            def load_post(i, x_tiles):
                if x_tiles:
                    pool.wait_ge(x_ready, x_tiles)
                pool.dma_start(post_row[:, :], d_post[i - 2:i - 1, :].broadcast_to([P, D])).then_inc(post_loaded, 16)

            of_tiles(NT)
            of_heads(0, 40, HD)
            of_heads(0, 16, GLA_DV)
            if layers > 1:
                pool.wait_ge(gla_done, 1)
                pool.dma_start(phase[:, 0:N_LATE], d_late).then_inc(late_loaded, 16)
            of_tiles(NT)
            add_sums(0)
            if layers > 2:
                load_post(2, 0)
            if layers > 1:
                of_tiles(NT)
                for lo, hi in ((0, Q_ROOTS), (Q_ROOTS, Q_ROOTS + 16), (Q_ROOTS + 16, Q_ROOTS + 32)):
                    of_heads(lo, hi, HD)
                of_tiles(LT)
                add_sums(1)
            for i in range(2, layers):
                of_rows(LT, scale_ready)
                if i == 3:
                    for g in range(4):
                        of_heads(4 * g, 4 * g + 4, 2 * HD)
                seen.next(half_squares, LT)
                nc.gpsimd.tensor_scalar(ss[:, 0:LT], ss_half[:, :, 0], 1.0 / D, EPS, ALU.mult, ALU.add).then_inc(mean_ready, 1)
                seen.next(mean_ready)
                for t in range(LT):
                    seen.next(half_squares)
                    nc.gpsimd.tensor_scalar(ss[:, t:t + 1], ss_half[:, t, 1:2], 1.0 / D, ss[:, t:t + 1], ALU.mult, ALU.add).then_inc(mean_ready, 1)
                    seen.next(mean_ready)
                    nc.gpsimd.tensor_tensor(rstd[:, t:t + 1], ss[:, t:t + 1], half_neg[:, 0:1], ALU.pow).then_inc(rstd_ready, 1)
                if i + 1 < layers:
                    load_post(i + 1, 12 + LT * (i - 1))
                if i == 2 and layers > 4:
                    pool.dma_start(rows[:, :], d_dilated).then_inc(dilated_loaded, 16)

        @block.sync
        def _(sp):
            n_early = SMALL["lam"][0]
            sp.dma_start(small[:, 0:n_early], d_small[:, 0:n_early]).then_inc(small_loaded, 16)
            sp.dma_start(x[:, 0:LT, :], d_x.rearrange("(t p) n -> p t n", p=P)).then_inc(x_loaded, 16)
            sp.dma_start(x[:, LT:NT, :], d_ctx.rearrange("(t p) n -> p t n", p=P)).then_inc(x_loaded, 16)
            n_res = N_CONST - 2 * 7 * P
            sp.dma_start(const[:, :], d_const[:, 0:n_res]).then_inc(const_loaded, 16)

            def load(n):
                if n == STREAM["in0"][0] + SLOTS:
                    sp.dma_start(small[:, n_early:], d_small[:, n_early:]).then_inc(small_loaded, 16)
                if n == STREAM["mod_late"][0]:
                    sp.dma_start(phase[:, 0:2 * 7 * P], d_const[:, n_res:N_CONST]).then_inc(masks_loaded, 16)
                slot = tenancy[n][0]
                if n >= SLOTS:
                    sp.wait_ge(*tenancy[n - SLOTS][1:])
                sp.dma_start(ring[:, slot, :], d_w[n]).then_inc(slot_full[slot], 16)

            def expert_loads(i):
                first, half0, d_base = moe_at[i]
                base, per = NE * i, 2 * (NT if i == 0 else LT)

                def slot(c):
                    return (first + c) % SLOTS

                def used(kind, e, kh, k0=0):
                    if kind == "up":
                        return (chunk_used, e + (half0 + 1)) if kh == 0 else (u_full, e * 2 + (2 * base + 2))
                    return d_full, e * per + (d_base + per)

                order = []
                for kind, e in expert_order():
                    order += [(kind, e, 0), (kind, e, 1)] if kind == "up" else [(kind, e, 0)]

                def load_c(c):
                    prev = first + c - SLOTS
                    if c >= SLOTS:
                        sp.wait_ge(*used(*order[c - SLOTS]))
                    elif prev >= 0:
                        sp.wait_ge(*tenancy[prev][1:])
                    sp.dma_start(ring[:, slot(c), :], d_w[first + c]).then_inc(slot_full[slot(c)], 16)

                for c in range(5 + 6):
                    load_c(c)
                with sp.Fori(2, NE // 2) as j:
                    for q in range(6):
                        c = 5 + 6 + q
                        kind, e, kh = order[c - SLOTS]
                        sp.wait_ge(*used(kind, j * 2 + (e - 4), kh))
                        src = d_w[bass.ds(j * 6 + (first + c - 12), 1)].rearrange("a p n -> (a p) n")
                        sp.dma_start(ring[:, slot(c), :], src).then_inc(slot_full[slot(c)], 16)
                load_c(3 * NE - 1)
                for c in range(3 * NE):
                    kind, e, kh = order[c]
                    tenancy[first + c][1:] = used(kind, e, kh)

            n = 0
            for i in range(min(layers, 2)):
                while n < moe_at[i][0]:
                    load(n)
                    n += 1
                expert_loads(i)
                n += 3 * NE
            while n < len(tenancy):
                load(n)
                n += 1
            sp.wait_ge(x_ready, {1: 8, 2: 12}.get(layers, 12 + 2 * (layers - 2)))
            sp.dma_start(d_out.rearrange("(t p) n -> p t n", p=P), x[:, 0:LT, :]).then_inc(out_done, 16)
            sp.wait_ge(out_done, 16)


def kernel(**inputs):
    import concourse.bacc as bacc
    from concourse.bass_utils import run_bass_kernel_spmd

    nc = bacc.Bacc("TRN2", target_bir_lowering=False, num_devices=1)
    laid = host_layout(inputs)
    arrays, aps = {}, []
    for name in ("x", "ctx", "weights", "small", "norm_post", "const", "late", "dilated"):
        arrays[name + "_dram"] = laid[name]
        aps.append(nc.dram_tensor(name + "_dram", laid[name].shape, F32, kind="ExternalInput").ap())
    aps.append(nc.dram_tensor("out_dram", (S, D), F32, kind="ExternalOutput").ap())
    build_program(nc, *aps)
    r = run_bass_kernel_spmd(nc, [arrays], core_ids=[0])
    return r.results[0]["out_dram"].reshape(1, S, D)
```
